# Optimizing a Trainium2 kernel written in Bass

```python
import jax, jax.numpy as jnp
from jax import lax
import numpy as np
import math

D_MODEL = 1024
BATCH = 1
SEQ = 1024
DEPTH = 1

CTX_LEN = 256
GRID_W = 64
N_MIXERS = 3
ALPHA = (2 * DEPTH) ** 0.25
BETA = (8 * DEPTH) ** -0.25
LN_EPS = 1e-6
RMS_EPS = 1e-6
N_MOD = 6
FFN_HIDDEN = -(-8 * D_MODEL // (3 * 256)) * 256
POOL_WINDOWS = (2, 4, 8, 16)
N_POOL_GROUPS = len(POOL_WINDOWS)
POOL_GROUP_DIM = D_MODEL // N_POOL_GROUPS
HGRN_HEAD_DIM = 128
HGRN_HEADS = D_MODEL // HGRN_HEAD_DIM
HGRN_CHUNK = 64
NA_HEAD_DIM = 64
NA_HEADS = D_MODEL // NA_HEAD_DIM
NA_ROWS = 8
NA_COLS = 16
NA_QBLOCK = 16
NA_KBAND = 32
N_POOL_LAYERS = len(range(0, DEPTH, N_MIXERS))
N_HGRN_LAYERS = len(range(1, DEPTH, N_MIXERS))
N_NA_LAYERS = len(range(2, DEPTH, N_MIXERS))


def layer_norm(x, g, b):
    xf = x.astype(jnp.float32)
    mu = jnp.mean(xf, axis=-1, keepdims=True)
    var = jnp.mean(jnp.square(xf - mu), axis=-1, keepdims=True)
    return ((xf - mu) * lax.rsqrt(var + LN_EPS) * g + b).astype(x.dtype)

def swiglu(h, w_in, w_out):
    gt, up = jnp.split(h @ w_in, 2, axis=-1)
    return (jax.nn.silu(gt) * up) @ w_out

def centred_window_mean(h, w):
    L = h.shape[1]
    lo = w // 2
    hi = w - 1 - lo
    t = np.arange(L)
    start = np.clip(t - lo, 0, L)
    end = np.clip(t + hi + 1, 0, L)
    hf = h.astype(jnp.float32)
    cs = jnp.concatenate([jnp.zeros_like(hf[:, :1]), jnp.cumsum(hf, axis=1)], axis=1)
    cnt = jnp.asarray((end - start).astype(np.float32))
    return ((cs[:, end] - cs[:, start]) / cnt[None, :, None]).astype(h.dtype)

def multiscale_pool(h, w_group, scale):
    B, L, D = h.shape
    outs = []
    for g, w in enumerate(POOL_WINDOWS):
        hg = h[..., g * POOL_GROUP_DIM:(g + 1) * POOL_GROUP_DIM]
        outs.append(centred_window_mean(hg, w) - hg)
    p = jnp.stack(outs, axis=2)
    y = jnp.einsum('blgc,gcd->blgd', p, w_group).reshape(B, L, D)
    return y * scale

def pool_mixer(hx, hc, w_group, scale, need_ctx):
    ox = multiscale_pool(hx, w_group, scale)
    oc = multiscale_pool(hc, w_group, scale) if need_ctx else None
    return ox, oc

def chunk_gated_scan(q, k, v, log_f, s0):
    B, H, L, DK = q.shape
    DV = v.shape[-1]
    C = HGRN_CHUNK
    n = L // C

    def chunks(a):
        return jnp.moveaxis(a.reshape(B, H, n, C, a.shape[-1]), 2, 0)

    lower = jnp.asarray(np.tril(np.ones((C, C), dtype=bool)))

    def step(s, inp):
        q_c, k_c, v_c, g_c = inp
        b = jnp.cumsum(g_c, axis=2)
        rel = jnp.where(lower[:, :, None], b[:, :, :, None, :] - b[:, :, None, :, :], -jnp.inf)
        a = jnp.einsum('bhtd,bhsd,bhtsd->bhts', q_c, k_c, jnp.exp(rel))
        o = jnp.einsum('bhts,bhse->bhte', a, v_c) + jnp.einsum('bhtd,bhde->bhte', q_c * jnp.exp(b), s)
        b_end = b[:, :, -1:, :]
        s_new = jnp.exp(b_end)[:, :, 0, :, None] * s + jnp.einsum('bhsd,bhse->bhde', k_c * jnp.exp(b_end - b), v_c)
        return s_new, o

    s_fin, o = lax.scan(step, s0, (chunks(q), chunks(k), chunks(v), chunks(log_f)))
    o = jnp.moveaxis(o, 0, 2).reshape(B, H, L, DV)
    return o, s_fin

def hgrn2_mixer(hx, hc, w_in, lb_fwd, lb_bwd, norm_w, w_out, need_ctx):
    def heads(a):
        B_, L_, _ = a.shape
        return a.reshape(B_, L_, HGRN_HEADS, HGRN_HEAD_DIM).transpose(0, 2, 1, 3).astype(jnp.float32)

    def project(h):
        q, v, zf, zb, g = jnp.split(h @ w_in, 5, axis=-1)
        return heads(jax.nn.silu(q)), heads(v), heads(zf), heads(zb), g

    def gate(z, lb):
        lb = lb.reshape(HGRN_HEADS, 1, HGRN_HEAD_DIM)
        f = lb + (1.0 - lb) * jax.nn.sigmoid(z)
        return 1.0 - f, jnp.log(f)

    def flip(a):
        return jnp.flip(a, axis=2)

    qx, vx, zfx, zbx, gx = project(hx)
    qc, vc, zfc, zbc, gc = project(hc)
    s0 = jnp.zeros((hc.shape[0], HGRN_HEADS, HGRN_HEAD_DIM, HGRN_HEAD_DIM), jnp.float32)
    kcf, lcf = gate(zfc, lb_fwd)
    kxf, lxf = gate(zfx, lb_fwd)
    oc_f, sc_f = chunk_gated_scan(qc, kcf, vc, lcf, s0)
    ox_f, _ = chunk_gated_scan(qx, kxf, vx, lxf, sc_f)
    kcb, lcb = gate(zbc, lb_bwd)
    kxb, lxb = gate(zbx, lb_bwd)
    oc_b, sc_b = chunk_gated_scan(flip(qc), flip(kcb), flip(vc), flip(lcb), s0)
    ox_b, _ = chunk_gated_scan(flip(qx), flip(kxb), flip(vx), flip(lxb), sc_b)

    def readout(o, g, dtype):
        B_, H_, L_, E_ = o.shape
        o = o * lax.rsqrt(jnp.mean(o * o, axis=-1, keepdims=True) + RMS_EPS)
        o = o.transpose(0, 2, 1, 3).reshape(B_, L_, H_ * E_).astype(dtype)
        return (o * norm_w * jax.nn.silu(g)) @ w_out

    ox = readout(ox_f + flip(ox_b), gx, hx.dtype)
    oc = readout(oc_f + flip(oc_b), gc, hc.dtype) if need_ctx else None
    return ox, oc

def na_mixer(hx, hc, w_qkv, rpb, w_out, need_ctx):
    B, L, D = hx.shape
    rows = L // GRID_W
    kr = min(NA_ROWS, rows)
    scale = NA_HEAD_DIM ** -0.5

    def qkv(h):
        B_, L_, _ = h.shape
        z = (h @ w_qkv).reshape(B_, L_, 3, NA_HEADS, NA_HEAD_DIM)
        return [jnp.moveaxis(z[:, :, m], 1, 2) for m in range(3)]

    qx, kx, vx = qkv(hx)
    qc, kc, vc = qkv(hc)

    def grid(a):
        return a.reshape(B, NA_HEADS, rows, GRID_W, NA_HEAD_DIM)

    qg, kg, vg = grid(qx), grid(kx), grid(vx)
    n_cb = GRID_W // NA_QBLOCK
    qcol = np.arange(GRID_W).reshape(n_cb, NA_QBLOCK)
    band_start = np.clip(np.arange(n_cb) * NA_QBLOCK - NA_COLS // 2, 0, GRID_W - NA_KBAND)
    kcol = band_start[:, None] + np.arange(NA_KBAND)
    win_start = np.clip(qcol - NA_COLS // 2, 0, GRID_W - NA_COLS)
    col_ok = (kcol[:, None, :] >= win_start[:, :, None]) & (kcol[:, None, :] < win_start[:, :, None] + NA_COLS)
    dcol_idx = np.clip(kcol[:, None, :] - qcol[:, :, None] + NA_COLS - 1, 0, 2 * NA_COLS - 2)
    col_ok = jnp.asarray(col_ok)
    n_loc = kr * NA_KBAND

    def row_block(r):
        rs = jnp.clip(r - kr // 2, 0, rows - kr)
        q_r = lax.dynamic_index_in_dim(qg, r, axis=2, keepdims=False)
        k_r = lax.dynamic_slice_in_dim(kg, rs, kr, axis=2)[:, :, :, kcol]
        v_r = lax.dynamic_slice_in_dim(vg, rs, kr, axis=2)[:, :, :, kcol]
        q_b = q_r.reshape(B, NA_HEADS, n_cb, NA_QBLOCK, NA_HEAD_DIM)
        s_loc = jnp.einsum('bhjqd,bhajkd->bhjqak', q_b, k_r).astype(jnp.float32) * scale
        drow = rs + jnp.arange(kr) - r + NA_ROWS - 1
        bias = rpb[:, drow][:, :, dcol_idx].transpose(0, 2, 3, 1, 4)
        s_loc = jnp.where(col_ok[:, :, None, :], s_loc + bias.astype(jnp.float32), -jnp.inf)
        s_loc = s_loc.reshape(B, NA_HEADS, n_cb, NA_QBLOCK, n_loc)
        s_ctx = jnp.einsum('bhjqd,bhmd->bhjqm', q_b, kc).astype(jnp.float32) * scale
        p = jax.nn.softmax(jnp.concatenate([s_loc, s_ctx], axis=-1), axis=-1).astype(vx.dtype)
        p_loc = p[..., :n_loc].reshape(B, NA_HEADS, n_cb, NA_QBLOCK, kr, NA_KBAND)
        o = jnp.einsum('bhjqak,bhajke->bhjqe', p_loc, v_r) + jnp.einsum('bhjqm,bhme->bhjqe', p[..., n_loc:], vc)
        return o.reshape(B, NA_HEADS, GRID_W, NA_HEAD_DIM)

    o = lax.map(row_block, jnp.arange(rows))
    ox = o.transpose(1, 0, 3, 2, 4).reshape(B, L, D) @ w_out
    oc = None
    if need_ctx:
        s = jnp.einsum('bhqd,bhkd->bhqk', qc, kc).astype(jnp.float32) * scale
        pc = jax.nn.softmax(s, axis=-1).astype(vc.dtype)
        occ = jnp.einsum('bhqk,bhkd->bhqd', pc, vc)
        oc = occ.transpose(0, 2, 1, 3).reshape(hc.shape[0], hc.shape[1], D) @ w_out
    return ox, oc

def first_inputs(seed: int = 0) -> dict:
    key = jax.random.key(seed)
    ks = jax.random.split(key, 20)
    D = D_MODEL
    F = FFN_HIDDEN
    GD = POOL_GROUP_DIM

    def nrm(k, shape, s):
        return jax.random.normal(k, shape, jnp.float32) * s

    return {
        'x': nrm(ks[0], (BATCH, SEQ, D), 1.0),
        'c': nrm(ks[1], (BATCH, D), 1.0),
        'ctx': nrm(ks[2], (BATCH, CTX_LEN, D), 1.0),
        'c_ctx': nrm(ks[3], (D,), 1.0),
        'mod_w': nrm(ks[4], (DEPTH, D, N_MOD * D), 0.5 * D ** -0.5),
        'mod_b': nrm(ks[5], (DEPTH, N_MOD * D), 0.02),
        'ln_g': 1.0 + nrm(ks[6], (DEPTH, 2, D), 0.02),
        'ln_b': nrm(ks[7], (DEPTH, 2, D), 0.02),
        'ffn_w_in': nrm(ks[8], (DEPTH, D, 2 * F), D ** -0.5),
        'ffn_w_out': nrm(ks[9], (DEPTH, F, D), BETA * F ** -0.5),
        'pool_w': nrm(ks[10], (N_POOL_LAYERS, N_POOL_GROUPS, GD, GD), BETA * GD ** -0.5),
        'pool_scale': 1.0 + nrm(ks[11], (N_POOL_LAYERS, D), 0.02),
        'hgrn_w_in': nrm(ks[12], (N_HGRN_LAYERS, D, 5 * D), D ** -0.5),
        'hgrn_lb_logits': 1.0 + nrm(ks[13], (2, DEPTH, D), 0.02),
        'hgrn_norm_w': 1.0 + nrm(ks[14], (N_HGRN_LAYERS, D), 0.02),
        'hgrn_w_out': nrm(ks[15], (N_HGRN_LAYERS, D, D), BETA * D ** -0.5),
        'na_w_qkv': nrm(ks[16], (N_NA_LAYERS, D, 3 * D), D ** -0.5),
        'na_rpb': nrm(ks[17], (N_NA_LAYERS, NA_HEADS, 2 * NA_ROWS - 1, 2 * NA_COLS - 1), 0.02),
        'na_w_out': nrm(ks[18], (N_NA_LAYERS, D, D), BETA * D ** -0.5),
    }

def first_block(x, c, ctx, c_ctx, mod_w, mod_b, ln_g, ln_b, ffn_w_in, ffn_w_out,
              pool_w, pool_scale, hgrn_w_in, hgrn_lb_logits, hgrn_norm_w, hgrn_w_out,
              na_w_qkv, na_rpb, na_w_out):
    p_lb = jax.nn.softmax(hgrn_lb_logits.astype(jnp.float32), axis=1)
    lower_bounds = jnp.cumsum(p_lb, axis=1) - p_lb[:, :1]
    s_c = jax.nn.silu(c)
    s_cc = jax.nn.silu(c_ctx)
    for i in range(DEPTH):
        last = i == DEPTH - 1
        kind = i % N_MIXERS
        j = i // N_MIXERS
        mod_x = s_c @ mod_w[i] + mod_b[i]
        mod_c = s_cc @ mod_w[i] + mod_b[i]
        sh1, sc1, g1, sh2, sc2, g2 = jnp.split(mod_x[:, None, :], N_MOD, axis=-1)
        csh1, csc1, cg1, csh2, csc2, cg2 = jnp.split(mod_c, N_MOD, axis=-1)
        hx = x * (1.0 + sc1) + sh1
        hc = ctx * (1.0 + csc1) + csh1 if (kind != 0 or not last) else None
        if kind == 0:
            ox, oc = pool_mixer(hx, hc, pool_w[j], pool_scale[j], not last)
        elif kind == 1:
            ox, oc = hgrn2_mixer(hx, hc, hgrn_w_in[j], lower_bounds[0, i], lower_bounds[1, i],
                                 hgrn_norm_w[j], hgrn_w_out[j], not last)
        else:
            ox, oc = na_mixer(hx, hc, na_w_qkv[j], na_rpb[j], na_w_out[j], not last)
        x = layer_norm(ALPHA * x + g1 * ox, ln_g[i, 0], ln_b[i, 0])
        x = layer_norm(ALPHA * x + g2 * swiglu(x * (1.0 + sc2) + sh2, ffn_w_in[i], ffn_w_out[i]),
                       ln_g[i, 1], ln_b[i, 1])
        if not last:
            ctx = layer_norm(ALPHA * ctx + cg1 * oc, ln_g[i, 0], ln_b[i, 0])
            ctx = layer_norm(ALPHA * ctx + cg2 * swiglu(ctx * (1.0 + csc2) + csh2, ffn_w_in[i], ffn_w_out[i]),
                             ln_g[i, 1], ln_b[i, 1])
    return x


DEPTH_2 = 2

EPS = 1e-6
DA_HEADS = 8
DA_QK_DIM = 64
DA_V_DIM = 2 * DA_QK_DIM
DA_WIDTH = DA_HEADS * DA_V_DIM
Q_BLOCK = 128
ML_HEADS = 4
ML_QK_DIM = 128
ML_V_DIM = 256
ML_WIDTH = ML_HEADS * ML_V_DIM
ML_CHUNK = 128
CONV_WIDTH = 4
SG_GROUPS = 8
SG_CHUNK = 128
SG_WIDTH = 2 * D_MODEL
SG_GROUP_DIM = SG_WIDTH // SG_GROUPS

EVEN_SIZES = (
    DA_HEADS * 2 * DA_QK_DIM,
    DA_HEADS * 2 * DA_QK_DIM,
    DA_WIDTH,
    DA_WIDTH,
    2 * ML_HEADS * ML_QK_DIM,
    ML_WIDTH,
    ML_HEADS,
    ML_HEADS,
    ML_WIDTH,
    ML_WIDTH,
)
EVEN_IN = sum(EVEN_SIZES)
ODD_SIZES = (SG_WIDTH, SG_WIDTH, SG_WIDTH)
ODD_IN = sum(ODD_SIZES)


def _split(t, sizes):
    out, off = [], 0
    for n in sizes:
        out.append(t[..., off:off + n])
        off += n
    return out

def rmsnorm(x, g):
    xf = x.astype(jnp.float32)
    y = xf * lax.rsqrt(jnp.mean(xf * xf, axis=-1, keepdims=True) + EPS)
    return (y * g.astype(jnp.float32)).astype(x.dtype)

def causal_dwconv(x, w, b):
    S = x.shape[1]
    xp = jnp.pad(x, ((0, 0), (CONV_WIDTH - 1, 0), (0, 0)))
    return sum(w[j] * xp[:, j:j + S] for j in range(CONV_WIDTH)) + b

def diff_attention(q, k, v, lam):
    B, S = q.shape[:2]
    nb = S // Q_BLOCK
    qb = (q * DA_QK_DIM ** -0.5).reshape(B, nb, Q_BLOCK, DA_HEADS, 2, DA_QK_DIM)
    qb = qb.transpose(1, 0, 3, 4, 2, 5)
    kt = k.transpose(0, 2, 3, 1, 4)
    vt = v.transpose(0, 2, 1, 3)
    k_pos = jnp.arange(S)

    def block(args):
        qi, i = args
        s = jnp.einsum('bhcqd,bhckd->bhcqk', qi, kt).astype(jnp.float32)
        q_pos = i * Q_BLOCK + jnp.arange(Q_BLOCK)
        s = jnp.where(k_pos[None, :] <= q_pos[:, None], s, -jnp.inf)
        p = jax.nn.softmax(s, axis=-1)
        a = p[:, :, 0] - lam * p[:, :, 1]
        return jnp.einsum('bhqk,bhkv->bhqv', a.astype(vt.dtype), vt)

    o = lax.map(block, (qb, jnp.arange(nb)))
    return o.transpose(1, 0, 3, 2, 4).reshape(B, S, DA_HEADS, DA_V_DIM)

def mlstm_chunkwise(q, k, v, i_pre, f_pre):
    B, S, H, dk = q.shape
    dv = v.shape[-1]
    L = ML_CHUNK
    nc = S // L
    f32 = jnp.float32

    def chunks(t):
        t = t.astype(f32).reshape(B, nc, L, H, *t.shape[3:])
        return jnp.moveaxis(t, 3, 1)

    qc = chunks(q) * dk ** -0.5
    kc = chunks(k)
    vc = chunks(v)
    ic = chunks(i_pre)
    lf = jax.nn.log_sigmoid(chunks(f_pre))
    bcum = jnp.cumsum(lf, axis=-1)
    b_last = bcum[..., -1]
    g = b_last[..., None] - bcum + ic

    def step(carry, inp):
        C, n, m = carry
        bl, gs, ks, vs = inp
        m_new = jnp.maximum(bl + m, jnp.max(gs, axis=-1))
        decay = jnp.exp(bl + m - m_new)
        w = jnp.exp(gs - m_new[..., None])
        C_new = decay[..., None, None] * C + jnp.einsum('bhl,bhlk,bhlv->bhkv', w, ks, vs)
        n_new = decay[..., None] * n + jnp.einsum('bhl,bhlk->bhk', w, ks)
        return (C_new, n_new, m_new), (C, n, m)

    init = (jnp.zeros((B, H, dk, dv), f32), jnp.zeros((B, H, dk), f32), jnp.zeros((B, H), f32))
    xs = (jnp.moveaxis(b_last, 2, 0), jnp.moveaxis(g, 2, 0),
          jnp.moveaxis(kc, 2, 0), jnp.moveaxis(vc, 2, 0))
    _, (C_prev, n_prev, m_prev) = lax.scan(step, init, xs)
    C_prev = jnp.moveaxis(C_prev, 0, 2)
    n_prev = jnp.moveaxis(n_prev, 0, 2)
    m_prev = jnp.moveaxis(m_prev, 0, 2)

    causal = jnp.tril(jnp.ones((L, L), dtype=bool))
    log_d = bcum[..., :, None] - bcum[..., None, :] + ic[..., None, :]
    log_d = jnp.where(causal, log_d, -jnp.inf)
    log_inter = bcum + m_prev[..., None]
    m_t = jnp.maximum(log_inter, jnp.max(log_d, axis=-1))
    dmat = jnp.exp(log_d - m_t[..., None])
    inter_w = jnp.exp(log_inter - m_t)
    qk = jnp.einsum('bhctd,bhcsd->bhcts', qc, kc) * dmat
    num = (jnp.einsum('bhcts,bhcsv->bhctv', qk, vc)
           + inter_w[..., None] * jnp.einsum('bhctd,bhcdv->bhctv', qc, C_prev))
    den = jnp.sum(qk, axis=-1) + inter_w * jnp.einsum('bhctd,bhcd->bhct', qc, n_prev)
    h = num / jnp.maximum(jnp.abs(den), jnp.exp(-m_t))[..., None]
    h = jnp.moveaxis(h, 1, 3).reshape(B, S, H, dv)
    return h.astype(q.dtype)

def even_mixer(h, layer, w_in, b_igate, b_fgate, conv_w, conv_b,
               lambda_q1, lambda_k1, lambda_q2, lambda_k2, da_head_g, ml_head_g, w_out):
    B, S, _ = h.shape
    p = jnp.einsum('bsd,de->bse', h, w_in)
    da_q, da_k, da_v, da_z, ml_qk, ml_v, ml_i, ml_f, ml_o, ml_z = _split(p, EVEN_SIZES)

    f32 = jnp.float32
    lam_init = 0.8 - 0.6 * math.exp(-0.3 * layer)
    lam = (jnp.exp(jnp.dot(lambda_q1.astype(f32), lambda_k1.astype(f32)))
           - jnp.exp(jnp.dot(lambda_q2.astype(f32), lambda_k2.astype(f32))) + lam_init)
    o_a = diff_attention(da_q.reshape(B, S, DA_HEADS, 2, DA_QK_DIM),
                         da_k.reshape(B, S, DA_HEADS, 2, DA_QK_DIM),
                         da_v.reshape(B, S, DA_HEADS, DA_V_DIM), lam)
    o_a = rmsnorm(o_a, da_head_g) * (1.0 - lam_init)
    y_a = o_a.reshape(B, S, DA_WIDTH) * jax.nn.silu(da_z)

    qk = jax.nn.silu(causal_dwconv(ml_qk, conv_w, conv_b))
    ml_q, ml_k = _split(qk, (ML_HEADS * ML_QK_DIM, ML_HEADS * ML_QK_DIM))
    hm = mlstm_chunkwise(ml_q.reshape(B, S, ML_HEADS, ML_QK_DIM),
                         ml_k.reshape(B, S, ML_HEADS, ML_QK_DIM),
                         ml_v.reshape(B, S, ML_HEADS, ML_V_DIM),
                         ml_i + b_igate, ml_f + b_fgate)
    hm = hm * jax.nn.sigmoid(ml_o).reshape(B, S, ML_HEADS, ML_V_DIM)
    hm = rmsnorm(hm, ml_head_g)
    y_b = hm.reshape(B, S, ML_WIDTH) * jax.nn.silu(ml_z)

    y = jnp.concatenate([y_a, y_b], axis=-1)
    return jnp.einsum('bse,ed->bsd', y, w_out)

def odd_mixer(h, sg_norm_g, w_in, w_spatial, b_spatial, w_out):
    B, S, _ = h.shape
    nc = S // SG_CHUNK
    p = jnp.einsum('bsd,de->bse', h, w_in)
    u, v, z = _split(p, ODD_SIZES)
    u = jax.nn.gelu(u)
    v = rmsnorm(jax.nn.gelu(v), sg_norm_g)
    vg = v.reshape(B, nc, SG_CHUNK, SG_GROUPS, SG_GROUP_DIM)
    causal = jnp.tril(jnp.ones((SG_CHUNK, SG_CHUNK), dtype=w_spatial.dtype))
    wm = w_spatial * causal
    vs = jnp.einsum('gts,bcsgd->bctgd', wm, vg) + b_spatial.T[None, None, :, :, None]
    y = u * vs.reshape(B, S, SG_WIDTH) * jax.nn.silu(z)
    return jnp.einsum('bse,ed->bsd', y, w_out)

def second_inputs(seed: int = 0) -> dict:
    key = jax.random.key(seed)
    ks = jax.random.split(key, 24)
    f32 = jnp.float32

    def nrm(k, shape, scale):
        return jax.random.normal(k, shape, f32) * scale

    def gain(k, n):
        return 1.0 + 0.05 * jax.random.normal(k, (n,), f32)

    return {
        "x": nrm(ks[0], (BATCH, SEQ, D_MODEL), 1.0),
        "l0_pre_g": gain(ks[1], D_MODEL),
        "l0_w_in": nrm(ks[2], (D_MODEL, EVEN_IN), D_MODEL ** -0.5),
        "l0_b_igate": nrm(ks[3], (ML_HEADS,), 0.1),
        "l0_b_fgate": 3.0 + nrm(ks[4], (ML_HEADS,), 0.5),
        "l0_conv_w": nrm(ks[5], (CONV_WIDTH, 2 * ML_HEADS * ML_QK_DIM), CONV_WIDTH ** -0.5),
        "l0_conv_b": nrm(ks[6], (2 * ML_HEADS * ML_QK_DIM,), 0.02),
        "l0_lambda_q1": nrm(ks[7], (DA_QK_DIM,), 0.1),
        "l0_lambda_k1": nrm(ks[8], (DA_QK_DIM,), 0.1),
        "l0_lambda_q2": nrm(ks[9], (DA_QK_DIM,), 0.1),
        "l0_lambda_k2": nrm(ks[10], (DA_QK_DIM,), 0.1),
        "l0_da_head_g": gain(ks[11], DA_V_DIM),
        "l0_ml_head_g": gain(ks[12], ML_V_DIM),
        "l0_w_out": nrm(ks[13], (DA_WIDTH + ML_WIDTH, D_MODEL), (DA_WIDTH + ML_WIDTH) ** -0.5),
        "l0_post_g": gain(ks[14], D_MODEL),
        "l1_pre_g": gain(ks[15], D_MODEL),
        "l1_w_in": nrm(ks[16], (D_MODEL, ODD_IN), D_MODEL ** -0.5),
        "l1_sg_norm_g": gain(ks[17], SG_WIDTH),
        "l1_w_spatial": nrm(ks[18], (SG_GROUPS, SG_CHUNK, SG_CHUNK), SG_CHUNK ** -0.5),
        "l1_b_spatial": 1.0 + nrm(ks[19], (SG_GROUPS, SG_CHUNK), 0.1),
        "l1_w_out": nrm(ks[20], (SG_WIDTH, D_MODEL), SG_WIDTH ** -0.5),
        "l1_post_g": gain(ks[21], D_MODEL),
    }

def second_block(x, l0_pre_g, l0_w_in, l0_b_igate, l0_b_fgate, l0_conv_w, l0_conv_b,
              l0_lambda_q1, l0_lambda_k1, l0_lambda_q2, l0_lambda_k2, l0_da_head_g,
              l0_ml_head_g, l0_w_out, l0_post_g,
              l1_pre_g, l1_w_in, l1_sg_norm_g, l1_w_spatial, l1_b_spatial, l1_w_out, l1_post_g):
    layers = [
        (l0_pre_g, l0_post_g, (l0_w_in, l0_b_igate, l0_b_fgate, l0_conv_w, l0_conv_b,
                               l0_lambda_q1, l0_lambda_k1, l0_lambda_q2, l0_lambda_k2,
                               l0_da_head_g, l0_ml_head_g, l0_w_out)),
        (l1_pre_g, l1_post_g, (l1_sg_norm_g, l1_w_in, l1_w_spatial, l1_b_spatial, l1_w_out)),
    ]
    h = x
    for l in range(DEPTH_2):
        pre_g, post_g, params = layers[l]
        hn = rmsnorm(h, pre_g)
        if l % 2 == 0:
            y = even_mixer(hn, l, *params)
        else:
            y = odd_mixer(hn, *params)
        h = h + rmsnorm(y, post_g)
    return h


def setup_inputs(seed=0):
    out = dict(first_inputs(seed))
    for name, value in second_inputs(seed + 1).items():
        if name != "x":
            out[name + "_2"] = value
    return out


def reference(
    x, c, ctx, c_ctx, mod_w, mod_b, ln_g, ln_b, ffn_w_in, ffn_w_out, pool_w, pool_scale,
    hgrn_w_in, hgrn_lb_logits, hgrn_norm_w, hgrn_w_out, na_w_qkv, na_rpb, na_w_out, l0_pre_g_2,
    l0_w_in_2, l0_b_igate_2, l0_b_fgate_2, l0_conv_w_2, l0_conv_b_2, l0_lambda_q1_2,
    l0_lambda_k1_2, l0_lambda_q2_2, l0_lambda_k2_2, l0_da_head_g_2, l0_ml_head_g_2, l0_w_out_2,
    l0_post_g_2, l1_pre_g_2, l1_w_in_2, l1_sg_norm_g_2, l1_w_spatial_2, l1_b_spatial_2,
    l1_w_out_2, l1_post_g_2,
):
    x = first_block(
        x, c, ctx, c_ctx, mod_w, mod_b, ln_g, ln_b, ffn_w_in, ffn_w_out, pool_w, pool_scale,
        hgrn_w_in, hgrn_lb_logits, hgrn_norm_w, hgrn_w_out, na_w_qkv, na_rpb, na_w_out,
    )
    return second_block(
        x, l0_pre_g_2, l0_w_in_2, l0_b_igate_2, l0_b_fgate_2, l0_conv_w_2, l0_conv_b_2,
        l0_lambda_q1_2, l0_lambda_k1_2, l0_lambda_q2_2, l0_lambda_k2_2, l0_da_head_g_2,
        l0_ml_head_g_2, l0_w_out_2, l0_post_g_2, l1_pre_g_2, l1_w_in_2, l1_sg_norm_g_2,
        l1_w_spatial_2, l1_b_spatial_2, l1_w_out_2, l1_post_g_2,
    )


_drawn_inputs = setup_inputs


def setup_inputs(seed=0):
    import zlib

    import numpy as np

    out = dict(_drawn_inputs(seed))
    spreads = {}
    factors = {'pool_scale': 8.0,
     'l0_b_igate_2': 64.0,
     'l0_conv_b_2': 4.337,
     'l0_lambda_k2_2': 7.049,
     'l1_sg_norm_g_2': 3.525}
    for name, (base, spread) in spreads.items():
        noise = np.random.default_rng([zlib.crc32(name.encode()), seed]).standard_normal(out[name].shape)
        drawn = base * np.exp(spread * noise) if base else spread * noise
        out[name] = __import__('jax').numpy.asarray(drawn.astype(out[name].dtype))
    for name, factor in factors.items():
        out[name] = (out[name] * factor).astype(out[name].dtype)
    return out
```

```python
import math
from contextlib import ExitStack

import numpy as np

import concourse.bass as bass
from concourse import mybir

F32 = mybir.dt.float32
F32R = mybir.dt.float32r
BF16 = mybir.dt.bfloat16
ALU = mybir.AluOpType
ACT = mybir.ActivationFunctionType
AX_X = mybir.AxisListType.X

P = 128
T = 1024
HALF = 512
D = 1024
KT = D // P
F_TILES = 2816 // P
N_MOD = 6
DA_HEADS, DA_QK, DA_V = 8, 64, 128
ML_HEADS, ML_QK, ML_V, CHUNK, CONV = 4, 128, 256, 128, 4
VA = ML_V + 2
SG_TILES, SG_GROUPS = 16, 8
NC = T // CHUNK
ALPHA = 2.0 ** 0.25
EPS = 1e-6
LAM_INIT = 0.8 - 0.6 * math.exp(0.0)
MASKED = -1e30

PARAMS = [("c", 8), ("mod_b", 48), ("ln_g0", 8), ("ln_b0", 8), ("ln_g1", 8), ("ln_b1", 8),
          ("pool_scale", 8), ("l0_pre_g", 8), ("l0_post_g", 8), ("l1_pre_g", 8), ("l1_post_g", 8),
          ("conv_w", 32), ("conv_b", 8), ("da_g", 1), ("ml_g", 2), ("sg_g", 16), ("gate_b", 1),
          ("lam_q", 2), ("lam_k", 2)]
COL, N_PAR = {}, 0
for _name, _n in PARAMS:
    COL[_name] = N_PAR
    N_PAR += _n

IN_DA = 2 * F_TILES
IN_ML = IN_DA + 4 * DA_HEADS
IN_SV = IN_ML + 8 * ML_HEADS
IN_SG = IN_SV + SG_TILES
N_IN = IN_SG + 2 * SG_TILES
C_GATES = F_TILES
C_DA = C_GATES + 1
C_ML = C_DA + DA_HEADS
C_SG = C_ML + 2 * ML_HEADS
N_C_DRAM = C_SG + SG_TILES
OUT_DA = F_TILES
OUT_ML = OUT_DA + DA_HEADS
OUT_SG = OUT_ML + 2 * ML_HEADS
GATE_STEPS = 5 + 5 * NC


class Beat:

    def __init__(self, sem, per=1, prime=0):
        self.sem, self.per, self.prime = sem, per, prime

    def at(self, turn, event=None):
        event = self.per - 1 if event is None else event
        return turn * self.per + (self.prime * self.per + event + 1)


def build(nc, x_t, params, mod_w, pool_w, w_in, w_c, edges, w_spatial, b_spatial, out):
    with ExitStack() as ctx:
        base = (nc.sbuf_base + 63) // 64 * 64
        place = [base]

        def at_offset(name, shape, dtype, offset):
            return nc.alloc_sbuf_tensor_at(name, shape, dtype, offset=offset)

        def fixed(name, shape, dtype=F32):
            size = int(np.prod(shape[1:])) * (2 if dtype == BF16 else 4)
            tile = at_offset(name, shape, dtype, place[0])
            place[0] += (size + 31) // 32 * 32
            return tile

        raw = [fixed(f"slab_raw{s}", [P, T]) for s in range(3)]
        whi = [fixed(f"slab_hi{s}", [P, KT, P], F32R) for s in range(3)]
        wlo = [fixed(f"slab_lo{s}", [P, KT, P], F32R) for s in range(3)]
        C = 2
        h_base = place[0]
        h_hi = fixed("h_hi", [P, KT, T], F32R)
        h_lo = fixed("h_lo", [P, KT, T], F32R)
        acc = fixed("acc", [P, KT, T])
        ident = fixed("ident", [P, P])
        ones = fixed("ones", [P, P])
        ident_b = fixed("ident_b", [P, P], BF16)
        mask_b = fixed("mask_b", [P, P], BF16)
        causal = fixed("causal", [P, P])
        zero = fixed("zero", [P, 1])
        eps = fixed("eps", [P, 1])
        par = fixed("par", [P, N_PAR])
        mod = fixed("mod", [P, N_MOD * KT])
        silu_c = fixed("silu_c", [P, KT])
        sc1p = fixed("sc1p", [P, KT])
        sc2p = fixed("sc2p", [P, KT])
        pool_gain = fixed("pool_gain", [P, KT])
        res_b0 = fixed("res_b0", [P, KT])
        ffn_b0 = fixed("ffn_b0", [P, KT])
        lam_prod = fixed("lam_prod", [P, 2])
        lam_exp = fixed("lam_exp", [P, 2])
        neg_lam = fixed("neg_lam", [P, 1])
        da_gain = fixed("da_gain", [P, 1])
        stat = fixed("stat", [P, 16])
        stat2 = fixed("stat2", [P, 16])
        ml_cols = fixed("ml_cols", [P, 3, NC])
        ssq = fixed("ssq", [P, NC, SG_TILES])
        resid_base = place[0]
        resid = fixed("resid", [P, KT, T])
        work_base = place[0]
        top = nc.sbuf_usable_end

        def overlay(start):
            cursor = [start]

            def take(name, shape, dtype=F32, at=None):
                size = int(np.prod(shape[1:])) * (2 if dtype == BF16 else 4)
                offset = cursor[0] if at is None else at
                if at is None:
                    cursor[0] += (size + 31) // 32 * 32
                assert offset + size <= top, (name, offset + size - top)
                tile = at_offset(name, shape, dtype, offset)
                return tile, offset
            return take

        def par_col(name, k=0):
            return par[:, COL[name] + k:COL[name] + k + 1]

        MOD_COLS = 6
        mod_big = [at_offset(f"mod_big{b}", [P, MOD_COLS, KT, P], F32, h_base + b * MOD_COLS * KT * P * 4)
                   for b in range(2)]
        take = overlay(work_base)
        PAD = 8
        TP = T + 2 * PAD
        hx = take("hx", [P, TP])[0]
        tree = [take(f"tree{n}", [P, TP])[0] for n in range(4)]
        pw = take("pw", [P, 4, 2, 256])[0]
        edge = take("edge", [P, 32])[0]
        take = overlay(work_base)
        sq = [take(f"sq{b}", [P, T])[0] for b in range(2)]
        mean = take("mean", [P, T])[0]
        rstd = take("rstd", [P, T])[0]
        std = take("std", [P, T])[0]
        tmp = [take(f"tmp{b}", [P, T])[0] for b in range(2)]
        take = overlay(work_base)
        ffn_g = take("ffn_g", [P, T])[0]
        ffn_p = take("ffn_p", [P, T])[0]
        ffn_hi = [take(f"ffn_hi{b}", [P, T], F32R)[0] for b in range(2)]
        ffn_lo = [take(f"ffn_lo{b}", [P, T], F32R)[0] for b in range(2)]
        take = overlay(resid_base)
        g_i, g_f, g_a, g_e, g_l, g_lf, g_cum, g_u, g_max, g_d = (
            take(f"gate_{n}", [ML_HEADS, NC, CHUNK])[0]
            for n in ("i", "f", "abs", "exp", "log", "lf", "cum", "u", "max", "d"))
        g_zero = take("gate_zero", [ML_HEADS, CHUNK])[0]
        g_m = take("gate_m", [ML_HEADS, NC + 1])[0]
        g_iw, g_w, g_emt, g_d2, g_d3 = g_a, g_e, g_l, g_f, g_i
        take = overlay(resid_base)
        q_hi, q_lo, k_hi, k_lo = (take(f"da_{n}", [P, T], F32R)[0] for n in ("qh", "ql", "kh", "kl"))
        v_t = take("da_vt", [P, T])[0]
        v_hi, v_lo = (take(f"da_{n}", [P, KT, P], F32R)[0] for n in ("vh", "vl"))
        da_z = take("da_z", [P, T])[0]
        p_0 = [take(f"da_p0{b}", [P, T])[0] for b in range(2)]
        p_1 = take("da_p1", [P, T])[0]
        a_hi = [take(f"da_ah{b}", [P, KT, P], F32R)[0] for b in range(2)]
        a_lo = [take(f"da_al{b}", [P, KT, P], F32R)[0] for b in range(2)]
        y_hi, y_lo = (take(f"da_{n}", [P, T], F32R)[0] for n in ("yh", "yl"))
        take = overlay(resid_base)
        xp = take("ml_xp", [P, CONV - 1 + T])[0]
        mt = take("ml_t", [P, T])[0]
        (mq_hi, o_q), (mq_lo, _) = (take(f"ml_{n}", [P, T], F32R) for n in ("qh", "ql"))
        (mi_hi, o_i), (mi_lo, _) = (take(f"ml_{n}", [P, T], F32R) for n in ("ih", "il"))
        (mk_hi, o_k), (mk_lo, _) = (take(f"ml_{n}", [P, T], F32R) for n in ("kh", "kl"))
        (kw_hi, o_w), (kw_lo, _) = (take(f"ml_{n}", [P, NC, P], F32R) for n in ("wh", "wl"))
        (va_hi, o_v), (va_lo, _) = (take(f"ml_{n}", [P, NC, VA], F32R) for n in ("vh", "vl"))
        decay_t = take("ml_dt", [P, T])[0]
        hm, o_hm = take("ml_hm", [P, NC, ML_V])
        c_32 = take("ml_c", [P, VA])[0]
        c_hi, c_lo = (take(f"ml_{n}", [P, VA], F32R)[0] for n in ("ch", "cl"))
        iw_b = take("ml_iw", [P, T], at=o_hm)[0]
        v_t0 = take("ml_vt0", [P, T], at=o_hm + 4 * T)[0]
        am_hi, am_lo = (take(f"ml_{n}", [P, T], F32R, at=o_q + 4 * T * n_)[0] for n_, n in enumerate(("ah", "al")))
        ml_so = take("ml_so", [P, NC, ML_V], at=o_v)[0]
        ml_z = [take(f"ml_z{b}", [P, T], at=o_w + 4 * T * b)[0] for b in range(2)]
        my_hi = [take(f"ml_yh{b}", [P, T], F32R, at=(o_i, o_k)[b])[0] for b in range(2)]
        my_lo = [take(f"ml_yl{b}", [P, T], F32R, at=(o_i, o_k)[b] + 4 * T)[0] for b in range(2)]
        take = overlay(resid_base)
        wsp = take("sg_w", [P, SG_GROUPS, P])[0]
        bsp = take("sg_b", [P, SG_GROUPS, P])[0]
        g_t = [take(f"sg_g{b}", [P, T])[0] for b in range(2)]
        g_tok = [take(f"sg_t{b}", [P, NC, P])[0] for b in range(2)]
        wr = take("sg_wr", [P, NC, P])[0]
        wr_hi, wr_lo = (take(f"sg_{n}", [P, NC, P], F32R)[0] for n in ("wrh", "wrl"))
        sg_v = take("sg_v", [P, T])[0]
        sy_hi = [take(f"sg_yh{b}", [P, T], F32R)[0] for b in range(2)]
        sy_lo = [take(f"sg_yl{b}", [P, T], F32R)[0] for b in range(2)]
        sg_u, sg_z = g_t

        ps = ctx.enter_context(nc.psum_tensor("ps", [P, 4 * T], F32))
        PS = [ps[:, n * T:(n + 1) * T] for n in range(4)]

        res_scr = nc.dram_tensor("res_scr", [P, KT, T], F32, kind="Internal").ap()
        gate_scr = nc.dram_tensor("gate_scr", [5, ML_HEADS, T], F32, kind="Internal").ap()
        gv_scr = nc.dram_tensor("gv_scr", [SG_TILES, P, T], F32, kind="Internal").ap()

        def beat(name, per=1, prime=0):
            return Beat(ctx.enter_context(nc.semaphore(name)), per, prime)

        in_load = [beat(f"in_load{s}", 16) for s in range(2)]
        c_load = beat("c_load", 16)
        in_hi, c_hi_done = beat("in_hi"), beat("c_hi")
        in_split, c_split = beat("in_split", 1, 2), beat("c_split", 1, 1)
        in_mm, c_mm = beat("in_mm", 1, 2), beat("c_mm", 1, 1)
        out_mm = beat("out_mm", KT - 1)
        out_ev = beat("out_ev", KT, 1)

        par_ld, x_ld, small_ld = beat("par_ld", 16), beat("x_ld", 16), beat("small_ld", 32)
        mod_ld = [beat(f"mod_ld{b}", 16) for b in range(2)]
        const = beat("const")
        siluc = beat("siluc")
        mod_mm, mod_col = beat("mod_mm", 1, 2), beat("mod_col")
        lam_mm, lam_x, lam_done = beat("lam_mm"), beat("lam_x"), beat("lam_done")
        px, px_step, p_done = beat("px"), beat("px_step"), beat("p_done")
        x_scaled, pool_mm, z_done = beat("x_scaled"), beat("pool_mm"), beat("z_done")
        n_mean_mm, n_mean, n_cent = beat("n_mean_mm"), beat("n_mean"), beat("n_cent", KT)
        n_sq, n_ssum, n_std, n_rstd = beat("n_sq", KT), beat("n_ssum", KT), beat("n_std"), beat("n_rstd")
        n_out = beat("n_out", KT)
        s_tmp, s_hi, s_lo = beat("s_tmp", KT), beat("s_hi", KT), beat("s_lo", KT)
        n_res, n_gain = beat("n_res", KT), beat("n_gain", KT)
        spill, refill, acc_zero = beat("spill", 16), beat("refill", 16), beat("acc_zero")
        post_t, post_h = beat("post_t", KT), beat("post_h", KT)
        store = beat("store", 16)

        f_silu, f_mul, f_hi, f_lo = beat("f_silu", 1, 1), beat("f_mul", 1, 1), beat("f_hi"), beat("f_lo", 1, 1)

        g_in, g_act, g_dve, g_st = beat("g_in"), beat("g_act"), beat("g_dve"), beat("g_st", 16)

        a_qh, a_kh, a_vt, a_z, a_vh = (beat(f"a_{n}") for n in ("qh", "kh", "vt", "z", "vh"))
        a_ql, a_kl, a_vl = (beat(f"a_{n}") for n in ("ql", "kl", "vl"))
        a_vtr, a_score, a_tr, a_pv, a_ss = (beat("a_vtr"), beat("a_score", 16), beat("a_tr", 8), beat("a_pv"), beat("a_ss"))
        a_max, a_exp, a_rec, a_nr = beat("a_max", 16), beat("a_exp", 16), beat("a_rec", 8), beat("a_nr", 8)
        a_p0, a_mix, a_hi_d, a_lo_d = beat("a_p0", 8), beat("a_mix", 8), beat("a_hi_d", 8), beat("a_lo_d", 8)
        a_sq, a_std, a_r, a_on, a_y, a_yh, a_yl = (beat(f"a_{n}") for n in ("sq", "std", "r", "on", "y", "yh", "yl"))

        m_ld = beat("m_ld", 80)
        m_x, m_conv, m_silu, m_q = beat("m_x", 2), beat("m_conv", 8), beat("m_silu", 2), beat("m_q", 2)
        m_qkh, m_qkl, m_vt, m_vh, m_vl = beat("m_qkh", 3), beat("m_qkl", 3), beat("m_vt", 2), beat("m_vh", 2), beat("m_vl", 6)
        m_ktr, m_kw, m_kwh, m_kwl = beat("m_ktr"), beat("m_kw", 8), beat("m_kwh"), beat("m_kwl")
        m_vtr, m_dt, m_de, m_mask = beat("m_vtr", 2), beat("m_dt", 8), beat("m_de"), beat("m_mask")
        m_s, m_am, m_ah, m_al = beat("m_s"), beat("m_am"), beat("m_ah"), beat("m_al")
        m_p, m_c, m_ch, m_cl, m_num = beat("m_p", 7), beat("m_c", 7), beat("m_ch", 7), beat("m_cl", 7), beat("m_num", 8)
        m_den, m_rd, m_hm = beat("m_den", 1 + 2 * NC), beat("m_rd", NC), beat("m_hm", NC)
        m_ot, m_otr, m_so, m_g = beat("m_ot", 2), beat("m_otr", 2), beat("m_so", 2), beat("m_g")
        m_ss, m_std, m_r, m_n = beat("m_ss", 8), beat("m_std"), beat("m_r"), beat("m_n", 8)
        m_ntr, m_z, m_y, m_yh, m_yl = beat("m_ntr", 2), beat("m_z", 2), beat("m_y", 4), beat("m_yh", 2), beat("m_yl", 2)

        v_g, v_tr, v_tok, v_sq = beat("v_g", 1, 2), beat("v_tr", 1, 2), beat("v_tok", 1, 2), beat("v_sq", 8, 2)
        v_st = [beat(f"v_st{b}", 16, 1) for b in range(2)]
        v_r = beat("v_r")
        w_s, w_h, w_l = beat("w_s", 8, 1), beat("w_h", 1, 1), beat("w_l", 1, 1)
        e_vs, e_u, e_z, e_v, e_y, e_yh, e_yl = (beat("e_vs"), beat("e_u", 1, 1), beat("e_z", 1, 1), beat("e_v", 1, 1),
                                              beat("e_y", 2, 1), beat("e_yh"), beat("e_yl", 1, 1))
        sp_ld = beat("sp_ld", 32)

        block = ctx.enter_context(nc.Block())

        @block.sync
        def _(sp):
            def load_in(n, slot):
                sp.wait_ge(in_split.sem, in_split.at(n - 2))
                sp.dma_start(raw[slot][:], w_in[bass.ds(n, 1)].rearrange("a p t -> p (a t)"))\
                  .then_inc(in_load[slot].sem, 16)

            def load_c(n, source, row):
                sp.wait_ge(c_split.sem, c_split.at(n - 1))
                sp.dma_start(raw[C][:], source[bass.ds(row, 1)].rearrange("a p t -> p (a t)"))\
                  .then_inc(c_load.sem, 16)

            sp.dma_start(resid[:], x_t).then_inc(x_ld.sem, 16)
            with sp.Fori(0, 2) as half:
                for j in range(4):
                    sp.wait_ge(mod_mm.sem, mod_mm.at(half * 4 + (j - 2)))
                    sp.dma_start(mod_big[j % 2][:], mod_w[bass.ds(half * 4 + j, 1)].rearrange("a p m k f -> p (a m) k f"))\
                      .then_inc(mod_ld[j % 2].sem, 16)
            load_in(0, 0)
            load_in(1, 1)
            with sp.Fori(1, F_TILES) as f:
                load_in(2 * f, 0)
                load_in(2 * f + 1, 1)
                load_c(f - 1, w_c, f - 1)
            load_c(F_TILES - 1, w_c, F_TILES - 1)
            load_c(C_GATES, w_c, C_GATES)
            for s in range(4):
                load_in(IN_DA + s, s % 2)
            with sp.Fori(1, DA_HEADS) as h:
                for s in range(4):
                    load_in(IN_DA + 4 * h + s, s % 2)
                    if s == 1:
                        load_c(C_DA + h - 1, w_c, C_DA + h - 1)
            load_c(C_DA + DA_HEADS - 1, w_c, C_DA + DA_HEADS - 1)
            with sp.Fori(0, ML_HEADS) as h:
                for s in range(8):
                    load_in(IN_ML + 8 * h + s, s % 2)
                for s in range(2):
                    load_c(C_ML + 2 * h + s, w_c, C_ML + 2 * h + s)
            with sp.Fori(0, SG_TILES // 2) as j:
                for s in range(2):
                    load_in(IN_SV + 2 * j + s, s)
            for b in range(2):
                sp.wait_ge(v_st[b].sem, v_st[b].at(SG_TILES // 2 - 1))
            load_in(IN_SG, 0)
            load_c(C_SG, gv_scr, 0)
            load_in(IN_SG + 1, 1)
            with sp.Fori(1, SG_TILES) as d:
                load_in(IN_SG + 2 * d, 0)
                load_c(C_SG + 2 * d - 1, gv_scr, d)
                load_in(IN_SG + 2 * d + 1, 1)
                load_c(C_SG + 2 * d, w_c, C_SG + d - 1)
            load_c(C_SG + 2 * SG_TILES - 1, w_c, C_SG + SG_TILES - 1)
            for k in range(KT):
                sp.wait_ge(post_h.sem, post_h.at(1, k))
                sp.dma_start(out[:, k, :], resid[:, k, :]).then_inc(store.sem, 16)
            sp.wait_ge(store.sem, 16 * KT)

        @block.gpsimd
        def _(pool):
            zeros = zero[:, 0:1].to_broadcast([P, T])
            pool.memset(ident[:], 0.0).then_inc(const.sem, 1)
            pool.memset(ident_b[:], 0.0).then_inc(const.sem, 1)
            pool.memset(mask_b[:], 0.0).then_inc(const.sem, 1)
            pool.memset(ones[:], 1.0).then_inc(const.sem, 1)
            pool.memset(causal[:], 1.0).then_inc(const.sem, 1)
            pool.memset(zero[:], 0.0).then_inc(const.sem, 1)
            pool.memset(eps[:], EPS).then_inc(const.sem, 1)
            pool.memset(hx[:], 0.0).then_inc(const.sem, 1)
            pool.wait_ge(const.sem, 8)
            for tile in (ident, ident_b):
                pool.affine_select(out=tile[:], in_=tile[:], compare_op=ALU.not_equal, fill=1.0, base=0,
                                   pattern=[[-1, P]], channel_multiplier=1).then_inc(const.sem, 1)
            pool.affine_select(out=mask_b[:], in_=mask_b[:], compare_op=ALU.is_ge, fill=MASKED, base=0,
                               pattern=[[-1, P]], channel_multiplier=1).then_inc(const.sem, 1)
            pool.affine_select(out=causal[:], in_=causal[:], compare_op=ALU.is_ge, fill=0.0, base=0,
                               pattern=[[1, P]], channel_multiplier=-1).then_inc(const.sem, 1)
            pool.sem_inc(in_split.sem, in_split.prime)
            pool.sem_inc(c_split.sem, c_split.prime)

            def split(n, slot, load, load_value, hi_done, used, done):
                pool.wait_ge(load.sem, load_value)
                pool.wait_ge(used.sem, used.at(n - used.prime))
                hi = whi[slot][:].rearrange("p k f -> p (k f)")
                pool.tensor_tensor(hi, raw[slot][:], zeros, ALU.add).then_inc(hi_done.sem, 1)
                pool.wait_ge(hi_done.sem, hi_done.at(n))
                pool.tensor_tensor(wlo[slot][:].rearrange("p k f -> p (k f)"), raw[slot][:], hi.bitcast(F32),
                                   ALU.subtract).then_inc(done.sem, 1)

            def split_in(n, slot, turn):
                split(n, slot, in_load[slot], in_load[slot].at(turn), in_hi, in_mm, in_split)

            def split_c(n):
                split(n, C, c_load, c_load.at(n), c_hi_done, c_mm, c_split)

            split_in(0, 0, 0)
            split_in(1, 1, 0)
            pool.wait_ge(z_done.sem, KT)
            pool.memset(acc[:], 0.0).then_inc(acc_zero.sem, 1)
            with pool.Fori(1, F_TILES) as f:
                split_in(2 * f, 0, f)
                split_in(2 * f + 1, 1, f)
                split_c(f - 1)
            split_c(F_TILES - 1)
            split_c(C_GATES)
            for s in range(4):
                split_in(IN_DA + s, s % 2, (IN_DA + s) // 2)
            with pool.Fori(1, DA_HEADS) as h:
                for s in range(4):
                    split_in(IN_DA + 4 * h + s, s % 2, 2 * h + (IN_DA + s) // 2)
                    if s == 1:
                        split_c(C_DA + h - 1)
            split_c(C_DA + DA_HEADS - 1)
            with pool.Fori(0, ML_HEADS) as h:
                for s in range(8):
                    split_in(IN_ML + 8 * h + s, s % 2, 4 * h + (IN_ML + s) // 2)
                    if s == 3:
                        pool.wait_ge(m_de.sem, m_de.at(h))
                        dt3 = decay_t[:].rearrange("s (c t) -> s c t", t=CHUNK)
                        pool.tensor_tensor(dt3, dt3, causal[:].unsqueeze(1).to_broadcast([P, NC, P]), ALU.mult).then_inc(m_mask.sem, 1)
                for s in range(2):
                    split_c(C_ML + 2 * h + s)
            pool.wait_ge(post_h.sem, post_h.at(0))
            pool.memset(acc[:], 0.0).then_inc(acc_zero.sem, 1)
            pool.wait_ge(sp_ld.sem, sp_ld.at(0))
            pool.tensor_tensor(wsp[:], wsp[:], causal[:].unsqueeze(1).to_broadcast([P, SG_GROUPS, P]), ALU.mult).then_inc(const.sem, 1)
            with pool.Fori(0, SG_TILES // 2) as j:
                for s in range(2):
                    split_in(IN_SV + 2 * j + s, s, j + IN_SV // 2)
            split_in(IN_SG, 0, IN_SG // 2)
            split_c(C_SG)
            split_in(IN_SG + 1, 1, IN_SG // 2)
            with pool.Fori(1, SG_TILES) as d:
                split_in(IN_SG + 2 * d, 0, d + IN_SG // 2)
                split_c(C_SG + 2 * d - 1)
                split_in(IN_SG + 2 * d + 1, 1, d + IN_SG // 2)
                split_c(C_SG + 2 * d)
            split_c(C_SG + 2 * SG_TILES - 1)

        @block.tensor
        def _(pe):
            pe.sem_inc(in_mm.sem, in_mm.prime)
            pe.sem_inc(c_mm.sem, c_mm.prime)
            pe.sem_inc(mod_mm.sem, mod_mm.prime)
            pe.sem_inc(v_tr.sem, v_tr.prime)

            def three(dst, w_h, w_l, r_h, r_l, first, last):
                pe.matmul(dst, w_h, r_h, start=first, stop=False, skip_group_check=True)
                pe.matmul(dst, w_h, r_l, start=False, stop=False, skip_group_check=True)
                return pe.matmul(dst, w_l, r_h, start=False, stop=last, skip_group_check=True)

            def project(n, slot, stream=in_split, done=in_mm, bank=None):
                dst = PS[slot if bank is None else bank]
                pe.wait_ge(stream.sem, stream.at(n))
                for t0 in (0, HALF):
                    for k in range(KT):
                        mm = three(dst[:, t0:t0 + HALF], whi[slot][:, k, :], wlo[slot][:, k, :],
                                   h_hi[:, k, t0:t0 + HALF], h_lo[:, k, t0:t0 + HALF], k == 0, k == KT - 1)
                mm.then_inc(done.sem, 1)

            def project_out(n, o, r_h, r_l):
                pe.wait_ge(c_split.sem, c_split.at(n))
                for d in range(KT):
                    dst = PS[2 + d % 2]
                    if d >= 2:
                        pe.wait_ge(out_ev.sem, out_ev.at(o, d - 2))
                    else:
                        pe.wait_ge(out_ev.sem, out_ev.at(o - 1, KT - 2 + d))
                    for t0 in (0, HALF):
                        mm = three(dst[:, t0:t0 + HALF], whi[C][:, d, :], wlo[C][:, d, :],
                                   r_h[:, t0:t0 + HALF], r_l[:, t0:t0 + HALF], True, True)
                    if d < KT - 1:
                        mm.then_inc(out_mm.sem, 1)
                    else:
                        mm.then_inc(c_mm.sem, 1)

            def sum_squares(norm):
                for k in range(KT):
                    pe.wait_ge(n_sq.sem, n_sq.at(norm, k))
                    for t0 in (0, HALF):
                        mm = pe.matmul(PS[0][:, t0:t0 + HALF], ones[:], sq[k % 2][:, t0:t0 + HALF],
                                       start=(k == 0), stop=(k == KT - 1), skip_group_check=True)
                    mm.then_inc(n_ssum.sem, 1)

            def turn_tiles(dst, src, sem):
                for b in range(KT):
                    mm = pe.transpose(dst[:, b * P:(b + 1) * P], src(b), ident[:])
                mm.then_inc(sem, 1)

            pe.wait_ge(const.sem, 12)
            pe.wait_ge(siluc.sem, 1)
            with pe.Fori(0, 2) as half:
                for j in range(4):
                    pe.wait_ge(mod_ld[j % 2].sem, mod_ld[j % 2].at(half * 2 + j // 2))
                    for m in range(MOD_COLS):
                        for k in range(KT):
                            mm = pe.matmul(ps[:, bass.ds(half * T + (2 * T + j * MOD_COLS + m), 1)],
                                           mod_big[j % 2][:, m, k, :], silu_c[:, k:k + 1],
                                           start=(k == 0), stop=(k == KT - 1), skip_group_check=True)
                    mm.then_inc(mod_mm.sem, 1)
            pe.wait_ge(lam_done.sem, 1)
            pe.matmul(PS[1][:, 0:2], ones[:], lam_prod[:], start=True, stop=True).then_inc(lam_mm.sem, 1)
            pe.wait_ge(small_ld.sem, small_ld.at(0))
            pe.wait_ge(lam_x.sem, 1)
            for j in range(KT):
                g, e = j // 2, j % 2
                pe.wait_ge(p_done.sem, 2 * g + 2)
                if j >= 2:
                    pe.wait_ge(z_done.sem, j - 1)
                for t0 in (0, HALF):
                    for k in range(2):
                        mm = pe.matmul(PS[e][:, t0:t0 + HALF], pw[:, g, k, e * P:(e + 1) * P],
                                       acc[:, 2 * g + k, t0:t0 + HALF], start=(k == 0), stop=(k == 1),
                                       skip_group_check=True)
                mm.then_inc(pool_mm.sem, 1)

            def mean_of(norm, ready, count):
                for k in range(KT):
                    pe.wait_ge(ready, count(k))
                    for t0 in (0, HALF):
                        mm = pe.matmul(PS[2][:, t0:t0 + HALF], ones[:], resid[:, k, t0:t0 + HALF],
                                       start=(k == 0), stop=(k == KT - 1), skip_group_check=True)
                mm.then_inc(n_mean_mm.sem, 1)

            pe.wait_ge(mod_col.sem, 2)
            mean_of(0, z_done.sem, lambda k: k + 1)
            sum_squares(0)
            pe.wait_ge(n_std.sem, 1)
            pe.wait_ge(s_lo.sem, s_lo.at(0))

            def ffn_in(f):
                pe.wait_ge(f_silu.sem, f_silu.at(f - 1))
                project(2 * f, 0)
                pe.wait_ge(f_mul.sem, f_mul.at(f - 1))
                project(2 * f + 1, 1)

            def ffn_out(f, b):
                pe.wait_ge(f_lo.sem, f_lo.at(f))
                project_out(f, f, ffn_hi[b], ffn_lo[b])

            ffn_in(0)
            with pe.Fori(0, F_TILES // 2 - 1) as j:
                for b in range(2):
                    ffn_in(2 * j + (1 + b))
                    ffn_out(2 * j + b, b)
            ffn_in(F_TILES - 1)
            ffn_out(F_TILES - 2, 0)
            ffn_out(F_TILES - 1, 1)
            for k in range(KT):
                pe.wait_ge(out_ev.sem, out_ev.at(F_TILES - 1, k))
                for t0 in (0, HALF):
                    if k == 0 and t0 == 0:
                        pe.wait_ge(out_ev.sem, out_ev.at(F_TILES - 1))
                    mm = pe.matmul(PS[2][:, t0:t0 + HALF], ones[:], resid[:, k, t0:t0 + HALF],
                                   start=(k == 0), stop=(k == KT - 1), skip_group_check=True)
            mm.then_inc(n_mean_mm.sem, 1)
            sum_squares(1)
            pe.wait_ge(n_std.sem, n_std.at(1))
            sum_squares(2)
            pe.wait_ge(n_std.sem, n_std.at(2))
            pe.wait_ge(s_lo.sem, s_lo.at(1))
            project(C_GATES, C, c_split, c_mm, bank=0)
            pe.wait_ge(g_in.sem, 2)

            def da_head(h, first):
                project(IN_DA + 4 * h, 0)
                project(IN_DA + 4 * h + 1, 1)
                if not first:
                    da_out(h - 1)
                pe.wait_ge(a_ql.sem, a_ql.at(h))
                project(IN_DA + 4 * h + 2, 0)
                pe.wait_ge(a_kl.sem, a_kl.at(h))
                project(IN_DA + 4 * h + 3, 1)
                pe.wait_ge(a_vt.sem, a_vt.at(h))
                pe.wait_ge(out_ev.sem, out_ev.at(OUT_DA + h - 1))
                turn_tiles(PS[2], lambda b: v_t[:, b * P:(b + 1) * P], a_vtr.sem)
                pe.wait_ge(a_z.sem, a_z.at(h))
                da_scores(h, 0)
                for i in range(KT):
                    if i + 1 < KT:
                        da_scores(h, i + 1)
                    pe.wait_ge(a_mix.sem, a_mix.at(h, i))
                    if i == 0:
                        pe.wait_ge(a_vl.sem, a_vl.at(h))
                    else:
                        pe.wait_ge(a_lo_d.sem, a_lo_d.at(h, i - 1))
                    for b in range(i + 1):
                        mm = pe.transpose(PS[2][:, b * P:(b + 1) * P], p_0[i % 2][:, b * P:(b + 1) * P], ident[:])
                    mm.then_inc(a_tr.sem, 1)
                    if i >= 1:
                        da_values(h, i - 1)
                da_values(h, KT - 1).then_inc(a_pv.sem, 1)
                pe.wait_ge(a_sq.sem, a_sq.at(h))
                for t0 in (0, HALF):
                    mm = pe.matmul(PS[2][:, t0:t0 + HALF], ones[:], v_t[:, t0:t0 + HALF], start=True, stop=True,
                                   skip_group_check=True)
                mm.then_inc(a_ss.sem, 1)

            def da_scores(h, i):
                for c in range(2):
                    rows = slice(c * DA_QK, (c + 1) * DA_QK)
                    cols = slice(i * P, (i + 1) * P)
                    if i >= 1:
                        pe.wait_ge(a_exp.sem, a_exp.at(h, 2 * (i - 1) + c))
                    for t0 in range(0, (i + 1) * P, HALF):
                        t1 = min(t0 + HALF, (i + 1) * P)
                        mm = three(PS[c][:, t0:t1], q_hi[rows, cols], q_lo[rows, cols],
                                   k_hi[rows, t0:t1], k_lo[rows, t0:t1], True, True)
                    mm = pe.matmul(PS[c][:, cols], ident_b[:], mask_b[:], start=False, stop=True, skip_group_check=True)
                    mm.then_inc(a_score.sem, 1)

            def da_values(h, i):
                pe.wait_ge(a_lo_d.sem, a_lo_d.at(h, i))
                for b in range(i + 1):
                    mm = three(PS[3][:, i * P:(i + 1) * P], v_hi[:, b, :], v_lo[:, b, :],
                               a_hi[i % 2][:, b, :], a_lo[i % 2][:, b, :], b == 0, b == i)
                return mm

            def da_out(h):
                pe.wait_ge(a_yl.sem, a_yl.at(h))
                project_out(C_DA + h, OUT_DA + h, y_hi, y_lo)

            da_head(0, True)
            with pe.Fori(1, DA_HEADS) as h:
                da_head(h, False)
            da_out(DA_HEADS - 1)

            with pe.Fori(0, ML_HEADS) as h:
                project(IN_ML + 8 * h, 0)
                project(IN_ML + 8 * h + 1, 1)
                pe.wait_ge(m_x.sem, m_x.at(h, 0))
                project(IN_ML + 8 * h + 2, 0)
                pe.wait_ge(m_x.sem, m_x.at(h, 1))
                project(IN_ML + 8 * h + 3, 1)
                pe.wait_ge(out_ev.sem, out_ev.at(OUT_ML + 2 * h - 1))
                pe.wait_ge(m_silu.sem, m_silu.at(h, 1))
                turn_tiles(PS[2], lambda b: mt[:, b * P:(b + 1) * P], m_ktr.sem)
                pe.wait_ge(m_qkl.sem, m_qkl.at(h, 2))
                for c in range(NC):
                    cols = slice(c * CHUNK, (c + 1) * CHUNK)
                    mm = three(PS[3][:, cols], mk_hi[:, cols], mk_lo[:, cols], mq_hi[:, cols], mq_lo[:, cols], True, True)
                mm.then_inc(m_s.sem, 1)
                pe.wait_ge(m_vt.sem, m_vt.at(h, 0))
                turn_tiles(PS[0], lambda b: v_t0[:, b * P:(b + 1) * P], m_vtr.sem)
                pe.wait_ge(m_vt.sem, m_vt.at(h, 1))
                turn_tiles(PS[1], lambda b: mt[:, b * P:(b + 1) * P], m_vtr.sem)

                def state_part(c):
                    if c >= 2:
                        pe.wait_ge(m_c.sem, m_c.at(h, c - 2))
                    dst = PS[3][:, (c % 2) * HALF:(c % 2) * HALF + VA]
                    three(dst, kw_hi[:, c, :], kw_lo[:, c, :], va_hi[:, c, :], va_lo[:, c, :], True, True)\
                        .then_inc(m_p.sem, 1)

                pe.wait_ge(m_kwl.sem, m_kwl.at(h))
                pe.wait_ge(m_vl.sem, m_vl.at(h))
                pe.wait_ge(m_am.sem, m_am.at(h))
                state_part(0)
                pe.wait_ge(m_al.sem, m_al.at(h))
                for c in range(NC):
                    if c + 1 < NC - 1:
                        state_part(c + 1)
                    if c >= 2:
                        pe.wait_ge(m_hm.sem, m_hm.at(h, c - 2))
                    cols = slice(c * CHUNK, (c + 1) * CHUNK)
                    dst = PS[2][:, (c % 2) * HALF:(c % 2) * HALF + VA]
                    mm = three(dst, am_hi[:, cols], am_lo[:, cols], va_hi[:, c, :], va_lo[:, c, :], True, c == 0)
                    if c >= 1:
                        pe.wait_ge(m_cl.sem, m_cl.at(h, c - 1))
                        mm = three(dst, mi_hi[:, cols], mi_lo[:, cols], c_hi[:], c_lo[:], False, True)
                    mm.then_inc(m_num.sem, 1)
                project(IN_ML + 8 * h + 4, 0)
                project(IN_ML + 8 * h + 5, 1)
                for e in range(2):
                    pe.wait_ge(m_ot.sem, m_ot.at(h, e))
                    if e == 0:
                        pe.wait_ge(m_hm.sem, m_hm.at(h))
                    turn_tiles(PS[2 + e], lambda b: (xp[:, b * P:(b + 1) * P], mt[:, b * P:(b + 1) * P])[e], m_otr.sem)
                project(IN_ML + 8 * h + 6, 0)
                project(IN_ML + 8 * h + 7, 1)
                pe.wait_ge(m_n.sem, m_n.at(h))
                for e in range(2):
                    turn_tiles(PS[2 + e], lambda b: hm[:, b, e * P:(e + 1) * P], m_ntr.sem)
                for e in range(2):
                    pe.wait_ge(m_yl.sem, m_yl.at(h, e))
                    if e == 0:
                        pe.wait_ge(m_y.sem, m_y.at(h, 1))
                    project_out(C_ML + 2 * h + e, OUT_ML + 2 * h + e, my_hi[e], my_lo[e])

            pe.wait_ge(m_z.sem, m_z.at(ML_HEADS - 1))
            sum_squares(3)
            pe.wait_ge(n_std.sem, n_std.at(3))
            sum_squares(4)
            pe.wait_ge(n_std.sem, n_std.at(4))
            pe.wait_ge(s_lo.sem, s_lo.at(2))

            with pe.Fori(0, SG_TILES // 2) as j:
                for s in range(2):
                    pe.wait_ge(v_g.sem, v_g.at(2 * j + (s - 2)))
                    project(IN_SV + 2 * j + s, s)
                for s in range(2):
                    pe.wait_ge(v_g.sem, v_g.at(2 * j + s))
                    pe.wait_ge(v_tok.sem, v_tok.at(2 * j + (s - 2)))
                    turn_tiles(PS[2 + s], lambda b: g_t[s][:, b * P:(b + 1) * P], v_tr.sem)

            def sg_tile(d, e, g, first):
                pe.wait_ge(e_u.sem, e_u.at(d - 1))
                if first and e == 0:
                    pe.wait_ge(v_tok.sem, v_tok.at(SG_TILES - 1))
                project(IN_SG + 2 * d, 0)
                n = C_SG if first and e == 0 else C_SG + 2 * d - 1
                pe.wait_ge(w_l.sem, w_l.at(g))
                pe.wait_ge(e_v.sem, e_v.at(d - 1))
                pe.wait_ge(c_split.sem, c_split.at(n))
                pe.wait_ge(out_ev.sem, out_ev.at(OUT_SG + d - 2))
                for c in range(NC):
                    mm = three(PS[2][:, c * CHUNK:(c + 1) * CHUNK], whi[C][:, c, :], wlo[C][:, c, :],
                               wr_hi[:, c, :], wr_lo[:, c, :], True, True)
                mm.then_inc(c_mm.sem, 1)
                pe.wait_ge(e_z.sem, e_z.at(d - 1))
                project(IN_SG + 2 * d + 1, 1)

            def sg_out(d, e, n):
                pe.wait_ge(e_yl.sem, e_yl.at(d))
                project_out(n, OUT_SG + d, sy_hi[e], sy_lo[e])

            sg_tile(0, 0, 0, True)
            sg_tile(1, 1, 0, True)
            pe.wait_ge(e_v.sem, e_v.at(1))
            sg_out(0, 0, C_SG + 2)
            with pe.Fori(1, SG_GROUPS) as g:
                for e in range(2):
                    sg_tile(2 * g + e, e, g, False)
                    pe.wait_ge(e_v.sem, e_v.at(2 * g + e))
                    sg_out(2 * g + (e - 1), 1 - e, C_SG + 4 * g + 2 * e)
            sg_out(SG_TILES - 1, 1, C_SG + 2 * SG_TILES - 1)
            pe.wait_ge(e_z.sem, e_z.at(SG_TILES - 1))
            sum_squares(5)

        @block.scalar
        def _(act):
            for b in (f_silu, v_g, v_sq, w_h, e_u, e_z):
                act.sem_inc(b.sem, b.prime * b.per)
            for b in v_st:
                act.sem_inc(b.sem, b.prime * b.per)
            act.dma_start(par[:], params).then_inc(par_ld.sem, 16)
            act.dma_start(pw[:], pool_w).then_inc(small_ld.sem, 16)
            act.dma_start(edge[:], edges).then_inc(small_ld.sem, 16)
            act.wait_ge(par_ld.sem, 16)
            act.activation(silu_c[:], par[:, COL["c"]:COL["c"] + KT], ACT.Silu).then_inc(siluc.sem, 1)
            act.wait_ge(lam_mm.sem, 1)
            act.activation(lam_exp[:], PS[1][:, 0:2], ACT.Exp).then_inc(lam_x.sem, 1)
            for k in range(KT):
                act.wait_ge(px.sem, k + 1)
                act.activation(resid[:, k, :], resid[:, k, :], ACT.Copy, scale=ALPHA).then_inc(x_scaled.sem, 1)

            def square(norm, src, ready, value):
                for k in range(KT):
                    act.wait_ge(ready, value(k))
                    if k >= 2:
                        act.wait_ge(n_ssum.sem, n_ssum.at(norm, k - 2))
                    act.activation(sq[k % 2][:], src[:, k, :], ACT.Square).then_inc(n_sq.sem, 1)
                act.wait_ge(n_ssum.sem, n_ssum.at(norm))
                act.activation(std[:], PS[0], ACT.Sqrt, bias=eps[:, 0:1], scale=1.0 / D).then_inc(n_std.sem, 1)

            def mean_out(norm):
                act.wait_ge(n_mean_mm.sem, n_mean_mm.at(norm))
                act.activation(mean[:], PS[2], ACT.Copy, scale=1.0 / D).then_inc(n_mean.sem, 1)

            def split_high(use):
                for k in range(KT):
                    act.wait_ge(s_tmp.sem, s_tmp.at(use, k))
                    act.activation(h_hi[:, k, :], tmp[k % 2][:], ACT.Copy).then_inc(s_hi.sem, 1)

            mean_out(0)
            square(0, resid, n_cent.sem, lambda k: n_cent.at(0, k))
            for k in range(KT):
                act.wait_ge(s_tmp.sem, s_tmp.at(0, k))
                act.activation(h_hi[:, k, :], tmp[k % 2][:], ACT.Copy).then_inc(s_hi.sem, 1)
                act.activation(resid[:, k, :], resid[:, k, :], ACT.Identity, scale=ALPHA,
                               bias=res_b0[:, k:k + 1]).then_inc(n_res.sem, 1)

            def ffn(f, b):
                act.wait_ge(in_mm.sem, in_mm.at(2 * f))
                act.wait_ge(f_mul.sem, f_mul.at(f - 1))
                act.activation(ffn_g[:], PS[0], ACT.Silu).then_inc(f_silu.sem, 1)
                act.wait_ge(f_mul.sem, f_mul.at(f))
                act.activation(ffn_hi[b][:], ffn_p[:], ACT.Copy).then_inc(f_hi.sem, 1)

            act.wait_ge(s_lo.sem, s_lo.at(0))
            with act.Fori(0, F_TILES // 2) as j:
                for b in range(2):
                    ffn(2 * j + b, b)

            mean_out(1)
            square(1, resid, n_cent.sem, lambda k: n_cent.at(1, k))
            square(2, resid, n_out.sem, lambda k: n_out.at(1, k))
            act.dma_start(res_scr, resid[:]).then_inc(spill.sem, 16)
            split_high(1)

            act.wait_ge(s_lo.sem, s_lo.at(1))
            act.wait_ge(spill.sem, spill.at(0))
            act.wait_ge(c_mm.sem, c_mm.at(C_GATES))
            gb = COL["gate_b"]
            flat = lambda tile: tile[:].rearrange("h c t -> h (c t)")
            act.activation(flat(g_i), PS[0][0:4, :], ACT.Identity, bias=par[0:4, gb:gb + 1]).then_inc(g_in.sem, 1)
            act.activation(flat(g_f), PS[0][32:36, :], ACT.Identity, bias=par[32:36, gb:gb + 1]).then_inc(g_in.sem, 1)
            act.wait_ge(g_in.sem, 2)
            act.activation(g_a[:], g_f[:], ACT.Abs).then_inc(g_act.sem, 1)
            act.wait_ge(g_act.sem, 1)
            act.activation(g_e[:], g_a[:], ACT.Exp, scale=-1.0).then_inc(g_act.sem, 1)
            act.wait_ge(g_act.sem, 2)
            act.activation(g_l[:], g_e[:], ACT.Ln, bias=ones[0:4, 0:1]).then_inc(g_act.sem, 1)

            def gate_rows():
                act.wait_ge(g_dve.sem, GATE_STEPS)
                act.activation(g_iw[:], g_d[:], ACT.Exp, scale=-1.0).then_inc(g_act.sem, 1)
                act.activation(g_emt[:], g_d2[:], ACT.Exp, scale=-1.0).then_inc(g_act.sem, 1)
                act.activation(g_w[:], g_d3[:], ACT.Exp).then_inc(g_act.sem, 1)
                act.wait_ge(g_act.sem, 6)
                for n, row in enumerate((g_max, g_iw, g_u, g_w, g_emt)):
                    act.dma_start(gate_scr[n], flat(row)).then_inc(g_st.sem, 16)

            def da_head(h, first):
                act.wait_ge(in_mm.sem, in_mm.at(IN_DA + 4 * h))
                act.activation(q_hi[:], PS[0], ACT.Copy, scale=DA_QK ** -0.5).then_inc(a_qh.sem, 1)
                act.wait_ge(in_mm.sem, in_mm.at(IN_DA + 4 * h + 1))
                act.activation(k_hi[:], PS[1], ACT.Copy).then_inc(a_kh.sem, 1)
                act.wait_ge(in_mm.sem, in_mm.at(IN_DA + 4 * h + 2))
                act.activation(v_t[:], PS[0], ACT.Copy).then_inc(a_vt.sem, 1)
                act.wait_ge(in_mm.sem, in_mm.at(IN_DA + 4 * h + 3))
                act.activation(da_z[:], PS[1], ACT.Silu).then_inc(a_z.sem, 1)
                act.wait_ge(a_vtr.sem, a_vtr.at(h))
                act.activation(v_hi[:].rearrange("p b v -> p (b v)"), PS[2], ACT.Copy).then_inc(a_vh.sem, 1)
                da_exp(h, 0)
                for i in range(KT):
                    if i + 1 < KT:
                        da_exp(h, i + 1)
                    act.wait_ge(a_tr.sem, a_tr.at(h, i))
                    act.activation(a_hi[i % 2][:, 0:i + 1, :].rearrange("p b q -> p (b q)"),
                                   PS[2][:, 0:(i + 1) * P], ACT.Copy).then_inc(a_hi_d.sem, 1)
                act.wait_ge(a_pv.sem, a_pv.at(h))
                act.activation(v_t[:], PS[3], ACT.Square).then_inc(a_sq.sem, 1)
                act.wait_ge(a_ss.sem, a_ss.at(h))
                act.activation(p_1[:], PS[2], ACT.Sqrt, bias=eps[:, 0:1], scale=1.0 / DA_V).then_inc(a_std.sem, 1)
                act.wait_ge(a_y.sem, a_y.at(h))
                act.activation(y_hi[:], p_0[0][:], ACT.Copy).then_inc(a_yh.sem, 1)

            def da_exp(h, i):
                n = (i + 1) * P
                for c in range(2):
                    act.wait_ge(a_max.sem, a_max.at(h, 2 * i + c))
                    dst = p_0[i % 2] if c == 0 else p_1
                    act.activation(dst[:, 0:n], PS[c][:, 0:n], ACT.Exp, bias=stat[:, 4 * (i % 2) + c:4 * (i % 2) + c + 1],
                                   accum_out=stat2[:, 4 * (i % 2) + c:4 * (i % 2) + c + 1]).then_inc(a_exp.sem, 1)

            gate_rows()
            act.wait_ge(g_st.sem, 16 * 5)
            da_head(0, True)
            with act.Fori(1, DA_HEADS) as h:
                da_head(h, False)

            with act.Fori(0, ML_HEADS) as h:
                act.wait_ge(out_ev.sem, out_ev.at(OUT_ML + 2 * h - 1))
                act.dma_start(decay_t[:], gate_scr[0, bass.ds(h, 1), :].to_broadcast([P, T])).then_inc(m_ld.sem, 16)
                act.dma_start(iw_b[:], gate_scr[1, bass.ds(h, 1), :].to_broadcast([P, T])).then_inc(m_ld.sem, 16)
                for n in range(3):
                    act.dma_start(ml_cols[:, n, :], gate_scr[2 + n, bass.ds(h, 1), :].rearrange("a (c s) -> s (a c)", s=CHUNK),
                                  allow_slow_non_contiguous=True).then_inc(m_ld.sem, 16)
                act.wait_ge(in_mm.sem, in_mm.at(IN_ML + 8 * h))
                act.activation(xp[:, CONV - 1:], PS[0], ACT.Copy).then_inc(m_x.sem, 1)
                act.wait_ge(m_conv.sem, m_conv.at(h, 3))
                act.activation(mt[:], mt[:], ACT.Silu).then_inc(m_silu.sem, 1)
                act.wait_ge(in_mm.sem, in_mm.at(IN_ML + 8 * h + 1))
                act.activation(xp[:, CONV - 1:], PS[1], ACT.Copy).then_inc(m_x.sem, 1)
                act.wait_ge(m_q.sem, m_q.at(h, 0))
                act.activation(mq_hi[:], mt[:], ACT.Copy).then_inc(m_qkh.sem, 1)
                act.wait_ge(m_q.sem, m_q.at(h, 1))
                act.activation(mi_hi[:], mt[:], ACT.Copy).then_inc(m_qkh.sem, 1)
                act.wait_ge(m_dt.sem, m_dt.at(h))
                act.activation(decay_t[:], decay_t[:], ACT.Exp, scale=-1.0).then_inc(m_de.sem, 1)
                act.wait_ge(m_conv.sem, m_conv.at(h, 7))
                act.activation(mt[:], mt[:], ACT.Silu).then_inc(m_silu.sem, 1)
                act.wait_ge(m_silu.sem, m_silu.at(h, 1))
                act.activation(mk_hi[:], mt[:], ACT.Copy).then_inc(m_qkh.sem, 1)
                act.wait_ge(in_mm.sem, in_mm.at(IN_ML + 8 * h + 2))
                act.activation(v_t0[:], PS[0], ACT.Copy).then_inc(m_vt.sem, 1)
                act.wait_ge(m_kw.sem, m_kw.at(h))
                act.activation(kw_hi[:].rearrange("p c k -> p (c k)"), xp[:, 0:T], ACT.Copy).then_inc(m_kwh.sem, 1)
                act.wait_ge(in_mm.sem, in_mm.at(IN_ML + 8 * h + 3))
                act.wait_ge(m_qkl.sem, m_qkl.at(h, 2))
                act.wait_ge(m_ktr.sem, m_ktr.at(h))
                act.activation(mt[:], PS[1], ACT.Copy).then_inc(m_vt.sem, 1)
                for e in range(2):
                    act.wait_ge(m_vtr.sem, m_vtr.at(h, e))
                    act.activation(va_hi[:, :, e * P:(e + 1) * P], PS[e].rearrange("p (c v) -> p c v", v=P), ACT.Copy)\
                       .then_inc(m_vh.sem, 1)
                act.wait_ge(m_am.sem, m_am.at(h))
                act.activation(am_hi[:], decay_t[:], ACT.Copy).then_inc(m_ah.sem, 1)
                for c in range(NC - 1):
                    act.wait_ge(m_c.sem, m_c.at(h, c))
                    act.wait_ge(m_num.sem, m_num.at(h, c))
                    act.activation(c_hi[:], c_32[:], ACT.Copy).then_inc(m_ch.sem, 1)
                act.wait_ge(in_mm.sem, in_mm.at(IN_ML + 8 * h + 4))
                act.activation(xp[:, 0:T], PS[0], ACT.Copy).then_inc(m_ot.sem, 1)
                act.wait_ge(in_mm.sem, in_mm.at(IN_ML + 8 * h + 5))
                act.activation(mt[:], PS[1], ACT.Copy).then_inc(m_ot.sem, 1)
                for e in range(2):
                    act.wait_ge(m_otr.sem, m_otr.at(h, e))
                    act.activation(ml_so[:, :, e * P:(e + 1) * P], PS[2 + e].rearrange("p (c v) -> p c v", v=P), ACT.Sigmoid)\
                       .then_inc(m_so.sem, 1)
                act.wait_ge(m_g.sem, m_g.at(h))
                for c in range(NC):
                    act.activation(ml_so[:, c, :], hm[:, c, :], ACT.Square, accum_out=stat2[:, c:c + 1]).then_inc(m_ss.sem, 1)
                act.wait_ge(m_ss.sem, m_ss.at(h))
                act.activation(stat2[:, 8:16], stat2[:, 0:8], ACT.Sqrt, bias=eps[:, 0:1], scale=1.0 / ML_V).then_inc(m_std.sem, 1)
                for e in range(2):
                    act.wait_ge(in_mm.sem, in_mm.at(IN_ML + 8 * h + 6 + e))
                    act.activation(ml_z[e][:], PS[e], ACT.Silu).then_inc(m_z.sem, 1)
                for e in range(2):
                    act.wait_ge(m_y.sem, m_y.at(h, 2 + e))
                    act.activation(my_hi[e][:], (xp[:, 0:T], mt[:])[e], ACT.Copy).then_inc(m_yh.sem, 1)

            act.wait_ge(m_yl.sem, m_yl.at(ML_HEADS - 1))
            act.wait_ge(c_mm.sem, c_mm.at(C_SG - 1))
            act.dma_start(resid[:], res_scr).then_inc(refill.sem, 16)
            square(3, acc, out_ev.sem, lambda k: out_ev.at(OUT_SG - 1, k))
            square(4, resid, post_h.sem, lambda k: post_h.at(0, k))
            act.dma_start(res_scr, resid[:]).then_inc(spill.sem, 16)
            split_high(2)
            act.wait_ge(s_lo.sem, s_lo.at(2))
            act.wait_ge(spill.sem, spill.at(1))
            act.dma_start(wsp[:], w_spatial).then_inc(sp_ld.sem, 16)
            act.dma_start(bsp[:].rearrange("p g t -> p (g t)"), b_spatial.to_broadcast([P, SG_GROUPS * P])).then_inc(sp_ld.sem, 16)

            with act.Fori(0, SG_TILES // 2) as j:
                for s in range(2):
                    act.wait_ge(in_mm.sem, in_mm.at(IN_SV + 2 * j + s))
                    act.wait_ge(v_tr.sem, v_tr.at(2 * j + (s - 2)))
                    act.activation(g_t[s][:], PS[s], ACT.Gelu_apprx_tanh).then_inc(v_g.sem, 1)
                for s in range(2):
                    act.wait_ge(v_tok.sem, v_tok.at(2 * j + s))
                    act.dma_start(gv_scr[bass.ds(2 * j + s, 1)].rearrange("a p t -> p (a t)"),
                                  g_tok[s][:].rearrange("p c d -> p (c d)")).then_inc(v_st[s].sem, 16)
                    act.wait_ge(v_sq.sem, v_sq.at(2 * j + (s - 1)))
                    for c in range(NC):
                        act.activation(wr[:, c, :], g_tok[s][:, c, :], ACT.Square,
                                       accum_out=ssq[:, c, bass.ds(2 * j + s, 1)]).then_inc(v_sq.sem, 1)
            act.wait_ge(v_r.sem, 1)
            act.activation(stat2[:, 0:8], stat[:, 0:8], ACT.Sqrt, bias=eps[:, 0:1], scale=1.0 / (SG_TILES * P)).then_inc(v_r.sem, 1)

            def sg_weights(g):
                act.wait_ge(w_s.sem, w_s.at(g))
                act.wait_ge(in_mm.sem, in_mm.at(IN_SG + 4 * g - 1))
                act.activation(wr_hi[:], wr[:], ACT.Copy).then_inc(w_h.sem, 1)

            def sg_tile(d, e):
                act.wait_ge(in_mm.sem, in_mm.at(IN_SG + 2 * d))
                act.wait_ge(e_y.sem, e_y.at(d - 1))
                act.activation(sg_u[:], PS[0], ACT.Gelu_apprx_tanh).then_inc(e_u.sem, 1)
                act.wait_ge(in_mm.sem, in_mm.at(IN_SG + 2 * d + 1))
                act.activation(sg_z[:], PS[1], ACT.Silu).then_inc(e_z.sem, 1)
                act.wait_ge(e_y.sem, e_y.at(d))
                act.activation(sy_hi[e][:], sg_v[:], ACT.Copy).then_inc(e_yh.sem, 1)

            with act.Fori(0, SG_GROUPS) as g:
                sg_weights(g)
                for e in range(2):
                    sg_tile(2 * g + e, e)

            act.wait_ge(e_yl.sem, e_yl.at(SG_TILES - 1))
            act.wait_ge(c_mm.sem, c_mm.at(C_SG + 2 * SG_TILES - 1))
            act.dma_start(resid[:], res_scr).then_inc(refill.sem, 16)
            square(5, acc, out_ev.sem, lambda k: out_ev.at(OUT_SG + SG_TILES - 1, k))

        @block.vector
        def _(dve):
            for b in (out_ev, f_mul, f_lo, v_tok, w_s, w_l, e_v, e_y, e_yl):
                dve.sem_inc(b.sem, b.prime * b.per)

            dve.wait_ge(par_ld.sem, 16)
            dve.tensor_tensor(lam_prod[:], par[:, COL["lam_q"]:COL["lam_q"] + 2], par[:, COL["lam_k"]:COL["lam_k"] + 2],
                              ALU.mult).then_inc(lam_done.sem, 1)
            step = [0]

            def chained(ins):
                step[0] += 1
                ins.then_inc(px_step.sem, 1)
                dve.wait_ge(px_step.sem, step[0])

            SH1, SC1, G1, SH2, SC2, G2 = (slice(n * KT, (n + 1) * KT) for n in range(N_MOD))
            dve.wait_ge(mod_mm.sem, mod_mm.at(3))
            nb = COL["mod_b"]
            dve.tensor_tensor(mod[:, 0:24], PS[2][:, 0:24], par[:, nb:nb + 24], ALU.add).then_inc(mod_col.sem, 1)
            dve.wait_ge(mod_col.sem, 1)
            dve.tensor_scalar(sc1p[:], mod[:, SC1], 1.0, None, ALU.add).then_inc(px_step.sem, 1)
            step[0] += 1
            chained(dve.tensor_tensor(pool_gain[:], mod[:, G1], par[:, COL["pool_scale"]:COL["pool_scale"] + KT], ALU.mult))

            dve.wait_ge(x_ld.sem, 16)
            dve.wait_ge(small_ld.sem, 32)
            dve.wait_ge(const.sem, 12)
            for k in range(KT):
                levels = k // 2 + 1
                w = 2 ** levels
                ins = dve.tensor_scalar(hx[:, PAD:PAD + T], resid[:, k, :], sc1p[:, k:k + 1], mod[:, k:k + 1], ALU.mult, ALU.add)
                ins.then_inc(px.sem, 1)
                dve.wait_ge(px.sem, k + 1)
                src, lo, hi = hx, 0, TP
                for n in range(levels):
                    back, ahead = (1, 0) if n == 0 else (2 ** (n - 1), 2 ** (n - 1))
                    lo, hi = lo + back, hi - ahead
                    chained(dve.tensor_tensor(tree[n][:, lo:hi], src[:, lo - back:hi - back], src[:, lo + ahead:hi + ahead], ALU.add))
                    src = tree[n]
                left, right = w // 2, w // 2 - 1
                e0 = w - 2
                chained(dve.tensor_tensor(src[:, PAD:PAD + left], src[:, PAD:PAD + left], edge[:, e0:e0 + left], ALU.mult))
                if right:
                    chained(dve.tensor_tensor(src[:, PAD + T - right:PAD + T], src[:, PAD + T - right:PAD + T],
                                              edge[:, e0 + left:e0 + left + right], ALU.mult))
                dve.scalar_tensor_tensor(acc[:, k, :], src[:, PAD:PAD + T], 1.0 / w, hx[:, PAD:PAD + T], ALU.mult, ALU.subtract)\
                   .then_inc(p_done.sem, 1)
                dve.wait_ge(p_done.sem, k + 1)
            dve.wait_ge(mod_mm.sem, mod_mm.at(7))
            dve.tensor_tensor(mod[:, 24:48], PS[3][:, 0:24], par[:, nb + 24:nb + 48], ALU.add).then_inc(mod_col.sem, 1)
            dve.wait_ge(mod_col.sem, 2)
            ln_b0 = par[:, COL["ln_b0"]:COL["ln_b0"] + KT]
            chained(dve.tensor_scalar(sc2p[:], mod[:, SC2], 1.0, None, ALU.add))
            chained(dve.tensor_scalar(res_b0[:], ln_b0, ALPHA, None, ALU.mult))
            chained(dve.tensor_tensor(ffn_b0[:], ln_b0, sc2p[:], ALU.mult))
            chained(dve.tensor_tensor(ffn_b0[:], ffn_b0[:], mod[:, SH2], ALU.add))
            chained(dve.tensor_scalar(da_gain[:], par_col("da_g"), 1.0 - LAM_INIT, None, ALU.mult))
            dve.wait_ge(lam_x.sem, 1)
            chained(dve.scalar_tensor_tensor(neg_lam[:], lam_exp[:, 1:2], LAM_INIT, lam_exp[:, 0:1], ALU.subtract, ALU.subtract))
            for j in range(KT):
                dve.wait_ge(pool_mm.sem, j + 1)
                dve.wait_ge(x_scaled.sem, j + 1)
                dve.scalar_tensor_tensor(resid[:, j, :], PS[j % 2], pool_gain[:, j:j + 1], resid[:, j, :], ALU.mult, ALU.add)\
                   .then_inc(z_done.sem, 1)

            def center(norm, ready, value):
                dve.wait_ge(n_mean.sem, n_mean.at(norm))
                dve.wait_ge(ready, value)
                for k in range(KT):
                    dve.tensor_tensor(resid[:, k, :], resid[:, k, :], mean[:], ALU.subtract).then_inc(n_cent.sem, 1)

            def reciprocal(norm):
                dve.wait_ge(n_std.sem, n_std.at(norm))
                dve.reciprocal(rstd[:], std[:]).then_inc(n_rstd.sem, 1)
                dve.wait_ge(n_rstd.sem, n_rstd.at(norm))

            def split_low(use, k):
                dve.wait_ge(s_hi.sem, s_hi.at(use, k))
                dve.tensor_tensor(h_lo[:, k, :], tmp[k % 2][:], h_hi[:, k, :].bitcast(F32), ALU.subtract).then_inc(s_lo.sem, 1)

            center(0, z_done.sem, KT)
            reciprocal(0)
            for k in range(KT):
                dve.scalar_tensor_tensor(resid[:, k, :], resid[:, k, :], par_col("ln_g0", k), rstd[:], ALU.mult, ALU.mult)\
                   .then_inc(n_out.sem, 1)
                dve.wait_ge(n_out.sem, n_out.at(0, k))
                dve.tensor_scalar(tmp[k % 2][:], resid[:, k, :], sc2p[:, k:k + 1], ffn_b0[:, k:k + 1], ALU.mult, ALU.add)\
                   .then_inc(s_tmp.sem, 1)
                if k >= 1:
                    split_low(0, k - 1)
            split_low(0, KT - 1)

            def add_out(n, o, gain=None, to=acc):
                dve.wait_ge(out_ev.sem, out_ev.at(o - 1))
                for d in range(KT):
                    if d < KT - 1:
                        dve.wait_ge(out_mm.sem, out_mm.at(o, d))
                    else:
                        dve.wait_ge(c_mm.sem, c_mm.at(n))
                    if gain is not None:
                        ins = dve.scalar_tensor_tensor(to[:, d, :], PS[2 + d % 2], gain[:, d:d + 1], to[:, d, :], ALU.mult, ALU.add)
                    else:
                        ins = dve.tensor_tensor(to[:, d, :], PS[2 + d % 2], to[:, d, :], ALU.add)
                    ins.then_inc(out_ev.sem, 1)

            def ffn(f, b):
                dve.wait_ge(in_mm.sem, in_mm.at(2 * f + 1))
                dve.wait_ge(f_silu.sem, f_silu.at(f))
                dve.wait_ge(f_lo.sem, f_lo.at(f - 1))
                dve.tensor_tensor(ffn_p[:], PS[1], ffn_g[:], ALU.mult).then_inc(f_mul.sem, 1)
                dve.wait_ge(f_hi.sem, f_hi.at(f))
                dve.tensor_tensor(ffn_lo[b][:], ffn_p[:], ffn_hi[b][:].bitcast(F32), ALU.subtract).then_inc(f_lo.sem, 1)

            g2 = mod[:, G2]
            dve.wait_ge(n_res.sem, n_res.at(0))
            ffn(0, 0)
            with dve.Fori(0, F_TILES // 2 - 1) as j:
                for b in range(2):
                    ffn(2 * j + (1 + b), 1 - b)
                    add_out(2 * j + b, 2 * j + b, g2, resid)
            ffn(F_TILES - 1, 1)
            for f in (F_TILES - 2, F_TILES - 1):
                add_out(f, f, g2, resid)

            center(1, out_ev.sem, out_ev.at(F_TILES - 1))
            reciprocal(1)
            for k in range(KT):
                dve.scalar_tensor_tensor(resid[:, k, :], resid[:, k, :], par_col("ln_g1", k), rstd[:], ALU.mult, ALU.mult)\
                   .then_inc(n_gain.sem, 1)
                dve.wait_ge(n_gain.sem, n_gain.at(0, k))
                dve.tensor_scalar(resid[:, k, :], resid[:, k, :], par_col("ln_b1", k), None, ALU.add).then_inc(n_out.sem, 1)

            def layer_input(norm, use, g_name):
                reciprocal(norm)
                for k in range(KT):
                    if k >= 2:
                        dve.wait_ge(s_lo.sem, s_lo.at(use, k - 2))
                    dve.scalar_tensor_tensor(tmp[k % 2][:], resid[:, k, :], par_col(g_name, k), rstd[:], ALU.mult, ALU.mult)\
                       .then_inc(s_tmp.sem, 1)
                    if k >= 1:
                        split_low(use, k - 1)
                split_low(use, KT - 1)

            layer_input(2, 1, "l0_pre_g")

            count = [0]

            def gate_step(ins):
                count[0] += 1
                ins.then_inc(g_dve.sem, 1)
                dve.wait_ge(g_dve.sem, count[0])

            dve.wait_ge(spill.sem, spill.at(0))
            dve.wait_ge(s_lo.sem, s_lo.at(1))
            gate_step(dve.memset(g_zero[:], 0.0))
            gate_step(dve.memset(g_m[:], 0.0))
            dve.wait_ge(g_act.sem, 3)
            gate_step(dve.scalar_tensor_tensor(g_lf[:], g_f[:], 0.0, g_l[:], ALU.min, ALU.subtract))
            for c in range(NC):
                gate_step(dve.tensor_tensor_scan(g_cum[:, c, :], g_lf[:, c, :], g_zero[:], 0.0, ALU.add, ALU.add))
            gate_step(dve.tensor_tensor(g_u[:], g_i[:], g_cum[:], ALU.subtract))
            for c in range(NC):
                gate_step(dve.tensor_tensor_scan(g_max[:, c, :], g_u[:, c, :], g_u[:, c, :], g_m[:, c:c + 1], ALU.max, ALU.max))
                gate_step(dve.tensor_tensor(g_m[:, c + 1:c + 2], g_cum[:, c, CHUNK - 1:CHUNK], g_max[:, c, CHUNK - 1:CHUNK], ALU.add))
            for c in range(NC):
                gate_step(dve.tensor_scalar(g_d[:, c, :], g_max[:, c, :], g_m[:, c:c + 1], None, ALU.subtract))
            gate_step(dve.tensor_tensor(g_d2[:], g_cum[:], g_max[:], ALU.add))
            for c in range(NC):
                gate_step(dve.tensor_scalar(g_d3[:, c, :], g_u[:, c, :], g_max[:, c, CHUNK - 1:CHUNK], None, ALU.subtract))
            assert count[0] == GATE_STEPS

            def da_head(h, first):
                dve.wait_ge(a_qh.sem, a_qh.at(h))
                dve.scalar_tensor_tensor(q_lo[:], PS[0], DA_QK ** -0.5, q_hi[:].bitcast(F32), ALU.mult, ALU.subtract).then_inc(a_ql.sem, 1)
                dve.wait_ge(a_kh.sem, a_kh.at(h))
                dve.tensor_tensor(k_lo[:], PS[1], k_hi[:].bitcast(F32), ALU.subtract).then_inc(a_kl.sem, 1)
                if not first:
                    add_out(C_DA + h - 1, OUT_DA + h - 1)
                dve.wait_ge(a_vh.sem, a_vh.at(h))
                dve.tensor_tensor(v_lo[:].rearrange("p b v -> p (b v)"), PS[2], v_hi[:].rearrange("p b v -> p (b v)").bitcast(F32),
                                  ALU.subtract).then_inc(a_vl.sem, 1)
                da_max(h, 0)
                for i in range(KT):
                    n = (i + 1) * P
                    st = 4 * (i % 2)
                    dve.wait_ge(a_exp.sem, a_exp.at(h, 2 * i + 1))
                    dve.reciprocal(stat2[:, st + 2:st + 4], stat2[:, st:st + 2]).then_inc(a_rec.sem, 1)
                    dve.wait_ge(a_rec.sem, a_rec.at(h, i))
                    dve.tensor_scalar(stat[:, st + 2:st + 3], stat2[:, st + 3:st + 4], neg_lam[:, 0:1], None, ALU.mult).then_inc(a_nr.sem, 1)
                    dve.tensor_scalar(p_0[i % 2][:, 0:n], p_0[i % 2][:, 0:n], stat2[:, st + 2:st + 3], None, ALU.mult).then_inc(a_p0.sem, 1)
                    dve.wait_ge(a_nr.sem, a_nr.at(h, i))
                    dve.wait_ge(a_p0.sem, a_p0.at(h, i))
                    dve.scalar_tensor_tensor(p_0[i % 2][:, 0:n], p_1[:, 0:n], stat[:, st + 2:st + 3], p_0[i % 2][:, 0:n],
                                             ALU.mult, ALU.add).then_inc(a_mix.sem, 1)
                    if i + 1 < KT:
                        da_max(h, i + 1)
                    dve.wait_ge(a_hi_d.sem, a_hi_d.at(h, i))
                    dve.tensor_tensor(a_lo[i % 2][:, 0:i + 1, :].rearrange("p b q -> p (b q)"), PS[2][:, 0:n],
                                      a_hi[i % 2][:, 0:i + 1, :].rearrange("p b q -> p (b q)").bitcast(F32), ALU.subtract)\
                       .then_inc(a_lo_d.sem, 1)
                dve.wait_ge(a_std.sem, a_std.at(h))
                dve.reciprocal(p_1[:], p_1[:]).then_inc(a_r.sem, 1)
                dve.wait_ge(a_r.sem, a_r.at(h))
                dve.scalar_tensor_tensor(p_0[0][:], PS[3], da_gain[:, 0:1], p_1[:], ALU.mult, ALU.mult).then_inc(a_on.sem, 1)
                dve.wait_ge(a_on.sem, a_on.at(h))
                dve.tensor_tensor(p_0[0][:], p_0[0][:], da_z[:], ALU.mult).then_inc(a_y.sem, 1)
                dve.wait_ge(a_yh.sem, a_yh.at(h))
                dve.tensor_tensor(y_lo[:], p_0[0][:], y_hi[:].bitcast(F32), ALU.subtract).then_inc(a_yl.sem, 1)

            def da_max(h, i):
                n = (i + 1) * P
                for c in range(2):
                    dve.wait_ge(a_score.sem, a_score.at(h, 2 * i + c))
                    dve.tensor_reduce(stat[:, 4 * (i % 2) + c:4 * (i % 2) + c + 1], PS[c][:, 0:n], AX_X, ALU.max, negate=True)\
                       .then_inc(a_max.sem, 1)

            dve.wait_ge(g_st.sem, 16 * 5)
            dve.wait_ge(acc_zero.sem, 1)
            da_head(0, True)
            with dve.Fori(1, DA_HEADS) as h:
                da_head(h, False)
            add_out(C_DA + DA_HEADS - 1, OUT_DA + DA_HEADS - 1)

            def conv(h, which, event):
                col = lambda j: par[:, bass.ds(h + (COL["conv_w"] + 8 * j + 4 * which), 1)]
                dve.tensor_scalar(mt[:], xp[:, 0:T], col(0), par[:, bass.ds(h + (COL["conv_b"] + 4 * which), 1)], ALU.mult, ALU.add)\
                   .then_inc(m_conv.sem, 1)
                for j in range(1, CONV):
                    dve.wait_ge(m_conv.sem, m_conv.at(h, event + j - 1))
                    dve.scalar_tensor_tensor(mt[:], xp[:, j:j + T], col(j), mt[:], ALU.mult, ALU.add).then_inc(m_conv.sem, 1)

            with dve.Fori(0, ML_HEADS) as h:
                dve.wait_ge(out_ev.sem, out_ev.at(OUT_ML + 2 * h - 1))
                dve.memset(xp[:, 0:CONV - 1], 0.0).then_inc(m_vl.sem, 1)
                dve.memset(va_hi[:, :, ML_V:ML_V + 1].bitcast(F32), 1.0).then_inc(m_vl.sem, 1)
                dve.memset(va_hi[:, :, ML_V + 1:VA].bitcast(F32), 0.0).then_inc(m_vl.sem, 1)
                dve.memset(va_lo[:, :, ML_V:VA].bitcast(F32), 0.0).then_inc(m_vl.sem, 1)
                dve.wait_ge(m_vl.sem, m_vl.at(h, 0))
                dve.wait_ge(m_x.sem, m_x.at(h, 0))
                conv(h, 0, 0)
                dve.wait_ge(m_silu.sem, m_silu.at(h, 0))
                dve.tensor_scalar(mt[:], mt[:], ML_QK ** -0.5, None, ALU.mult).then_inc(m_q.sem, 1)
                dve.wait_ge(m_qkh.sem, m_qkh.at(h, 0))
                dve.tensor_tensor(mq_lo[:], mt[:], mq_hi[:].bitcast(F32), ALU.subtract).then_inc(m_qkl.sem, 1)
                dve.wait_ge(m_ld.sem, m_ld.at(h))
                dve.wait_ge(m_qkl.sem, m_qkl.at(h, 0))
                dve.tensor_tensor(mt[:], mt[:], iw_b[:], ALU.mult).then_inc(m_q.sem, 1)
                for c in range(NC):
                    cols = slice(c * CHUNK, (c + 1) * CHUNK)
                    dve.tensor_scalar(decay_t[:, cols], decay_t[:, cols], ml_cols[:, 0, c:c + 1], 0.0, ALU.subtract, ALU.max)\
                       .then_inc(m_dt.sem, 1)
                dve.tensor_copy(stat[:, 8:16], iw_b[:, CHUNK - 1:T:CHUNK]).then_inc(m_den.sem, 1)
                dve.wait_ge(m_qkh.sem, m_qkh.at(h, 1))
                dve.tensor_tensor(mi_lo[:], mt[:], mi_hi[:].bitcast(F32), ALU.subtract).then_inc(m_qkl.sem, 1)
                dve.wait_ge(m_x.sem, m_x.at(h, 1))
                dve.wait_ge(m_qkl.sem, m_qkl.at(h, 1))
                conv(h, 1, 4)
                dve.wait_ge(m_qkh.sem, m_qkh.at(h, 2))
                dve.tensor_tensor(mk_lo[:], mt[:], mk_hi[:].bitcast(F32), ALU.subtract).then_inc(m_qkl.sem, 1)
                dve.wait_ge(m_ktr.sem, m_ktr.at(h))
                for c in range(NC):
                    cols = slice(c * CHUNK, (c + 1) * CHUNK)
                    dve.tensor_scalar(xp[:, cols], PS[2][:, cols], ml_cols[:, 1, c:c + 1], None, ALU.mult).then_inc(m_kw.sem, 1)
                dve.wait_ge(m_kwh.sem, m_kwh.at(h))
                dve.tensor_tensor(kw_lo[:].rearrange("p c k -> p (c k)"), xp[:, 0:T],
                                  kw_hi[:].rearrange("p c k -> p (c k)").bitcast(F32), ALU.subtract).then_inc(m_kwl.sem, 1)
                dve.wait_ge(m_s.sem, m_s.at(h))
                dve.wait_ge(m_mask.sem, m_mask.at(h))
                dve.tensor_tensor(decay_t[:], PS[3], decay_t[:], ALU.mult).then_inc(m_am.sem, 1)
                for e in range(2):
                    dve.wait_ge(m_vh.sem, m_vh.at(h, e))
                    dve.tensor_tensor(va_lo[:, :, e * P:(e + 1) * P], PS[e].rearrange("p (c v) -> p c v", v=P),
                                      va_hi[:, :, e * P:(e + 1) * P].bitcast(F32), ALU.subtract).then_inc(m_vl.sem, 1)
                dve.wait_ge(m_ah.sem, m_ah.at(h))
                dve.tensor_tensor(am_lo[:], decay_t[:], am_hi[:].bitcast(F32), ALU.subtract).then_inc(m_al.sem, 1)
                for c in range(NC):
                    if c < NC - 1:
                        part = PS[3][:, (c % 2) * HALF:(c % 2) * HALF + VA]
                        dve.wait_ge(m_p.sem, m_p.at(h, c))
                        if c == 0:
                            dve.tensor_copy(c_32[:], part).then_inc(m_c.sem, 1)
                        else:
                            dve.wait_ge(m_cl.sem, m_cl.at(h, c - 1))
                            dve.scalar_tensor_tensor(c_32[:], c_32[:], stat[:, 8 + c:9 + c], part, ALU.mult, ALU.add).then_inc(m_c.sem, 1)
                        dve.wait_ge(m_ch.sem, m_ch.at(h, c))
                        dve.tensor_tensor(c_lo[:], c_32[:], c_hi[:].bitcast(F32), ALU.subtract).then_inc(m_cl.sem, 1)
                    num = PS[2][:, (c % 2) * HALF:(c % 2) * HALF + VA]
                    dve.wait_ge(m_num.sem, m_num.at(h, c))
                    den = num[:, ML_V:ML_V + 1]
                    dve.tensor_scalar(stat[:, 2:3], den, -1.0, ml_cols[:, 2, c:c + 1], ALU.mult, ALU.max).then_inc(m_den.sem, 1)
                    dve.wait_ge(m_den.sem, m_den.at(h, 1 + 2 * c))
                    dve.tensor_tensor(stat[:, 0:1], den, stat[:, 2:3], ALU.max).then_inc(m_den.sem, 1)
                    dve.wait_ge(m_den.sem, m_den.at(h, 2 + 2 * c))
                    dve.reciprocal(stat[:, 1:2], stat[:, 0:1]).then_inc(m_rd.sem, 1)
                    dve.wait_ge(m_rd.sem, m_rd.at(h, c))
                    dve.tensor_scalar(hm[:, c, :], num[:, 0:ML_V], stat[:, 1:2], None, ALU.mult).then_inc(m_hm.sem, 1)
                dve.wait_ge(m_so.sem, m_so.at(h))
                dve.wait_ge(m_hm.sem, m_hm.at(h))
                dve.tensor_tensor(hm[:], hm[:], ml_so[:], ALU.mult).then_inc(m_g.sem, 1)
                dve.wait_ge(m_std.sem, m_std.at(h))
                dve.reciprocal(stat[:, 0:8], stat2[:, 8:16]).then_inc(m_r.sem, 1)
                dve.wait_ge(m_r.sem, m_r.at(h))
                for c in range(NC):
                    dve.tensor_scalar(hm[:, c, :], hm[:, c, :], stat[:, c:c + 1], None, ALU.mult).then_inc(m_n.sem, 1)
                for e in range(2):
                    dst = (xp[:, 0:T], mt[:])[e]
                    dve.wait_ge(m_ntr.sem, m_ntr.at(h, e))
                    dve.tensor_scalar(dst, PS[2 + e], par_col("ml_g", e), None, ALU.mult).then_inc(m_y.sem, 1)
                for e in range(2):
                    dst = (xp[:, 0:T], mt[:])[e]
                    dve.wait_ge(m_y.sem, m_y.at(h, e))
                    dve.wait_ge(m_z.sem, m_z.at(h, e))
                    dve.tensor_tensor(dst, dst, ml_z[e][:], ALU.mult).then_inc(m_y.sem, 1)
                for e in range(2):
                    dve.wait_ge(m_yh.sem, m_yh.at(h, e))
                    dve.tensor_tensor(my_lo[e][:], (xp[:, 0:T], mt[:])[e], my_hi[e][:].bitcast(F32), ALU.subtract).then_inc(m_yl.sem, 1)
                for e in range(2):
                    add_out(C_ML + 2 * h + e, OUT_ML + 2 * h + e)

            def layer_output(norm, use, g_name):
                reciprocal(norm)
                dve.wait_ge(refill.sem, refill.at(use))
                for k in range(KT):
                    dve.scalar_tensor_tensor(acc[:, k, :], acc[:, k, :], par_col(g_name, k), rstd[:], ALU.mult, ALU.mult)\
                       .then_inc(post_t.sem, 1)
                    if k >= 1:
                        residual(use, k - 1)
                residual(use, KT - 1)

            def residual(use, k):
                dve.wait_ge(post_t.sem, post_t.at(use, k))
                dve.tensor_tensor(resid[:, k, :], resid[:, k, :], acc[:, k, :], ALU.add).then_inc(post_h.sem, 1)

            layer_output(3, 0, "l0_post_g")
            layer_input(4, 2, "l1_pre_g")

            dve.wait_ge(sp_ld.sem, sp_ld.at(0))
            dve.wait_ge(acc_zero.sem, 2)
            with dve.Fori(0, SG_TILES // 2) as j:
                for s in range(2):
                    dve.wait_ge(v_tr.sem, v_tr.at(2 * j + s))
                    dve.wait_ge(v_st[s].sem, v_st[s].at(j - 1))
                    dve.wait_ge(v_sq.sem, v_sq.at(2 * j + (s - 2)))
                    dve.tensor_copy(g_tok[s][:].rearrange("p c d -> p (c d)"), PS[2 + s]).then_inc(v_tok.sem, 1)
            dve.wait_ge(v_sq.sem, v_sq.at(SG_TILES - 1))
            dve.tensor_reduce(stat[:, 0:8], ssq[:], AX_X, ALU.add).then_inc(v_r.sem, 1)
            dve.wait_ge(v_r.sem, 2)
            dve.reciprocal(stat[:, 8:16], stat2[:, 0:8]).then_inc(v_r.sem, 1)
            dve.wait_ge(v_r.sem, 3)
            dve.wait_ge(const.sem, 13)

            def sg_weights(g):
                dve.wait_ge(w_l.sem, w_l.at(g - 1))
                for c in range(NC):
                    dve.tensor_scalar(wr[:, c, :], wsp[:, bass.ds(g, 1), :].rearrange("p a t -> p (a t)"), stat[:, 8 + c:9 + c],
                                      None, ALU.mult).then_inc(w_s.sem, 1)
                dve.wait_ge(w_h.sem, w_h.at(g))
                dve.tensor_tensor(wr_lo[:], wr[:], wr_hi[:].bitcast(F32), ALU.subtract).then_inc(w_l.sem, 1)

            def sg_tile(d, g, n):
                dve.wait_ge(c_mm.sem, c_mm.at(n))
                dve.wait_ge(e_yl.sem, e_yl.at(d - 1))
                dve.scalar_tensor_tensor(sg_v[:].rearrange("p (c t) -> p c t", t=P), PS[2].rearrange("p (c t) -> p c t", t=P),
                                         par[:, bass.ds(d + COL["sg_g"], 1)],
                                         bsp[:, bass.ds(g, 1), :].to_broadcast([P, NC, P]), ALU.mult, ALU.add).then_inc(e_v.sem, 1)
                dve.wait_ge(e_v.sem, e_v.at(d))
                dve.wait_ge(e_u.sem, e_u.at(d))
                dve.tensor_tensor(sg_v[:], sg_v[:], sg_u[:], ALU.mult).then_inc(e_y.sem, 1)
                dve.wait_ge(e_y.sem, e_y.at(d, 0))
                dve.wait_ge(e_z.sem, e_z.at(d))
                dve.tensor_tensor(sg_v[:], sg_v[:], sg_z[:], ALU.mult).then_inc(e_y.sem, 1)

            def sg_low(d, e):
                dve.wait_ge(e_yh.sem, e_yh.at(d))
                dve.tensor_tensor(sy_lo[e][:], sg_v[:], sy_hi[e][:].bitcast(F32), ALU.subtract).then_inc(e_yl.sem, 1)

            sg_weights(0)
            sg_tile(0, 0, C_SG)
            sg_low(0, 0)
            sg_tile(1, 0, C_SG + 1)
            sg_low(1, 1)
            add_out(C_SG + 2, OUT_SG)
            with dve.Fori(1, SG_GROUPS) as g:
                sg_weights(g)
                for e in range(2):
                    sg_tile(2 * g + e, g, C_SG + 4 * g + (2 * e - 1))
                    sg_low(2 * g + e, e)
                    add_out(C_SG + 4 * g + 2 * e, OUT_SG + 2 * g + (e - 1))
            add_out(C_SG + 2 * SG_TILES - 1, OUT_SG + SG_TILES - 1)
            layer_output(5, 1, "l1_post_g")


def columns(v):
    return np.asarray(v).reshape(-1, P).T


def in_slab(w, cols):
    return np.asarray(w)[:, cols:cols + P].reshape(KT, P, P).transpose(1, 0, 2).reshape(P, T)


def kernel(**inputs):
    import concourse.bacc as bacc
    from concourse.bass_utils import run_bass_kernel_spmd

    a = {k: np.asarray(v) for k, v in inputs.items()}
    f32 = np.float32
    par = np.zeros((P, N_PAR), f32)

    def put(name, cols):
        par[:cols.shape[0], COL[name]:COL[name] + cols.shape[1]] = cols

    put("c", columns(a["c"][0]))
    put("mod_b", columns(a["mod_b"][0]))
    for n in range(2):
        put(f"ln_g{n}", columns(a["ln_g"][0, n]))
        put(f"ln_b{n}", columns(a["ln_b"][0, n]))
    put("pool_scale", columns(a["pool_scale"][0]))
    put("l0_pre_g", columns(a["l0_pre_g_2"]))
    put("l0_post_g", columns(a["l0_post_g_2"]))
    put("l1_pre_g", columns(a["l1_pre_g_2"]))
    put("l1_post_g", columns(a["l1_post_g_2"]))
    put("conv_w", columns(a["l0_conv_w_2"]))
    put("conv_b", columns(a["l0_conv_b_2"]))
    put("da_g", columns(a["l0_da_head_g_2"]))
    put("ml_g", columns(a["l0_ml_head_g_2"]))
    put("sg_g", columns(a["l1_sg_norm_g_2"]))
    par[0:ML_HEADS, COL["gate_b"]] = a["l0_b_igate_2"]
    par[32:32 + ML_HEADS, COL["gate_b"]] = a["l0_b_fgate_2"]
    put("lam_q", np.stack([a["l0_lambda_q1_2"], a["l0_lambda_q2_2"]], 1))
    put("lam_k", np.stack([a["l0_lambda_k1_2"], a["l0_lambda_k2_2"]], 1))

    edges = np.ones((P, 32), f32)
    for w in (2, 4, 8, 16):
        counts = [t + w // 2 for t in range(w // 2)] + [w - 1 - r for r in range(w // 2 - 1)]
        edges[:, w - 2:w - 2 + len(counts)] = np.array([w / n for n in counts], f32)

    ffn_in, w0, w1 = a["ffn_w_in"][0], a["l0_w_in_2"], a["l1_w_in_2"]
    hidden = F_TILES * P
    w_in = np.empty((N_IN, P, T), f32)
    for f in range(F_TILES):
        w_in[2 * f] = in_slab(ffn_in, f * P)
        w_in[2 * f + 1] = in_slab(ffn_in, hidden + f * P)
    da, qk = DA_HEADS * DA_V, ML_HEADS * ML_QK
    ml_qk = 4 * da
    ml_v = ml_qk + 2 * qk
    ml_i = ml_v + ML_HEADS * ML_V
    ml_o = ml_i + 2 * ML_HEADS
    ml_z = ml_o + ML_HEADS * ML_V
    for h in range(DA_HEADS):
        for s in range(4):
            w_in[IN_DA + 4 * h + s] = in_slab(w0, s * da + h * P)
    for h in range(ML_HEADS):
        places = [ml_qk + h * ML_QK, ml_qk + qk + h * ML_QK]
        places += [first + h * ML_V + e * P for first in (ml_v, ml_o, ml_z) for e in range(2)]
        for s, cols in enumerate(places):
            w_in[IN_ML + 8 * h + s] = in_slab(w0, cols)
    width = SG_TILES * P
    for d in range(SG_TILES):
        w_in[IN_SV + d] = in_slab(w1, width + d * P)
        w_in[IN_SG + 2 * d] = in_slab(w1, d * P)
        w_in[IN_SG + 2 * d + 1] = in_slab(w1, 2 * width + d * P)
    w_c = np.zeros((N_C_DRAM, P, T), f32)
    w_c[0:F_TILES] = a["ffn_w_out"][0].reshape(F_TILES, P, D)
    gates = w_c[C_GATES].reshape(P, KT, P)
    gates[:, :, 0:ML_HEADS] = w0[:, ml_i:ml_i + ML_HEADS].reshape(KT, P, ML_HEADS).transpose(1, 0, 2)
    gates[:, :, 32:32 + ML_HEADS] = w0[:, ml_i + ML_HEADS:ml_o].reshape(KT, P, ML_HEADS).transpose(1, 0, 2)
    w_c[C_DA:C_SG] = a["l0_w_out_2"].reshape(-1, P, D)
    w_c[C_SG:] = a["l1_w_out_2"].reshape(SG_TILES, P, D)

    n_loads = N_MOD * KT // 6
    mod_w = a["mod_w"][0].reshape(KT, P, n_loads, 6, P).transpose(2, 1, 3, 0, 4)
    arrays = {
        "x_t": a["x"][0].T.reshape(KT, P, T).transpose(1, 0, 2),
        "params": par,
        "mod_w": mod_w,
        "pool_w": a["pool_w"][0].reshape(4, 2, P, 256).transpose(2, 0, 1, 3),
        "w_in": w_in,
        "w_c": w_c,
        "edges": edges,
        "w_spatial": a["l1_w_spatial_2"].transpose(2, 0, 1),
        "b_spatial": a["l1_b_spatial_2"].reshape(1, SG_GROUPS * P),
    }
    arrays = {k: np.ascontiguousarray(v) for k, v in arrays.items()}
    nc = bacc.Bacc("TRN2", target_bir_lowering=False, num_devices=1)
    args = {k: nc.dram_tensor(k, v.shape, F32, kind="ExternalInput").ap() for k, v in arrays.items()}
    out = nc.dram_tensor("out", (P, KT, T), F32, kind="ExternalOutput").ap()
    build(nc, out=out, **args)
    result = run_bass_kernel_spmd(nc, [arrays], core_ids=[0]).results[0]["out"]
    return result.transpose(2, 1, 0).reshape(1, T, D)
```

```python
import math
from contextlib import ExitStack

import numpy as np

import concourse.bass as bass
from concourse import mybir

F32 = mybir.dt.float32
F32R = mybir.dt.float32r
BF16 = mybir.dt.bfloat16
ALU = mybir.AluOpType
ACT = mybir.ActivationFunctionType
AX_X = mybir.AxisListType.X

P = 128
T = 1024
HALF = 512
D = 1024
KT = D // P
F_TILES = 2816 // P
N_MOD = 6
DA_HEADS, DA_QK, DA_V = 8, 64, 128
ML_HEADS, ML_QK, ML_V, CHUNK, CONV = 4, 128, 256, 128, 4
VA = ML_V + 2
SG_TILES, SG_GROUPS = 16, 8
NC = T // CHUNK
ALPHA = 2.0 ** 0.25
EPS = 1e-6
LAM_INIT = 0.8 - 0.6 * math.exp(0.0)
MASKED = -1e30

PARAMS = [("c", 8), ("mod_b", 48), ("ln_g0", 8), ("ln_b0", 8), ("ln_g1", 8), ("ln_b1", 8),
          ("pool_scale", 8), ("l0_pre_g", 8), ("l0_post_g", 8), ("l1_pre_g", 8), ("l1_post_g", 8),
          ("conv_w", 32), ("conv_b", 8), ("da_g", 1), ("ml_g", 2), ("sg_g", 16), ("gate_b", 1),
          ("lam_q", 2), ("lam_k", 2)]
COL, N_PAR = {}, 0
for _name, _n in PARAMS:
    COL[_name] = N_PAR
    N_PAR += _n

IN_FFN_OUT = 2 * F_TILES
IN_DA = IN_FFN_OUT + 2
DA_V_SLAB, DA_Q_SLAB, DA_K_SLAB, DA_Z_SLAB = range(4)
IN_ML = IN_DA + 4 * DA_HEADS
IN_SV = IN_ML + 10 * ML_HEADS
IN_SG = IN_SV + SG_TILES
IN_SG_OUT = IN_SG + 2 * SG_TILES
N_IN = IN_SG_OUT + 2
C_GATES = F_TILES - 2
C_DA = C_GATES + 1
C_SG = C_DA + DA_HEADS
N_C_DRAM = C_SG + SG_TILES - 2
OUT_DA = F_TILES
OUT_ML = OUT_DA + DA_HEADS
OUT_SG = OUT_ML + 2 * ML_HEADS
GATE_STEPS = 5 + 5 * NC


def turn_event(i, part):
    return i if i < 4 else 4 + 2 * (i - 4) + part


class Beat:

    def __init__(self, sem, per=1, prime=0):
        self.sem, self.per, self.prime = sem, per, prime

    def at(self, turn, event=None):
        event = self.per - 1 if event is None else event
        return turn * self.per + (self.prime * self.per + event + 1)


def build(nc, x_t, params, mod_w, pool_w, w_in, w_c, edges, w_spatial, b_spatial, out):
    with ExitStack() as ctx:
        base = (nc.sbuf_base + 63) // 64 * 64
        place = [base]

        def at_offset(name, shape, dtype, offset):
            return nc.alloc_sbuf_tensor_at(name, shape, dtype, offset=offset)

        def fixed(name, shape, dtype=F32):
            size = int(np.prod(shape[1:])) * (2 if dtype == BF16 else 4)
            tile = at_offset(name, shape, dtype, place[0])
            place[0] += (size + 31) // 32 * 32
            return tile

        raw = [fixed(f"slab_raw{s}", [P, T]) for s in range(3)]
        whi = [fixed(f"slab_hi{s}", [P, KT, P], F32R) for s in range(3)]
        wlo = [fixed(f"slab_lo{s}", [P, KT, P], F32R) for s in range(3)]
        C = 2
        h_base = place[0]
        h_hi = fixed("h_hi", [P, KT, T], F32R)
        h_lo = fixed("h_lo", [P, KT, T], F32R)
        acc_base = place[0]
        acc = fixed("acc", [P, KT, T])
        ident = fixed("ident", [P, P])
        ones = fixed("ones", [P, P])
        ident_b = fixed("ident_b", [P, P], BF16)
        mask_b = fixed("mask_b", [P, P], BF16)
        causal = fixed("causal", [P, P])
        zero = fixed("zero", [P, 1])
        eps = fixed("eps", [P, 1])
        par = fixed("par", [P, N_PAR])
        mod = fixed("mod", [P, N_MOD * KT])
        silu_c = fixed("silu_c", [P, KT])
        sc1p = fixed("sc1p", [P, KT])
        sc2p = fixed("sc2p", [P, KT])
        pool_gain = fixed("pool_gain", [P, KT])
        res_b0 = fixed("res_b0", [P, KT])
        ffn_b0 = fixed("ffn_b0", [P, KT])
        lam_prod = fixed("lam_prod", [P, 2])
        lam_exp = fixed("lam_exp", [P, 2])
        neg_lam = fixed("neg_lam", [P, 1])
        da_gain = fixed("da_gain", [P, 1])
        stat = fixed("stat", [P, 16])
        stat2 = fixed("stat2", [P, 16])
        ml_cols = fixed("ml_cols", [P, 3, NC])
        ssq = fixed("ssq", [P, NC, SG_TILES])
        resid_base = place[0]
        resid = fixed("resid", [P, KT, T])
        work_base = place[0]
        top = nc.sbuf_usable_end

        def overlay(start):
            cursor = [start]

            def take(name, shape, dtype=F32, at=None):
                size = int(np.prod(shape[1:])) * (2 if dtype == BF16 else 4)
                offset = cursor[0] if at is None else at
                if at is None:
                    cursor[0] += (size + 31) // 32 * 32
                assert offset + size <= top, (name, offset + size - top)
                tile = at_offset(name, shape, dtype, offset)
                return tile, offset
            return take

        def par_col(name, k=0):
            return par[:, COL[name] + k:COL[name] + k + 1]

        MOD_BLOCKS, MOD_BUFFERS = N_MOD * D // HALF, 3
        MOD_HALF = MOD_BLOCKS // 2
        mod_big = [at_offset(f"mod_big{b}", [P, KT, HALF], F32, h_base + b * KT * HALF * 4) for b in range(MOD_BUFFERS)]
        mod_row = at_offset("mod_row", [1, MOD_HALF, HALF], F32, h_base + MOD_BUFFERS * KT * HALF * 4)
        take = overlay(work_base)
        PAD = 8
        TP = T + 2 * PAD
        xpad = [take(f"xpad{b}", [P, TP])[0] for b in range(2)]
        tree = [take(f"tree{n}", [P, TP])[0] for n in range(4)]
        pw = take("pw", [P, 4, 2, 256])[0]
        edge = take("edge", [P, 32])[0]
        take = overlay(work_base)
        sq = [take(f"sq{b}", [P, T])[0] for b in range(2)]
        mean = take("mean", [P, T])[0]
        rstd = take("rstd", [P, T])[0]
        std = take("std", [P, T])[0]
        tmp = [take(f"tmp{b}", [P, T])[0] for b in range(2)]
        take = overlay(work_base)
        ffn_g = take("ffn_g", [P, T])[0]
        ffn_p = take("ffn_p", [P, T])[0]
        ffn_hi = [take(f"ffn_hi{b}", [P, T], F32R)[0] for b in range(2)]
        ffn_lo = [take(f"ffn_lo{b}", [P, T], F32R)[0] for b in range(2)]
        take = overlay(acc_base)
        g_i, g_f, g_a, g_cum, g_u, g_max, g_d = (
            take(f"gate_{n}", [ML_HEADS, NC, CHUNK])[0] for n in ("i", "f", "log", "cum", "u", "max", "d"))
        g_zero = take("gate_zero", [ML_HEADS, CHUNK])[0]
        g_m = take("gate_m", [ML_HEADS, NC + 1])[0]
        g_lf, g_d2, g_d3 = g_a, g_f, g_i
        take = overlay(resid_base)
        q_hi, q_lo, k_hi, k_lo = (take(f"da_{n}", [P, T], F32R)[0] for n in ("qh", "ql", "kh", "kl"))
        v_t = take("da_vt", [P, T])[0]
        v_hi, v_lo = (take(f"da_{n}", [P, KT, P], F32R)[0] for n in ("vh", "vl"))
        da_z = take("da_z", [P, T])[0]
        p_0 = [take(f"da_p0{b}", [P, T])[0] for b in range(2)]
        p_1 = take("da_p1", [P, T])[0]
        a_hi, a_lo = (take(f"da_{n}", [P, KT, P], F32R)[0] for n in ("ah", "al"))
        da_o = take("da_o", [P, T])[0]
        da_sq = take("da_sq", [P, T])[0]
        y_hi, y_lo = (take(f"da_{n}", [P, T], F32R)[0] for n in ("yh", "yl"))
        take = overlay(resid_base)
        xp = take("ml_xp", [P, CONV - 1 + T])[0]
        mt = take("ml_t", [P, T])[0]
        (mq_hi, o_q), (mq_lo, _) = (take(f"ml_{n}", [P, T], F32R) for n in ("qh", "ql"))
        (mi_hi, o_i), (mi_lo, _) = (take(f"ml_{n}", [P, T], F32R) for n in ("ih", "il"))
        (mk_hi, o_k), (mk_lo, _) = (take(f"ml_{n}", [P, T], F32R) for n in ("kh", "kl"))
        (kw_hi, o_w), (kw_lo, _) = (take(f"ml_{n}", [P, NC, P], F32R) for n in ("wh", "wl"))
        (va_hi, o_v), (va_lo, _) = (take(f"ml_{n}", [P, NC, VA], F32R) for n in ("vh", "vl"))
        decay_t = take("ml_dt", [P, T])[0]
        hm, o_hm = take("ml_hm", [P, NC, ML_V])
        c_32 = take("ml_c", [P, VA])[0]
        c_hi, c_lo = (take(f"ml_{n}", [P, VA], F32R)[0] for n in ("ch", "cl"))
        iw_b = take("ml_iw", [P, T], at=o_hm)[0]
        v_t0 = take("ml_vt0", [P, T], at=o_hm + 4 * T)[0]
        am_hi, am_lo = (take(f"ml_{n}", [P, T], F32R, at=o_q + 4 * T * n_)[0] for n_, n in enumerate(("ah", "al")))
        ml_so = take("ml_so", [P, NC, ML_V], at=o_v)[0]
        ml_z = [take(f"ml_z{b}", [P, T], at=o_w + 4 * T * b)[0] for b in range(2)]
        my_hi = [take(f"ml_yh{b}", [P, T], F32R, at=(o_i, o_k)[b])[0] for b in range(2)]
        my_lo = [take(f"ml_yl{b}", [P, T], F32R, at=(o_i, o_k)[b] + 4 * T)[0] for b in range(2)]
        take = overlay(resid_base)
        wsp = take("sg_w", [P, SG_GROUPS, P])[0]
        bsp = take("sg_b", [P, SG_GROUPS, P])[0]
        g_t = [take(f"sg_g{b}", [P, T])[0] for b in range(2)]
        g_tok = [take(f"sg_t{b}", [P, NC, P])[0] for b in range(2)]
        wr = take("sg_wr", [P, NC, P])[0]
        wr_hi, wr_lo = (take(f"sg_{n}", [P, NC, P], F32R)[0] for n in ("wrh", "wrl"))
        sg_v = take("sg_v", [P, T])[0]
        sy_hi = [take(f"sg_yh{b}", [P, T], F32R)[0] for b in range(2)]
        sy_lo = [take(f"sg_yl{b}", [P, T], F32R)[0] for b in range(2)]
        sg_u, sg_z = g_t

        ps = ctx.enter_context(nc.psum_tensor("ps", [P, 4 * T], F32))
        PS = [ps[:, n * T:(n + 1) * T] for n in range(4)]

        res_scr = nc.dram_tensor("res_scr", [P, KT, T], F32, kind="Internal").ap()
        gate_scr = nc.dram_tensor("gate_scr", [5, ML_HEADS, T], F32, kind="Internal").ap()
        gv_scr = nc.dram_tensor("gv_scr", [SG_TILES, P, T], F32, kind="Internal").ap()

        def beat(name, per=1, prime=0):
            return Beat(ctx.enter_context(nc.semaphore(name)), per, prime)

        in_load = [beat(f"in_load{s}", 16) for s in range(2)]
        c_load = beat("c_load", 16)
        in_hi, c_hi_done = beat("in_hi"), beat("c_hi")
        in_split, c_split = beat("in_split", 1, 2), beat("c_split", 1, 1)
        in_mm, c_mm = beat("in_mm", 1, 2), beat("c_mm", 1, 1)
        out_mm = beat("out_mm", 2 * KT - 1)
        out_ev = beat("out_ev", 2 * KT, 1)

        par_ld, small_ld = beat("par_ld", 16), beat("small_ld", 32)
        x_ld = [beat(f"x_ld{n}", 16) for n in range(2)]
        mod_ld = [beat(f"mod_ld{b}", 16) for b in range(MOD_BUFFERS)]
        const = beat("const")
        siluc = beat("siluc")
        mod_mm, mod_out, mod_turn, mod_col = beat("mod_mm"), beat("mod_out"), beat("mod_turn"), beat("mod_col")
        sc1_done = beat("sc1_done")
        lam_mm, lam_x, lam_done = beat("lam_mm"), beat("lam_x"), beat("lam_done")
        px, p_sum, p_hx, px_step, p_done = beat("px"), beat("p_sum"), beat("p_hx"), beat("px_step"), beat("p_done")
        x_scaled, pool_mm, z_done = beat("x_scaled"), beat("pool_mm"), beat("z_done")
        n_mean_mm, n_mean, n_cent = beat("n_mean_mm"), beat("n_mean"), beat("n_cent", KT)
        n_sq, n_ssum, n_std, n_rstd = beat("n_sq", KT), beat("n_ssum", KT), beat("n_std"), beat("n_rstd")
        n_out = beat("n_out", KT)
        s_tmp, s_hi, s_lo = beat("s_tmp", KT), beat("s_hi", KT), beat("s_lo", KT)
        n_res, n_gain = beat("n_res", KT), beat("n_gain", KT)
        spill, refill, acc_zero = beat("spill", 16), beat("refill", 16), beat("acc_zero")
        post_t, post_h = beat("post_t", KT), beat("post_h", KT)
        store = beat("store", 16)

        f_silu, f_mul, f_hi, f_lo = beat("f_silu", 1, 1), beat("f_mul", 1, 1), beat("f_hi"), beat("f_lo", 1, 1)

        g_in, g_act, g_dve, g_st = beat("g_in"), beat("g_act"), beat("g_dve"), beat("g_st", 16)

        in_half = beat("in_half")
        a_qh, a_ql, a_kh, a_kl, a_v, a_z = (beat(f"a_{n}", 2) for n in ("qh", "ql", "kh", "kl", "v", "z"))
        a_vtr, a_vh, a_vl = beat("a_vtr", 2), beat("a_vh", 2), beat("a_vl", 2)
        a_score, a_max, a_exp = beat("a_score", 16), beat("a_max", 16), beat("a_exp", 16)
        a_rec, a_nr, a_p0, a_mix = beat("a_rec", 8), beat("a_nr", 8), beat("a_p0", 8), beat("a_mix", 8)
        a_tr, a_hi_d, a_lo_d = beat("a_tr", 12), beat("a_hi_d", 12), beat("a_lo_d", 12)
        a_pv, a_o, a_sq, a_r = beat("a_pv", 2), beat("a_o", 2), beat("a_sq", 2), beat("a_r", 2)
        a_ss, a_std, a_y, a_yh, a_yl = (beat(f"a_{n}") for n in ("ss", "std", "y", "yh", "yl"))

        m_ld = beat("m_ld", 80)
        m_x, m_conv, m_silu, m_q = beat("m_x", 2), beat("m_conv", 8), beat("m_silu", 2), beat("m_q", 2)
        m_qkh, m_qkl, m_vt, m_vh, m_vl = beat("m_qkh", 3), beat("m_qkl", 3), beat("m_vt", 2), beat("m_vh", 2), beat("m_vl", 6)
        m_ktr, m_kw, m_kwh, m_kwl = beat("m_ktr"), beat("m_kw", 8), beat("m_kwh"), beat("m_kwl")
        m_vtr, m_dt, m_de, m_mask = beat("m_vtr", 2), beat("m_dt", 8), beat("m_de"), beat("m_mask")
        m_s, m_am, m_ah, m_al = beat("m_s"), beat("m_am"), beat("m_ah"), beat("m_al")
        m_p, m_c, m_ch, m_cl, m_num = beat("m_p", 7), beat("m_c", 7), beat("m_ch", 7), beat("m_cl", 7), beat("m_num", 8)
        m_den, m_rd, m_hm = beat("m_den", 1 + 2 * NC), beat("m_rd", NC), beat("m_hm", NC)
        m_ot, m_otr, m_so, m_g = beat("m_ot", 2), beat("m_otr", 2), beat("m_so", 2), beat("m_g")
        m_ss, m_std, m_r, m_n = beat("m_ss", 8), beat("m_std"), beat("m_r"), beat("m_n", 8)
        m_ntr, m_z, m_y, m_yh, m_yl = beat("m_ntr", 2), beat("m_z", 2), beat("m_y", 4), beat("m_yh", 2), beat("m_yl", 2)

        v_g, v_tr, v_tok, v_sq = beat("v_g", 1, 2), beat("v_tr", 1, 2), beat("v_tok", 1, 2), beat("v_sq", 8, 2)
        v_st = [beat(f"v_st{b}", 16, 1) for b in range(2)]
        v_r = beat("v_r")
        w_s, w_h, w_l = beat("w_s", 8, 1), beat("w_h", 1, 1), beat("w_l", 1, 1)
        e_vs, e_u, e_z, e_v, e_y, e_yh, e_yl = (beat("e_vs"), beat("e_u", 1, 1), beat("e_z", 1, 1), beat("e_v", 1, 1),
                                              beat("e_y", 2, 1), beat("e_yh"), beat("e_yl", 1, 1))
        sp_ld = beat("sp_ld", 32)

        block = ctx.enter_context(nc.Block())

        @block.sync
        def _(sp):
            def load_in(n, slot):
                sp.wait_ge(in_split.sem, in_split.at(n - 2))
                sp.dma_start(raw[slot][:], w_in[bass.ds(n, 1)].rearrange("a p t -> p (a t)"))\
                  .then_inc(in_load[slot].sem, 16)

            def load_c(n, source, row):
                sp.wait_ge(c_split.sem, c_split.at(n - 1))
                sp.dma_start(raw[C][:], source[bass.ds(row, 1)].rearrange("a p t -> p (a t)"))\
                  .then_inc(c_load.sem, 16)

            for n in range(MOD_BLOCKS):
                if n >= MOD_BUFFERS:
                    sp.wait_ge(mod_mm.sem, mod_mm.at(n - MOD_BUFFERS))
                sp.dma_start(mod_big[n % MOD_BUFFERS][:], mod_w[n]).then_inc(mod_ld[n % MOD_BUFFERS].sem, 16)
                if n < 2:
                    tiles = slice(n * KT // 2, (n + 1) * KT // 2)
                    sp.dma_start(resid[:, tiles, :], x_t[:, tiles, :]).then_inc(x_ld[n].sem, 16)
            load_in(0, 0)
            load_in(1, 1)
            with sp.Fori(1, F_TILES - 1) as f:
                load_in(2 * f, 0)
                load_in(2 * f + 1, 1)
                load_c(f - 1, w_c, f - 1)
            for s in range(4):
                load_in(IN_FFN_OUT - 2 + s, s % 2)
            load_c(C_GATES, w_c, C_GATES)
            for s in range(8):
                load_in(IN_DA + s, s % 2)
            with sp.Fori(1, DA_HEADS - 1) as h:
                for s in range(4):
                    load_in(IN_DA + 4 * h + (4 + s), s % 2)
                    if s == 0:
                        load_c(C_DA + h - 1, w_c, C_DA + h - 1)
            load_c(C_SG - 2, w_c, C_SG - 2)
            for s in range(2):
                load_in(IN_ML + s, s)
            load_c(C_SG - 1, w_c, C_SG - 1)
            with sp.Fori(0, ML_HEADS - 1) as h:
                for s in range(10):
                    load_in(IN_ML + 10 * h + (2 + s), s % 2)
            for s in range(8):
                load_in(IN_SV - 8 + s, s % 2)
            with sp.Fori(0, SG_TILES // 2) as j:
                for s in range(2):
                    load_in(IN_SV + 2 * j + s, s)
            load_in(IN_SG, 0)
            load_in(IN_SG + 1, 1)
            for b in range(2):
                sp.wait_ge(v_st[b].sem, v_st[b].at(SG_TILES // 2 - 1))
            load_c(C_SG, gv_scr, 0)
            with sp.Fori(1, SG_TILES - 1) as d:
                load_in(IN_SG + 2 * d, 0)
                load_c(C_SG + 2 * d - 1, gv_scr, d)
                load_in(IN_SG + 2 * d + 1, 1)
                load_c(C_SG + 2 * d, w_c, C_SG + d - 1)
            load_in(IN_SG_OUT - 2, 0)
            load_c(C_SG + 2 * SG_TILES - 3, gv_scr, SG_TILES - 1)
            for s in range(1, 4):
                load_in(IN_SG_OUT - 2 + s, s % 2)
            for k in range(KT):
                sp.wait_ge(post_h.sem, post_h.at(1, k))
                sp.dma_start(out[:, k, :], resid[:, k, :]).then_inc(store.sem, 16)
            sp.wait_ge(store.sem, 16 * KT)

        @block.gpsimd
        def _(pool):
            zeros = zero[:, 0:1].to_broadcast([P, T])
            pool.memset(ident[:], 0.0).then_inc(const.sem, 1)
            pool.memset(ident_b[:], 0.0).then_inc(const.sem, 1)
            pool.memset(mask_b[:], 0.0).then_inc(const.sem, 1)
            pool.memset(ones[:], 1.0).then_inc(const.sem, 1)
            pool.memset(causal[:], 1.0).then_inc(const.sem, 1)
            pool.memset(zero[:], 0.0).then_inc(const.sem, 1)
            pool.memset(eps[:], EPS).then_inc(const.sem, 1)
            for b in range(2):
                pool.memset(xpad[b][:], 0.0).then_inc(const.sem, 1)
            pool.wait_ge(const.sem, 9)
            for tile in (ident, ident_b):
                pool.affine_select(out=tile[:], in_=tile[:], compare_op=ALU.not_equal, fill=1.0, base=0,
                                   pattern=[[-1, P]], channel_multiplier=1).then_inc(const.sem, 1)
            pool.affine_select(out=mask_b[:], in_=mask_b[:], compare_op=ALU.is_ge, fill=MASKED, base=0,
                               pattern=[[-1, P]], channel_multiplier=1).then_inc(const.sem, 1)
            pool.affine_select(out=causal[:], in_=causal[:], compare_op=ALU.is_ge, fill=0.0, base=0,
                               pattern=[[1, P]], channel_multiplier=-1).then_inc(const.sem, 1)
            pool.sem_inc(in_split.sem, in_split.prime)
            pool.sem_inc(c_split.sem, c_split.prime)

            def split(n, slot, load, load_value, hi_done, used, done):
                pool.wait_ge(load.sem, load_value)
                pool.wait_ge(used.sem, used.at(n - used.prime))
                hi = whi[slot][:].rearrange("p k f -> p (k f)")
                pool.tensor_tensor(hi, raw[slot][:], zeros, ALU.add).then_inc(hi_done.sem, 1)
                pool.wait_ge(hi_done.sem, hi_done.at(n))
                pool.tensor_tensor(wlo[slot][:].rearrange("p k f -> p (k f)"), raw[slot][:], hi.bitcast(F32),
                                   ALU.subtract).then_inc(done.sem, 1)

            def split_in(n, slot, turn):
                split(n, slot, in_load[slot], in_load[slot].at(turn), in_hi, in_mm, in_split)

            def split_c(n):
                split(n, C, c_load, c_load.at(n), c_hi_done, c_mm, c_split)

            split_in(0, 0, 0)
            split_in(1, 1, 0)

            def low_part(hi_done, done, turn, low, src, high):
                pool.wait_ge(hi_done.sem, hi_done.at(turn))
                pool.tensor_tensor(low[:], src[:], high[:].bitcast(F32), ALU.subtract).then_inc(done.sem, 1)

            with pool.Fori(0, F_TILES // 2 - 1) as j:
                for b in range(2):
                    split_in(4 * j + 2 * (1 + b), 0, 2 * j + (1 + b))
                    split_in(4 * j + (2 * (1 + b) + 1), 1, 2 * j + (1 + b))
                    low_part(f_hi, f_lo, 2 * j + b, ffn_lo[b], ffn_p, ffn_hi[b])
                    split_c(2 * j + b)
            split_in(2 * F_TILES - 2, 0, F_TILES - 1)
            split_in(2 * F_TILES - 1, 1, F_TILES - 1)
            low_part(f_hi, f_lo, F_TILES - 2, ffn_lo[0], ffn_p, ffn_hi[0])
            for s in range(2):
                split_in(IN_FFN_OUT + s, s, IN_FFN_OUT // 2)
            low_part(f_hi, f_lo, F_TILES - 1, ffn_lo[1], ffn_p, ffn_hi[1])
            split_c(C_GATES)
            for s in range(8):
                split_in(IN_DA + s, s % 2, (IN_DA + s) // 2)
            pool.wait_ge(g_st.sem, 16 * 5)
            pool.memset(acc[:], 0.0).then_inc(acc_zero.sem, 1)
            with pool.Fori(1, DA_HEADS - 1) as h:
                for s in range(4):
                    split_in(IN_DA + 4 * h + (4 + s), s % 2, 2 * h + (IN_DA + 4 + s) // 2)
                    if s == 0:
                        split_c(C_DA + h - 1)
            split_c(C_SG - 2)
            for s in range(2):
                split_in(IN_ML + s, s, IN_ML // 2)
            split_c(C_SG - 1)
            def causal_decays(h):
                pool.wait_ge(m_de.sem, m_de.at(h))
                dt3 = decay_t[:].rearrange("s (c t) -> s c t", t=CHUNK)
                pool.tensor_tensor(dt3, dt3, causal[:].unsqueeze(1).to_broadcast([P, NC, P]), ALU.mult).then_inc(m_mask.sem, 1)

            with pool.Fori(0, ML_HEADS - 1) as h:
                for s in range(10):
                    split_in(IN_ML + 10 * h + (2 + s), s % 2, 5 * h + (IN_ML + 2 + s) // 2)
                    if s == 1:
                        causal_decays(h)
            for s in range(8):
                split_in(IN_SV - 8 + s, s % 2, (IN_SV - 8 + s) // 2)
                if s == 1:
                    causal_decays(ML_HEADS - 1)
            for s in range(2):
                split_in(IN_SV + s, s, IN_SV // 2)
            pool.wait_ge(post_h.sem, post_h.at(0))
            pool.memset(acc[:], 0.0).then_inc(acc_zero.sem, 1)
            pool.wait_ge(sp_ld.sem, sp_ld.at(0))
            pool.tensor_tensor(wsp[:], wsp[:], causal[:].unsqueeze(1).to_broadcast([P, SG_GROUPS, P]), ALU.mult).then_inc(const.sem, 1)
            with pool.Fori(1, SG_TILES // 2) as j:
                for s in range(2):
                    split_in(IN_SV + 2 * j + s, s, j + IN_SV // 2)
            for s in range(2):
                split_in(IN_SG + s, s, IN_SG // 2)
            split_c(C_SG)

            def sg_tile(d, e, last=False):
                split_in(IN_SG + 2 * d, 0, d + IN_SG // 2)
                low_part(e_yh, e_yl, d - 1, sy_lo[1 - e], sg_v, sy_hi[1 - e])
                split_c(C_SG + 2 * d - 1)
                split_in(IN_SG + 2 * d + 1, 1, d + IN_SG // 2)
                if not last:
                    split_c(C_SG + 2 * d)

            sg_tile(1, 1)
            with pool.Fori(1, SG_GROUPS - 1) as g:
                for e in range(2):
                    sg_tile(2 * g + e, e)
            sg_tile(SG_TILES - 2, 0)
            sg_tile(SG_TILES - 1, 1, last=True)
            for s in range(2):
                split_in(IN_SG_OUT + s, s, IN_SG_OUT // 2)
            low_part(e_yh, e_yl, SG_TILES - 1, sy_lo[1], sg_v, sy_hi[1])

        @block.tensor
        def _(pe):
            pe.sem_inc(in_mm.sem, in_mm.prime)
            pe.sem_inc(c_mm.sem, c_mm.prime)
            pe.sem_inc(v_tr.sem, v_tr.prime)

            def three(dst, w_h, w_l, r_h, r_l, first, last):
                pe.matmul(dst, w_h, r_h, start=first, stop=False, skip_group_check=True)
                pe.matmul(dst, w_h, r_l, start=False, stop=False, skip_group_check=True)
                return pe.matmul(dst, w_l, r_h, start=False, stop=last, skip_group_check=True)

            def project(n, slot, stream=in_split, done=in_mm, bank=None):
                dst = PS[slot if bank is None else bank]
                pe.wait_ge(stream.sem, stream.at(n))
                for t0 in (0, HALF):
                    for k in range(KT):
                        mm = three(dst[:, t0:t0 + HALF], whi[slot][:, k, :], wlo[slot][:, k, :],
                                   h_hi[:, k, t0:t0 + HALF], h_lo[:, k, t0:t0 + HALF], k == 0, k == KT - 1)
                mm.then_inc(done.sem, 1)

            def project_first(use, slabs):
                for slot, split, value, _, _ in slabs:
                    pe.wait_ge(split.sem, value)
                for k in range(KT):
                    pe.wait_ge(s_lo.sem, s_lo.at(use, k))
                    for slot, _, _, bank, done in slabs:
                        for e in range(2):
                            cols = slice(e * HALF, (e + 1) * HALF)
                            mm = three(PS[bank][:, cols], whi[slot][:, k, :], wlo[slot][:, k, :],
                                       h_hi[:, k, cols], h_lo[:, k, cols], k == 0, k == KT - 1)
                            if k == KT - 1 and done[e] is not None:
                                mm.then_inc(done[e].sem, 1)

            def project_quarter(n, slot, part):
                t0 = part // 2 * HALF
                if part == 0:
                    pe.wait_ge(in_split.sem, in_split.at(n))
                for k in range(part % 2 * (KT // 2), (part % 2 + 1) * (KT // 2)):
                    mm = three(PS[slot][:, t0:t0 + HALF], whi[slot][:, k, :], wlo[slot][:, k, :],
                               h_hi[:, k, t0:t0 + HALF], h_lo[:, k, t0:t0 + HALF], k == 0, k == KT - 1)
                if part == 3:
                    mm.then_inc(in_mm.sem, 1)

            def out_half(slot, d, e, dst, r_h, r_l, done):
                cols = slice(e * HALF, (e + 1) * HALF)
                mm = three(dst[:, cols], whi[slot][:, d, :], wlo[slot][:, d, :], r_h[:, cols], r_l[:, cols], True, True)
                mm.then_inc((done if d == KT - 1 and e == 1 else out_mm).sem, 1)

            def project_out(n, o, r_h, r_l, slot=C, split=c_split, done=c_mm):
                pe.wait_ge(split.sem, split.at(n))
                for d in range(KT):
                    for e in range(2):
                        if d >= 2:
                            pe.wait_ge(out_ev.sem, out_ev.at(o, 2 * (d - 2) + e))
                        else:
                            pe.wait_ge(out_ev.sem, out_ev.at(o - 1, 2 * (KT - 2 + d) + e))
                        out_half(slot, d, e, PS[2 + d % 2], r_h, r_l, done)

            def project_out_in(n, o, r_h, r_l, slot):
                project_out(n, o, r_h, r_l, slot, in_split, in_mm)

            def sum_squares(norm):
                for k in range(KT):
                    pe.wait_ge(n_sq.sem, n_sq.at(norm, k))
                    for t0 in (0, HALF):
                        mm = pe.matmul(PS[0][:, t0:t0 + HALF], ones[:], sq[k % 2][:, t0:t0 + HALF],
                                       start=(k == 0), stop=(k == KT - 1), skip_group_check=True)
                    mm.then_inc(n_ssum.sem, 1)

            def turn_tiles(dst, src, sem):
                for b in range(KT):
                    mm = pe.transpose(dst[:, b * P:(b + 1) * P], src(b), ident[:])
                mm.then_inc(sem, 1)

            def mod_block(n):
                pe.wait_ge(mod_ld[n % MOD_BUFFERS].sem, mod_ld[n % MOD_BUFFERS].at(n // MOD_BUFFERS))
                if n >= 2:
                    pe.wait_ge(mod_out.sem, mod_out.at(n - 2))
                for k in range(KT):
                    mm = pe.matmul(PS[3][0:1, n % 2 * HALF:(n % 2 + 1) * HALF], silu_c[:, k:k + 1], mod_big[n % MOD_BUFFERS][:, k, :],
                                   start=(k == 0), stop=(k == KT - 1), skip_group_check=True)
                mm.then_inc(mod_mm.sem, 1)

            def mod_columns(half):
                pe.wait_ge(mod_out.sem, mod_out.at((half + 1) * MOD_HALF - 1))
                for j in range(MOD_HALF * HALF // P):
                    row = mod_row[0:1, j * P // HALF, j * P % HALF:j * P % HALF + P]
                    mm = pe.transpose(PS[1][:, HALF + j:HALF + j + 1], row, ident[0:1, 0:1])
                mm.then_inc(mod_turn.sem, 1)

            pe.wait_ge(const.sem, 13)
            pe.wait_ge(siluc.sem, 1)
            for n in range(MOD_HALF):
                mod_block(n)
            mod_columns(0)
            pe.wait_ge(lam_done.sem, 1)
            pe.matmul(PS[0][:, 0:2], ones[:], lam_prod[:], start=True, stop=True).then_inc(lam_mm.sem, 1)
            for n in range(MOD_HALF, MOD_BLOCKS - 1):
                mod_block(n)
            pe.wait_ge(small_ld.sem, small_ld.at(0))
            pe.wait_ge(lam_x.sem, 1)
            pe.wait_ge(mod_col.sem, 1)
            for j in range(KT):
                g, e = j // 2, j % 2
                pe.wait_ge(p_done.sem, 2 * g + 2)
                if j >= 2:
                    pe.wait_ge(z_done.sem, j - 1)
                for t0 in (0, HALF):
                    for k in range(2):
                        mm = pe.matmul(PS[e][:, t0:t0 + HALF], pw[:, g, k, e * P:(e + 1) * P],
                                       acc[:, 2 * g + k, t0:t0 + HALF], start=(k == 0), stop=(k == 1),
                                       skip_group_check=True)
                mm.then_inc(pool_mm.sem, 1)

            def mean_of(norm, ready, count):
                for k in range(KT):
                    pe.wait_ge(ready, count(k))
                    for t0 in (0, HALF):
                        mm = pe.matmul(PS[2][:, t0:t0 + HALF], ones[:], resid[:, k, t0:t0 + HALF],
                                       start=(k == 0), stop=(k == KT - 1), skip_group_check=True)
                mm.then_inc(n_mean_mm.sem, 1)

            mean_of(0, z_done.sem, lambda k: k + 1)
            sum_squares(0)
            mod_block(MOD_BLOCKS - 1)
            mod_columns(1)
            pe.wait_ge(n_std.sem, 1)
            pe.wait_ge(mod_col.sem, 2)
            project_first(0, [(slot, in_split, in_split.at(slot), slot, (None, in_mm)) for slot in range(2)])

            def ffn_in(f):
                pe.wait_ge(f_silu.sem, f_silu.at(f - 1))
                project(2 * f, 0)
                pe.wait_ge(f_mul.sem, f_mul.at(f - 1))
                project(2 * f + 1, 1)

            def ffn_out(f, b):
                pe.wait_ge(f_lo.sem, f_lo.at(f))
                project_out(f, f, ffn_hi[b], ffn_lo[b])

            with pe.Fori(0, F_TILES // 2 - 1) as j:
                for b in range(2):
                    ffn_in(2 * j + (1 + b))
                    ffn_out(2 * j + b, b)
            ffn_in(F_TILES - 1)
            for b in range(2):
                pe.wait_ge(f_lo.sem, f_lo.at(F_TILES - 2 + b))
                project_out_in(IN_FFN_OUT + b, F_TILES - 2 + b, ffn_hi[b], ffn_lo[b], b)
            for k in range(KT):
                pe.wait_ge(out_ev.sem, out_ev.at(F_TILES - 1, 2 * k + 1))
                for t0 in (0, HALF):
                    if k == 0 and t0 == 0:
                        pe.wait_ge(out_ev.sem, out_ev.at(F_TILES - 1))
                    mm = pe.matmul(PS[2][:, t0:t0 + HALF], ones[:], resid[:, k, t0:t0 + HALF],
                                   start=(k == 0), stop=(k == KT - 1), skip_group_check=True)
            mm.then_inc(n_mean_mm.sem, 1)
            sum_squares(1)
            pe.wait_ge(n_std.sem, n_std.at(1))
            sum_squares(2)
            pe.wait_ge(n_std.sem, n_std.at(2))
            project_first(1, [(C, c_split, c_split.at(C_GATES), 0, (None, c_mm)),
                              (0, in_split, in_split.at(IN_DA), 3, (in_half, in_mm))])

            score_bank = (PS[0], PS[1])
            turn_bank = PS[2][:, 0:HALF]
            value_bank = PS[2][:, HALF:T]

            def da_half(h, s, e, ks=range(KT)):
                slot, t0 = s % 2, e * HALF
                if e == 0 and ks[0] == 0:
                    pe.wait_ge(in_split.sem, in_split.at(4 * h + (IN_DA + s)))
                for k in ks:
                    mm = three(PS[3][:, t0:t0 + HALF], whi[slot][:, k, :], wlo[slot][:, k, :],
                               h_hi[:, k, t0:t0 + HALF], h_lo[:, k, t0:t0 + HALF], k == 0, k == KT - 1)
                if ks[-1] == KT - 1:
                    mm.then_inc((in_half, in_mm)[e].sem, 1)

            def da_out_tile(h, d, before=None):
                if d == 0:
                    pe.wait_ge(c_split.sem, c_split.at(C_DA + h))
                    pe.wait_ge(a_yl.sem, a_yl.at(h))
                for e in range(2):
                    if before is not None:
                        pe.wait_ge(out_ev.sem, out_ev.at(OUT_DA + h, 2 * before + e))
                    out_half(C, d, e, PS[3], y_hi, y_lo, c_mm)

            def da_scores(h, i):
                if i == 0:
                    pe.wait_ge(a_kl.sem, a_kl.at(h, 0))
                if i == HALF // P:
                    pe.wait_ge(a_kl.sem, a_kl.at(h, 1))
                    pe.wait_ge(a_vl.sem, a_vl.at(h))
                cols = slice(i * P, (i + 1) * P)
                for c in range(2):
                    rows = slice(c * DA_QK, (c + 1) * DA_QK)
                    if i >= 1:
                        pe.wait_ge(a_exp.sem, a_exp.at(h, 2 * (i - 1) + c))
                    for t0 in range(0, (i + 1) * P, HALF):
                        t1 = min(t0 + HALF, (i + 1) * P)
                        three(score_bank[c][:, t0:t1], q_hi[rows, cols], q_lo[rows, cols],
                              k_hi[rows, t0:t1], k_lo[rows, t0:t1], True, True)
                    pe.matmul(score_bank[c][:, cols], ident_b[:], mask_b[:], start=False, stop=True,
                              skip_group_check=True).then_inc(a_score.sem, 1)

            def da_turn(h, i, part):
                pe.wait_ge(a_mix.sem, a_mix.at(h, i))
                if part == 1 or i >= 1:
                    pe.wait_ge(a_lo_d.sem, a_lo_d.at(h, turn_event(i, part) - 1))
                for b in range(4 * part, min(4 * part + 4, i + 1)):
                    mm = pe.transpose(turn_bank[:, (b % 4) * P:(b % 4 + 1) * P], p_0[i % 2][:, b * P:(b + 1) * P], ident[:])
                mm.then_inc(a_tr.sem, 1)

            def da_values(h, i):
                pe.wait_ge(a_lo_d.sem, a_lo_d.at(h, turn_event(i, i // 4)))
                if i == 0:
                    pe.wait_ge(a_vl.sem, a_vl.at(h))
                if i == 4:
                    pe.wait_ge(a_o.sem, a_o.at(h, 0))
                    pe.wait_ge(a_sq.sem, a_sq.at(h, 0))
                for b in range(i + 1):
                    mm = three(value_bank[:, (i % 4) * P:(i % 4 + 1) * P], v_hi[:, b, :], v_lo[:, b, :],
                               a_hi[:, b, :], a_lo[:, b, :], b == 0, b == i)
                if i % 4 == 3:
                    mm.then_inc(a_pv.sem, 1)

            def da_squares(h):
                pe.wait_ge(a_sq.sem, a_sq.at(h))
                pe.wait_ge(a_o.sem, a_o.at(h))
                for t0 in (0, HALF):
                    mm = pe.matmul(PS[2][:, t0:t0 + HALF], ones[:], da_sq[:, t0:t0 + HALF], start=True, stop=True,
                                   skip_group_check=True)
                mm.then_inc(a_ss.sem, 1)

            def da_head(h, first=False, last=False):
                out = not first
                if not first:
                    da_values(h - 1, KT - 1)
                da_scores(h, 0)
                pe.wait_ge(a_v.sem, a_v.at(h))
                for e in range(2):
                    for b in range(4):
                        mm = pe.transpose(score_bank[e][:, HALF + b * P:HALF + (b + 1) * P],
                                          v_t[:, (4 * e + b) * P:(4 * e + b + 1) * P], ident[:])
                    mm.then_inc(a_vtr.sem, 1)
                if out:
                    da_half(h, DA_Z_SLAB, 0, range(0, KT // 2))
                    da_squares(h - 1)
                    da_half(h, DA_Z_SLAB, 0, range(KT // 2, KT))
                else:
                    da_half(h, DA_Z_SLAB, 0)
                da_scores(h, 1)
                if out:
                    pe.wait_ge(a_std.sem, a_std.at(h - 1))
                da_turn(h, 0, 0)
                pe.wait_ge(a_kl.sem, a_kl.at(h, 1))
                da_half(h, DA_Z_SLAB, 1)
                da_scores(h, 2)
                da_values(h, 0)
                da_turn(h, 1, 0)
                if not last:
                    pe.wait_ge(a_z.sem, a_z.at(h, 0))
                    da_half(h + 1, DA_V_SLAB, 0)
                da_scores(h, 3)
                if out:
                    pe.wait_ge(a_z.sem, a_z.at(h, 1))
                    if not last:
                        pe.wait_ge(a_v.sem, a_v.at(h + 1, 0))
                    da_out_tile(h - 1, 0)
                da_values(h, 1)
                da_turn(h, 2, 0)
                if not last:
                    if out:
                        pe.wait_ge(out_ev.sem, out_ev.at(OUT_DA + h - 1, 1))
                    else:
                        pe.wait_ge(a_z.sem, a_z.at(h, 1))
                    da_half(h + 1, DA_V_SLAB, 1)
                da_scores(h, 4)
                if out:
                    if not last:
                        pe.wait_ge(a_v.sem, a_v.at(h + 1, 1))
                    da_out_tile(h - 1, 1, before=0)
                da_values(h, 2)
                da_turn(h, 3, 0)
                if out:
                    for d in (2, 3):
                        da_out_tile(h - 1, d, before=d - 1)
                for i in range(4, KT):
                    s, e = (DA_Q_SLAB, DA_K_SLAB)[(i - 4) // 2], i % 2
                    if i + 1 < KT:
                        da_scores(h, i + 1)
                    if not last and i >= 5:
                        before = (a_ql, a_ql, a_kl)[i - 5]
                        pe.wait_ge(before.sem, before.at(h + 1, (0, 1, 0)[i - 5]))
                    if not last and i == 4 and first:
                        pe.wait_ge(a_v.sem, a_v.at(h + 1, 1))
                    if out:
                        da_out_tile(h - 1, i, before=i - 1)
                    da_values(h, i - 1)
                    da_turn(h, i, 0)
                    if out:
                        pe.wait_ge(out_ev.sem, out_ev.at(OUT_DA + h - 1, 2 * i + e))
                    if not last:
                        da_half(h + 1, s, e)
                    da_turn(h, i, 1)

            for n, (s, e) in enumerate((s, e) for s in (DA_Q_SLAB, DA_K_SLAB) for e in range(2)):
                read = (a_v, a_ql)[n // 2]
                pe.wait_ge(read.sem, read.at(0, e))
                da_half(0, s, e)
            pe.wait_ge(g_in.sem, 2)
            da_head(0, first=True)
            with pe.Fori(1, DA_HEADS - 1) as h:
                da_head(h)
            da_head(DA_HEADS - 1, last=True)
            da_values(DA_HEADS - 1, KT - 1)
            project(IN_ML, 0)
            da_squares(DA_HEADS - 1)
            project(IN_ML + 1, 1)
            pe.wait_ge(a_std.sem, a_std.at(DA_HEADS - 1))
            pe.wait_ge(a_yl.sem, a_yl.at(DA_HEADS - 1))
            project_out(C_DA + DA_HEADS - 1, OUT_DA + DA_HEADS - 1, y_hi, y_lo)

            def ml_head(h, last=False):
                pe.wait_ge(m_x.sem, m_x.at(h, 0))
                project(IN_ML + 10 * h + 2, 0)
                pe.wait_ge(m_x.sem, m_x.at(h, 1))
                project(IN_ML + 10 * h + 3, 1)
                pe.wait_ge(out_ev.sem, out_ev.at(OUT_ML + 2 * h - 1))
                pe.wait_ge(m_silu.sem, m_silu.at(h, 1))
                turn_tiles(PS[2], lambda b: mt[:, b * P:(b + 1) * P], m_ktr.sem)
                pe.wait_ge(m_qkl.sem, m_qkl.at(h, 2))
                for c in range(NC):
                    cols = slice(c * CHUNK, (c + 1) * CHUNK)
                    mm = three(PS[3][:, cols], mk_hi[:, cols], mk_lo[:, cols], mq_hi[:, cols], mq_lo[:, cols], True, True)
                mm.then_inc(m_s.sem, 1)
                pe.wait_ge(m_vt.sem, m_vt.at(h, 0))
                turn_tiles(PS[0], lambda b: v_t0[:, b * P:(b + 1) * P], m_vtr.sem)
                pe.wait_ge(m_vt.sem, m_vt.at(h, 1))
                turn_tiles(PS[1], lambda b: mt[:, b * P:(b + 1) * P], m_vtr.sem)

                def state_part(c):
                    if c >= 2:
                        pe.wait_ge(m_c.sem, m_c.at(h, c - 2))
                    dst = PS[3][:, (c % 2) * HALF:(c % 2) * HALF + VA]
                    three(dst, kw_hi[:, c, :], kw_lo[:, c, :], va_hi[:, c, :], va_lo[:, c, :], True, True)\
                        .then_inc(m_p.sem, 1)

                pe.wait_ge(m_kwl.sem, m_kwl.at(h))
                pe.wait_ge(m_vl.sem, m_vl.at(h))
                pe.wait_ge(m_am.sem, m_am.at(h))
                state_part(0)
                pe.wait_ge(m_al.sem, m_al.at(h))
                for c in range(NC):
                    if c + 1 < NC - 1:
                        state_part(c + 1)
                    if c >= 2:
                        pe.wait_ge(m_hm.sem, m_hm.at(h, c - 2))
                    cols = slice(c * CHUNK, (c + 1) * CHUNK)
                    dst = PS[2][:, (c % 2) * HALF:(c % 2) * HALF + VA]
                    mm = three(dst, am_hi[:, cols], am_lo[:, cols], va_hi[:, c, :], va_lo[:, c, :], True, c == 0)
                    if c >= 1:
                        pe.wait_ge(m_cl.sem, m_cl.at(h, c - 1))
                        mm = three(dst, mi_hi[:, cols], mi_lo[:, cols], c_hi[:], c_lo[:], False, True)
                    mm.then_inc(m_num.sem, 1)
                    project_quarter(IN_ML + 10 * h + (4 + c // 4), c // 4, c % 4)
                pe.wait_ge(m_ot.sem, m_ot.at(h, 0))
                project(IN_ML + 10 * h + 6, 0)
                for e in range(2):
                    pe.wait_ge(m_ot.sem, m_ot.at(h, e))
                    if e == 0:
                        pe.wait_ge(m_hm.sem, m_hm.at(h))
                    turn_tiles(PS[2 + e], lambda b: (xp[:, b * P:(b + 1) * P], mt[:, b * P:(b + 1) * P])[e], m_otr.sem)
                project(IN_ML + 10 * h + 7, 1)
                pe.wait_ge(m_n.sem, m_n.at(h))
                for e in range(2):
                    turn_tiles(PS[2 + e], lambda b: hm[:, b, e * P:(e + 1) * P], m_ntr.sem)
                if not last:
                    for e in range(2):
                        pe.wait_ge(m_z.sem, m_z.at(h, e))
                        project(IN_ML + 10 * h + (8 + e), e)
                for e in range(2):
                    pe.wait_ge(m_yl.sem, m_yl.at(h, e))
                    if e == 0:
                        pe.wait_ge(m_y.sem, m_y.at(h, 1))
                    project_out_in(IN_ML + 10 * h + ((8 if last else 10) + e), OUT_ML + 2 * h + e, my_hi[e], my_lo[e], e)

            with pe.Fori(0, ML_HEADS - 1) as h:
                ml_head(h)
            ml_head(ML_HEADS - 1, last=True)

            pe.wait_ge(m_z.sem, m_z.at(ML_HEADS - 1))
            sum_squares(3)
            pe.wait_ge(n_std.sem, n_std.at(3))
            sum_squares(4)
            pe.wait_ge(n_std.sem, n_std.at(4))
            def sg_turn(j, s):
                pe.wait_ge(v_g.sem, v_g.at(2 * j + s))
                pe.wait_ge(v_tok.sem, v_tok.at(2 * j + (s - 2)))
                turn_tiles(PS[2 + s], lambda b: g_t[s][:, b * P:(b + 1) * P], v_tr.sem)

            project_first(2, [(s, in_split, in_split.at(IN_SV + s), s, (None, in_mm)) for s in range(2)])
            sg_turn(0, 0)
            with pe.Fori(1, SG_TILES // 2) as j:
                for s in range(2):
                    pe.wait_ge(v_g.sem, v_g.at(2 * j + (s - 2)))
                    project(IN_SV + 2 * j + s, s)
                    sg_turn(j + (s - 1), 1 - s)
            sg_turn(SG_TILES // 2 - 1, 1)

            def sg_tile(d, e, g, first):
                pe.wait_ge(e_u.sem, e_u.at(d - 1))
                project(IN_SG + 2 * d, 0)
                if first and e == 0:
                    pe.wait_ge(v_tok.sem, v_tok.at(SG_TILES - 1))
                n = C_SG if first and e == 0 else C_SG + 2 * d - 1
                pe.wait_ge(w_l.sem, w_l.at(g))
                pe.wait_ge(e_v.sem, e_v.at(d - 1))
                pe.wait_ge(c_split.sem, c_split.at(n))
                pe.wait_ge(out_ev.sem, out_ev.at(OUT_SG + d - 2))
                for c in range(NC):
                    mm = three(PS[2][:, c * CHUNK:(c + 1) * CHUNK], whi[C][:, c, :], wlo[C][:, c, :],
                               wr_hi[:, c, :], wr_lo[:, c, :], True, True)
                mm.then_inc(c_mm.sem, 1)
                pe.wait_ge(e_z.sem, e_z.at(d - 1))
                project(IN_SG + 2 * d + 1, 1)

            def sg_out(d, e, n):
                pe.wait_ge(e_yl.sem, e_yl.at(d))
                project_out(n, OUT_SG + d, sy_hi[e], sy_lo[e])

            sg_tile(0, 0, 0, True)
            sg_tile(1, 1, 0, True)
            pe.wait_ge(e_v.sem, e_v.at(1))
            sg_out(0, 0, C_SG + 2)

            def sg_turn_out(g, e):
                sg_tile(2 * g + e, e, g, False)
                pe.wait_ge(e_v.sem, e_v.at(2 * g + e))
                sg_out(2 * g + (e - 1), 1 - e, C_SG + 4 * g + 2 * e)

            with pe.Fori(1, SG_GROUPS - 1) as g:
                for e in range(2):
                    sg_turn_out(g, e)
            sg_turn_out(SG_GROUPS - 1, 0)
            sg_tile(SG_TILES - 1, 1, SG_GROUPS - 1, False)
            pe.wait_ge(e_v.sem, e_v.at(SG_TILES - 1))
            for b in range(2):
                pe.wait_ge(e_yl.sem, e_yl.at(SG_TILES - 2 + b))
                project_out_in(IN_SG_OUT + b, OUT_SG + SG_TILES - 2 + b, sy_hi[b], sy_lo[b], b)
            pe.wait_ge(e_z.sem, e_z.at(SG_TILES - 1))
            sum_squares(5)

        @block.scalar
        def _(act):
            for b in (f_silu, v_g, v_sq, w_h, e_u, e_z):
                act.sem_inc(b.sem, b.prime * b.per)
            for b in v_st:
                act.sem_inc(b.sem, b.prime * b.per)
            act.dma_start(par[:], params).then_inc(par_ld.sem, 16)
            act.dma_start(pw[:], pool_w).then_inc(small_ld.sem, 16)
            act.dma_start(edge[:], edges).then_inc(small_ld.sem, 16)
            act.wait_ge(par_ld.sem, 16)
            act.activation(silu_c[:], par[:, COL["c"]:COL["c"] + KT], ACT.Silu).then_inc(siluc.sem, 1)

            def mod_read(n):
                act.wait_ge(mod_mm.sem, mod_mm.at(n))
                if n == MOD_HALF:
                    act.wait_ge(mod_turn.sem, mod_turn.at(0))
                act.activation(mod_row[0:1, n % MOD_HALF, :], PS[3][0:1, n % 2 * HALF:(n % 2 + 1) * HALF], ACT.Copy)\
                   .then_inc(mod_out.sem, 1)

            def pad(k):
                act.wait_ge(x_ld[k // (KT // 2)].sem, 16)
                if k >= 2:
                    act.wait_ge(p_sum.sem, p_sum.at(k - 2))
                act.activation(xpad[k % 2][:, PAD:PAD + T], resid[:, k, :], ACT.Copy).then_inc(px.sem, 1)

            def modulate(k):
                if k >= 2:
                    act.wait_ge(p_done.sem, p_done.at(k - 2))
                act.activation(xpad[k % 2][:, PAD:PAD + T], resid[:, k, :], ACT.Identity, scale=sc1p[:, k:k + 1], bias=mod[:, k:k + 1])\
                   .then_inc(p_hx.sem, 1)
                act.wait_ge(p_hx.sem, p_hx.at(k))
                act.activation(resid[:, k, :], resid[:, k, :], ACT.Copy, scale=ALPHA).then_inc(x_scaled.sem, 1)

            act.wait_ge(const.sem, 13)
            pad(0)
            for k in range(1, MOD_HALF):
                mod_read(k - 1)
                pad(k)
            mod_read(MOD_HALF - 1)
            for k in range(MOD_HALF, KT):
                pad(k)
            act.wait_ge(lam_mm.sem, 1)
            act.activation(lam_exp[:], PS[0][:, 0:2], ACT.Exp).then_inc(lam_x.sem, 1)
            act.wait_ge(sc1_done.sem, 1)
            for k in range(KT):
                modulate(k)
                if k in (2, 5):
                    mod_read(MOD_HALF + k // 3)
            for n in range(MOD_HALF + 2, MOD_BLOCKS - 1):
                mod_read(n)

            def square(norm, src, ready, value):
                for k in range(KT):
                    act.wait_ge(ready, value(k))
                    if k >= 2:
                        act.wait_ge(n_ssum.sem, n_ssum.at(norm, k - 2))
                    act.activation(sq[k % 2][:], src[:, k, :], ACT.Square).then_inc(n_sq.sem, 1)
                act.wait_ge(n_ssum.sem, n_ssum.at(norm))
                act.activation(std[:], PS[0], ACT.Sqrt, bias=eps[:, 0:1], scale=1.0 / D).then_inc(n_std.sem, 1)

            def mean_out(norm):
                act.wait_ge(n_mean_mm.sem, n_mean_mm.at(norm))
                act.activation(mean[:], PS[2], ACT.Copy, scale=1.0 / D).then_inc(n_mean.sem, 1)

            def split_high(use):
                for k in range(KT):
                    act.wait_ge(s_tmp.sem, s_tmp.at(use, k))
                    act.activation(h_hi[:, k, :], tmp[k % 2][:], ACT.Copy).then_inc(s_hi.sem, 1)

            mean_out(0)
            square(0, resid, n_cent.sem, lambda k: n_cent.at(0, k))
            mod_read(MOD_BLOCKS - 1)
            act.wait_ge(mod_col.sem, 2)
            for k in range(KT):
                act.wait_ge(n_out.sem, n_out.at(0, k))
                if k >= 2:
                    act.wait_ge(s_lo.sem, s_lo.at(0, k - 2))
                act.activation(tmp[k % 2][:], resid[:, k, :], ACT.Identity, scale=sc2p[:, k:k + 1], bias=ffn_b0[:, k:k + 1])\
                   .then_inc(s_tmp.sem, 1)
                act.wait_ge(s_tmp.sem, s_tmp.at(0, k))
                act.activation(h_hi[:, k, :], tmp[k % 2][:], ACT.Copy).then_inc(s_hi.sem, 1)
            for k in range(KT):
                act.activation(resid[:, k, :], resid[:, k, :], ACT.Identity, scale=ALPHA,
                               bias=res_b0[:, k:k + 1]).then_inc(n_res.sem, 1)

            def ffn(f, b):
                act.wait_ge(in_mm.sem, in_mm.at(2 * f))
                act.wait_ge(f_mul.sem, f_mul.at(f - 1))
                act.activation(ffn_g[:], PS[0], ACT.Silu).then_inc(f_silu.sem, 1)
                act.wait_ge(f_mul.sem, f_mul.at(f))
                act.activation(ffn_hi[b][:], ffn_p[:], ACT.Copy).then_inc(f_hi.sem, 1)

            act.wait_ge(s_lo.sem, s_lo.at(0))
            with act.Fori(0, F_TILES // 2) as j:
                for b in range(2):
                    ffn(2 * j + b, b)

            mean_out(1)
            square(1, resid, n_cent.sem, lambda k: n_cent.at(1, k))
            square(2, resid, n_out.sem, lambda k: n_out.at(1, k))
            act.dma_start(res_scr, resid[:]).then_inc(spill.sem, 16)
            split_high(1)

            act.wait_ge(s_lo.sem, s_lo.at(1))
            act.wait_ge(spill.sem, spill.at(0))
            act.wait_ge(c_mm.sem, c_mm.at(C_GATES))
            gb = COL["gate_b"]
            flat = lambda tile: tile[:].rearrange("h c t -> h (c t)")
            act.activation(flat(g_i), PS[0][0:4, :], ACT.Identity, bias=par[0:4, gb:gb + 1]).then_inc(g_in.sem, 1)
            act.activation(flat(g_f), PS[0][32:36, :], ACT.Identity, bias=par[32:36, gb:gb + 1]).then_inc(g_in.sem, 1)
            act.wait_ge(g_in.sem, 2)
            act.activation(g_a[:], g_f[:], ACT.Abs).then_inc(g_act.sem, 1)
            act.wait_ge(g_act.sem, 1)
            act.activation(g_a[:], g_a[:], ACT.Exp, scale=-1.0).then_inc(g_act.sem, 1)
            act.wait_ge(g_act.sem, 2)
            act.activation(g_a[:], g_a[:], ACT.Ln, bias=ones[0:4, 0:1]).then_inc(g_act.sem, 1)

            def gate_rows():
                act.wait_ge(g_dve.sem, GATE_STEPS)
                act.activation(g_d[:], g_d[:], ACT.Exp, scale=-1.0).then_inc(g_act.sem, 1)
                act.activation(g_d2[:], g_d2[:], ACT.Exp, scale=-1.0).then_inc(g_act.sem, 1)
                act.activation(g_d3[:], g_d3[:], ACT.Exp).then_inc(g_act.sem, 1)
                act.wait_ge(g_act.sem, 6)
                for n, row in enumerate((g_max, g_d, g_u, g_d3, g_d2)):
                    act.dma_start(gate_scr[n], flat(row)).then_inc(g_st.sem, 16)

            turn_bank = PS[2][:, 0:HALF]
            value_bank = PS[2][:, HALF:T]
            half_of = lambda e: slice(e * HALF, (e + 1) * HALF)

            def half_done(h, s, e):
                done, n = (in_half, 4 * h + s) if e == 0 else (in_mm, 4 * h + (IN_DA + s))
                act.wait_ge(done.sem, done.at(n))

            def da_z_half(h, e, first):
                half_done(h, DA_Z_SLAB, e)
                if not first:
                    act.wait_ge(a_o.sem, a_o.at(h - 1, e))
                act.activation(da_z[:, half_of(e)], PS[3][:, half_of(e)], ACT.Silu).then_inc(a_z.sem, 1)

            def da_v_half(h, e):
                half_done(h, DA_V_SLAB, e)
                act.activation(v_t[:, half_of(e)], PS[3][:, half_of(e)], ACT.Copy).then_inc(a_v.sem, 1)

            def da_q_half(h, e, first=False):
                half_done(h, DA_Q_SLAB, e)
                if not first:
                    act.wait_ge(a_score.sem, a_score.at(h - 1, (7, 15)[e]))
                act.activation(q_hi[:, half_of(e)], PS[3][:, half_of(e)], ACT.Copy, scale=DA_QK ** -0.5).then_inc(a_qh.sem, 1)

            def da_k_half(h, e, first=False):
                half_done(h, DA_K_SLAB, e)
                if not first:
                    act.wait_ge(a_score.sem, a_score.at(h - 1))
                act.activation(k_hi[:, half_of(e)], PS[3][:, half_of(e)], ACT.Copy).then_inc(a_kh.sem, 1)

            def da_turned(h, i, part):
                blocks = slice(4 * part, min(4 * part + 4, i + 1))
                act.wait_ge(a_tr.sem, a_tr.at(h, turn_event(i, part)))
                act.activation(a_hi[:, blocks, :].rearrange("p b q -> p (b q)"),
                               turn_bank[:, 0:(blocks.stop - blocks.start) * P], ACT.Copy).then_inc(a_hi_d.sem, 1)

            def da_square(h, e):
                act.wait_ge(a_o.sem, a_o.at(h, e))
                act.activation(da_sq[:, half_of(e)], value_bank, ACT.Square).then_inc(a_sq.sem, 1)

            def da_root(h):
                act.wait_ge(a_ss.sem, a_ss.at(h))
                act.activation(da_sq[:], PS[2], ACT.Sqrt, bias=eps[:, 0:1], scale=1.0 / DA_V).then_inc(a_std.sem, 1)

            def da_high(h):
                act.wait_ge(a_y.sem, a_y.at(h))
                act.activation(y_hi[:], da_o[:], ACT.Copy).then_inc(a_yh.sem, 1)

            def da_head(h, first=False, last=False):
                if not first:
                    da_square(h - 1, 1)
                da_exp(h, 0)
                for e in range(2):
                    act.wait_ge(a_vtr.sem, a_vtr.at(h, e))
                    act.activation(v_hi[:, 4 * e:4 * e + 4, :].rearrange("p b v -> p (b v)"), PS[e][:, HALF:T], ACT.Copy)\
                       .then_inc(a_vh.sem, 1)
                if not first:
                    da_root(h - 1)
                da_z_half(h, 0, first)
                for i in range(KT):
                    if i + 1 < KT:
                        da_exp(h, i + 1)
                    if i == 4:
                        da_square(h, 0)
                    da_turned(h, i, 0)
                    if i == 0:
                        da_z_half(h, 1, first)
                    elif not last and i in (1, 2):
                        da_v_half(h + 1, i - 1)
                    elif not last and i in (4, 5):
                        da_q_half(h + 1, i - 4)
                    elif not last and i in (6, 7):
                        da_k_half(h + 1, i - 6)
                    if i >= 4:
                        da_turned(h, i, 1)
                    if i == 1 and not first:
                        da_high(h - 1)

            def da_exp(h, i):
                n = (i + 1) * P
                for c in range(2):
                    act.wait_ge(a_max.sem, a_max.at(h, 2 * i + c))
                    dst = p_0[i % 2] if c == 0 else p_1
                    act.activation(dst[:, 0:n], PS[c][:, 0:n], ACT.Exp, bias=stat[:, 4 * (i % 2) + c:4 * (i % 2) + c + 1],
                                   accum_out=stat2[:, 4 * (i % 2) + c:4 * (i % 2) + c + 1]).then_inc(a_exp.sem, 1)

            for e in range(2):
                da_v_half(0, e)
            for e in range(2):
                da_q_half(0, e, True)
            gate_rows()
            for e in range(2):
                da_k_half(0, e, True)
            da_head(0, first=True)
            with act.Fori(1, DA_HEADS - 1) as h:
                da_head(h)
            da_head(DA_HEADS - 1, last=True)
            da_square(DA_HEADS - 1, 1)
            da_root(DA_HEADS - 1)
            da_high(DA_HEADS - 1)

            def ml_qk(h, first=False):
                if not first:
                    act.wait_ge(m_yl.sem, m_yl.at(h - 1))
                n = IN_ML if first else IN_ML + 10 * h - 2
                act.wait_ge(in_mm.sem, in_mm.at(n))
                act.activation(xp[:, CONV - 1:], PS[0], ACT.Copy).then_inc(m_x.sem, 1)
                act.wait_ge(out_ev.sem, out_ev.at(OUT_ML + 2 * h - 1))
                act.dma_start(decay_t[:], gate_scr[0, bass.ds(h, 1), :].to_broadcast([P, T])).then_inc(m_ld.sem, 16)
                act.dma_start(iw_b[:], gate_scr[1, bass.ds(h, 1), :].to_broadcast([P, T])).then_inc(m_ld.sem, 16)
                for n in range(3):
                    act.dma_start(ml_cols[:, n, :], gate_scr[2 + n, bass.ds(h, 1), :].rearrange("a (c s) -> s (a c)", s=CHUNK),
                                  allow_slow_non_contiguous=True).then_inc(m_ld.sem, 16)
                act.wait_ge(m_conv.sem, m_conv.at(h, 3))
                act.activation(mt[:], mt[:], ACT.Silu).then_inc(m_silu.sem, 1)
                act.wait_ge(in_mm.sem, in_mm.at(n + 1))
                act.activation(xp[:, CONV - 1:], PS[1], ACT.Copy).then_inc(m_x.sem, 1)
                act.wait_ge(m_q.sem, m_q.at(h, 0))
                act.activation(mq_hi[:], mt[:], ACT.Copy).then_inc(m_qkh.sem, 1)
                act.wait_ge(m_q.sem, m_q.at(h, 1))
                act.activation(mi_hi[:], mt[:], ACT.Copy).then_inc(m_qkh.sem, 1)
                act.wait_ge(m_dt.sem, m_dt.at(h))
                act.activation(decay_t[:], decay_t[:], ACT.Exp, scale=-1.0).then_inc(m_de.sem, 1)
                act.wait_ge(m_conv.sem, m_conv.at(h, 7))
                act.activation(mt[:], mt[:], ACT.Silu).then_inc(m_silu.sem, 1)
                act.wait_ge(m_silu.sem, m_silu.at(h, 1))
                act.activation(mk_hi[:], mt[:], ACT.Copy).then_inc(m_qkh.sem, 1)

            def ml_gate(h, e):
                act.wait_ge(in_mm.sem, in_mm.at(IN_ML + 10 * h + (6 + e)))
                act.activation(ml_z[e][:], PS[e], ACT.Silu).then_inc(m_z.sem, 1)

            def ml_head(h):
                act.wait_ge(in_mm.sem, in_mm.at(IN_ML + 10 * h + 2))
                act.activation(v_t0[:], PS[0], ACT.Copy).then_inc(m_vt.sem, 1)
                act.wait_ge(m_kw.sem, m_kw.at(h))
                act.activation(kw_hi[:].rearrange("p c k -> p (c k)"), xp[:, 0:T], ACT.Copy).then_inc(m_kwh.sem, 1)
                act.wait_ge(in_mm.sem, in_mm.at(IN_ML + 10 * h + 3))
                act.wait_ge(m_qkl.sem, m_qkl.at(h, 2))
                act.wait_ge(m_ktr.sem, m_ktr.at(h))
                act.activation(mt[:], PS[1], ACT.Copy).then_inc(m_vt.sem, 1)
                for e in range(2):
                    act.wait_ge(m_vtr.sem, m_vtr.at(h, e))
                    act.activation(va_hi[:, :, e * P:(e + 1) * P], PS[e].rearrange("p (c v) -> p c v", v=P), ACT.Copy)\
                       .then_inc(m_vh.sem, 1)
                act.wait_ge(m_am.sem, m_am.at(h))
                act.activation(am_hi[:], decay_t[:], ACT.Copy).then_inc(m_ah.sem, 1)
                for c in range(NC - 1):
                    act.wait_ge(m_c.sem, m_c.at(h, c))
                    act.wait_ge(m_num.sem, m_num.at(h, c))
                    act.activation(c_hi[:], c_32[:], ACT.Copy).then_inc(m_ch.sem, 1)
                    if c == 4:
                        act.wait_ge(in_mm.sem, in_mm.at(IN_ML + 10 * h + 4))
                        act.activation(xp[:, 0:T], PS[0], ACT.Copy).then_inc(m_ot.sem, 1)
                act.wait_ge(in_mm.sem, in_mm.at(IN_ML + 10 * h + 5))
                act.activation(mt[:], PS[1], ACT.Copy).then_inc(m_ot.sem, 1)
                ml_gate(h, 0)
                for e in range(2):
                    act.wait_ge(m_otr.sem, m_otr.at(h, e))
                    act.activation(ml_so[:, :, e * P:(e + 1) * P], PS[2 + e].rearrange("p (c v) -> p c v", v=P), ACT.Sigmoid)\
                       .then_inc(m_so.sem, 1)
                act.wait_ge(m_g.sem, m_g.at(h))
                for c in range(NC):
                    act.activation(ml_so[:, c, :], hm[:, c, :], ACT.Square, accum_out=stat2[:, c:c + 1]).then_inc(m_ss.sem, 1)
                act.wait_ge(m_ss.sem, m_ss.at(h))
                act.activation(stat2[:, 8:16], stat2[:, 0:8], ACT.Sqrt, bias=eps[:, 0:1], scale=1.0 / ML_V).then_inc(m_std.sem, 1)
                ml_gate(h, 1)
                for e in range(2):
                    act.wait_ge(m_y.sem, m_y.at(h, 2 + e))
                    act.activation(my_hi[e][:], (xp[:, 0:T], mt[:])[e], ACT.Copy).then_inc(m_yh.sem, 1)

            ml_qk(0, first=True)
            with act.Fori(0, ML_HEADS - 1) as h:
                ml_head(h)
                ml_qk(h + 1)
            ml_head(ML_HEADS - 1)

            act.wait_ge(m_yl.sem, m_yl.at(ML_HEADS - 1))
            act.wait_ge(in_mm.sem, in_mm.at(IN_SV - 1))
            act.dma_start(resid[:], res_scr).then_inc(refill.sem, 16)
            square(3, acc, out_ev.sem, lambda k: out_ev.at(OUT_SG - 1, 2 * k + 1))
            square(4, resid, post_h.sem, lambda k: post_h.at(0, k))
            act.dma_start(res_scr, resid[:]).then_inc(spill.sem, 16)
            split_high(2)
            act.wait_ge(s_lo.sem, s_lo.at(2))
            act.wait_ge(spill.sem, spill.at(1))
            act.dma_start(wsp[:], w_spatial).then_inc(sp_ld.sem, 16)
            act.dma_start(bsp[:].rearrange("p g t -> p (g t)"), b_spatial.to_broadcast([P, SG_GROUPS * P])).then_inc(sp_ld.sem, 16)

            with act.Fori(0, SG_TILES // 2) as j:
                for s in range(2):
                    act.wait_ge(in_mm.sem, in_mm.at(IN_SV + 2 * j + s))
                    act.wait_ge(v_tr.sem, v_tr.at(2 * j + (s - 2)))
                    act.activation(g_t[s][:], PS[s], ACT.Gelu_apprx_tanh).then_inc(v_g.sem, 1)
                for s in range(2):
                    act.wait_ge(v_tok.sem, v_tok.at(2 * j + s))
                    act.dma_start(gv_scr[bass.ds(2 * j + s, 1)].rearrange("a p t -> p (a t)"),
                                  g_tok[s][:].rearrange("p c d -> p (c d)")).then_inc(v_st[s].sem, 16)
                    act.wait_ge(v_sq.sem, v_sq.at(2 * j + (s - 1)))
                    for c in range(NC):
                        act.activation(wr[:, c, :], g_tok[s][:, c, :], ACT.Square,
                                       accum_out=ssq[:, c, bass.ds(2 * j + s, 1)]).then_inc(v_sq.sem, 1)
            act.wait_ge(v_r.sem, 1)
            act.activation(stat2[:, 0:8], stat[:, 0:8], ACT.Sqrt, bias=eps[:, 0:1], scale=1.0 / (SG_TILES * P)).then_inc(v_r.sem, 1)

            def sg_weights(g):
                act.wait_ge(w_s.sem, w_s.at(g))
                act.wait_ge(in_mm.sem, in_mm.at(IN_SG + 4 * g - 1))
                act.activation(wr_hi[:], wr[:], ACT.Copy).then_inc(w_h.sem, 1)

            def sg_tile(d, e):
                act.wait_ge(in_mm.sem, in_mm.at(IN_SG + 2 * d))
                act.wait_ge(e_y.sem, e_y.at(d - 1))
                act.activation(sg_u[:], PS[0], ACT.Gelu_apprx_tanh).then_inc(e_u.sem, 1)
                act.wait_ge(in_mm.sem, in_mm.at(IN_SG + 2 * d + 1))
                act.activation(sg_z[:], PS[1], ACT.Silu).then_inc(e_z.sem, 1)
                act.wait_ge(e_y.sem, e_y.at(d))
                act.activation(sy_hi[e][:], sg_v[:], ACT.Copy).then_inc(e_yh.sem, 1)

            with act.Fori(0, SG_GROUPS) as g:
                sg_weights(g)
                for e in range(2):
                    sg_tile(2 * g + e, e)

            act.wait_ge(e_yl.sem, e_yl.at(SG_TILES - 1))
            act.wait_ge(in_mm.sem, in_mm.at(N_IN - 1))
            act.dma_start(resid[:], res_scr).then_inc(refill.sem, 16)
            square(5, acc, out_ev.sem, lambda k: out_ev.at(OUT_SG + SG_TILES - 1, 2 * k + 1))

        @block.vector
        def _(dve):
            for b in (out_ev, f_mul, f_lo, v_tok, w_s, w_l, e_v, e_y, e_yl):
                dve.sem_inc(b.sem, b.prime * b.per)

            dve.wait_ge(par_ld.sem, 16)
            dve.tensor_tensor(lam_prod[:], par[:, COL["lam_q"]:COL["lam_q"] + 2], par[:, COL["lam_k"]:COL["lam_k"] + 2],
                              ALU.mult).then_inc(lam_done.sem, 1)
            step = [0]

            def chained(ins):
                step[0] += 1
                ins.then_inc(px_step.sem, 1)
                dve.wait_ge(px_step.sem, step[0])

            SH1, SC1, G1, SH2, SC2, G2 = (slice(n * KT, (n + 1) * KT) for n in range(N_MOD))
            dve.wait_ge(small_ld.sem, 32)
            for k in range(KT):
                levels = k // 2 + 1
                w = 2 ** levels
                dve.wait_ge(px.sem, px.at(k))
                src, lo, hi = xpad[k % 2], 0, TP
                for n in range(levels):
                    back, ahead = (1, 0) if n == 0 else (2 ** (n - 1), 2 ** (n - 1))
                    lo, hi = lo + back, hi - ahead
                    ins = dve.tensor_tensor(tree[n][:, lo:hi], src[:, lo - back:hi - back], src[:, lo + ahead:hi + ahead], ALU.add)
                    if n == 0:
                        ins.then_inc(p_sum.sem, 1)
                        dve.wait_ge(p_sum.sem, p_sum.at(k))
                    else:
                        chained(ins)
                    src = tree[n]
                left, right = w // 2, w // 2 - 1
                e0 = w - 2
                chained(dve.tensor_tensor(src[:, PAD:PAD + left], src[:, PAD:PAD + left], edge[:, e0:e0 + left], ALU.mult))
                if right:
                    chained(dve.tensor_tensor(src[:, PAD + T - right:PAD + T], src[:, PAD + T - right:PAD + T],
                                              edge[:, e0 + left:e0 + left + right], ALU.mult))
                chained(dve.tensor_scalar(acc[:, k, :], src[:, PAD:PAD + T], 1.0 / w, None, ALU.mult))

            dve.wait_ge(mod_turn.sem, mod_turn.at(0))
            nb = COL["mod_b"]
            dve.tensor_tensor(mod[:, 0:24], PS[1][:, HALF:HALF + 24], par[:, nb:nb + 24], ALU.add).then_inc(mod_col.sem, 1)
            dve.wait_ge(mod_col.sem, 1)
            dve.tensor_scalar(sc1p[:], mod[:, SC1], 1.0, None, ALU.add).then_inc(sc1_done.sem, 1)
            dve.wait_ge(sc1_done.sem, 1)
            chained(dve.tensor_tensor(pool_gain[:], mod[:, G1], par[:, COL["pool_scale"]:COL["pool_scale"] + KT], ALU.mult))
            for k in range(KT):
                chained(dve.tensor_scalar(acc[:, k, :], acc[:, k, :], sc1p[:, k:k + 1], mod[:, k:k + 1], ALU.mult, ALU.add))
                dve.wait_ge(p_hx.sem, p_hx.at(k))
                dve.tensor_tensor(acc[:, k, :], acc[:, k, :], xpad[k % 2][:, PAD:PAD + T], ALU.subtract).then_inc(p_done.sem, 1)

            def modulation_rest():
                dve.wait_ge(mod_turn.sem, mod_turn.at(1))
                dve.tensor_tensor(mod[:, 24:48], PS[1][:, HALF:HALF + 24], par[:, nb + 24:nb + 48], ALU.add).then_inc(mod_col.sem, 1)
                dve.wait_ge(mod_col.sem, 2)
                chained(dve.tensor_scalar(sc2p[:], mod[:, SC2], 1.0, None, ALU.add))
                chained(dve.tensor_tensor(ffn_b0[:], ln_b0, sc2p[:], ALU.mult))
                chained(dve.tensor_tensor(ffn_b0[:], ffn_b0[:], mod[:, SH2], ALU.add))

            ln_b0 = par[:, COL["ln_b0"]:COL["ln_b0"] + KT]
            chained(dve.tensor_scalar(res_b0[:], ln_b0, ALPHA, None, ALU.mult))
            chained(dve.tensor_scalar(da_gain[:], par_col("da_g"), 1.0 - LAM_INIT, None, ALU.mult))
            dve.wait_ge(lam_x.sem, 1)
            chained(dve.scalar_tensor_tensor(neg_lam[:], lam_exp[:, 1:2], LAM_INIT, lam_exp[:, 0:1], ALU.subtract, ALU.subtract))
            for j in range(KT):
                dve.wait_ge(pool_mm.sem, j + 1)
                dve.wait_ge(x_scaled.sem, j + 1)
                dve.scalar_tensor_tensor(resid[:, j, :], PS[j % 2], pool_gain[:, j:j + 1], resid[:, j, :], ALU.mult, ALU.add)\
                   .then_inc(z_done.sem, 1)

            def center(norm, ready, value):
                dve.wait_ge(n_mean.sem, n_mean.at(norm))
                dve.wait_ge(ready, value)
                for k in range(KT):
                    dve.tensor_tensor(resid[:, k, :], resid[:, k, :], mean[:], ALU.subtract).then_inc(n_cent.sem, 1)

            def reciprocal(norm):
                dve.wait_ge(n_std.sem, n_std.at(norm))
                dve.reciprocal(rstd[:], std[:]).then_inc(n_rstd.sem, 1)
                dve.wait_ge(n_rstd.sem, n_rstd.at(norm))

            def split_low(use, k):
                dve.wait_ge(s_hi.sem, s_hi.at(use, k))
                dve.tensor_tensor(h_lo[:, k, :], tmp[k % 2][:], h_hi[:, k, :].bitcast(F32), ALU.subtract).then_inc(s_lo.sem, 1)

            center(0, z_done.sem, KT)
            reciprocal(0)
            modulation_rest()
            for k in range(KT):
                dve.scalar_tensor_tensor(resid[:, k, :], resid[:, k, :], par_col("ln_g0", k), rstd[:], ALU.mult, ALU.mult)\
                   .then_inc(n_out.sem, 1)
                if k >= 1:
                    split_low(0, k - 1)
            split_low(0, KT - 1)

            def add_out(n, o, gain=None, to=acc, done=c_mm):
                dve.wait_ge(out_ev.sem, out_ev.at(o - 1))
                for d in range(KT):
                    for e in range(2):
                        add_half(PS[2 + d % 2], n, o, d, e, gain, to, done)

            def add_half(src, n, o, d, e, gain=None, to=acc, done=c_mm):
                cols = slice(e * HALF, (e + 1) * HALF)
                if 2 * d + e < 2 * KT - 1:
                    dve.wait_ge(out_mm.sem, out_mm.at(o, 2 * d + e))
                else:
                    dve.wait_ge(done.sem, done.at(n))
                if gain is not None:
                    ins = dve.scalar_tensor_tensor(to[:, d, cols], src[:, cols], gain[:, d:d + 1], to[:, d, cols], ALU.mult, ALU.add)
                else:
                    ins = dve.tensor_tensor(to[:, d, cols], src[:, cols], to[:, d, cols], ALU.add)
                ins.then_inc(out_ev.sem, 1)

            def ffn(f):
                dve.wait_ge(in_mm.sem, in_mm.at(2 * f + 1))
                dve.wait_ge(f_silu.sem, f_silu.at(f))
                dve.wait_ge(f_lo.sem, f_lo.at(f - 1))
                dve.tensor_tensor(ffn_p[:], PS[1], ffn_g[:], ALU.mult).then_inc(f_mul.sem, 1)

            g2 = mod[:, G2]
            dve.wait_ge(n_res.sem, n_res.at(0))
            ffn(0)
            with dve.Fori(0, F_TILES // 2 - 1) as j:
                for b in range(2):
                    ffn(2 * j + (1 + b))
                    add_out(2 * j + b, 2 * j + b, g2, resid)
            ffn(F_TILES - 1)
            for b in range(2):
                add_out(IN_FFN_OUT + b, F_TILES - 2 + b, g2, resid, in_mm)

            center(1, out_ev.sem, out_ev.at(F_TILES - 1))
            reciprocal(1)
            for k in range(KT):
                dve.scalar_tensor_tensor(resid[:, k, :], resid[:, k, :], par_col("ln_g1", k), rstd[:], ALU.mult, ALU.mult)\
                   .then_inc(n_gain.sem, 1)
                dve.wait_ge(n_gain.sem, n_gain.at(0, k))
                dve.tensor_scalar(resid[:, k, :], resid[:, k, :], par_col("ln_b1", k), None, ALU.add).then_inc(n_out.sem, 1)

            def layer_input(norm, use, g_name):
                reciprocal(norm)
                for k in range(KT):
                    if k >= 2:
                        dve.wait_ge(s_lo.sem, s_lo.at(use, k - 2))
                    dve.scalar_tensor_tensor(tmp[k % 2][:], resid[:, k, :], par_col(g_name, k), rstd[:], ALU.mult, ALU.mult)\
                       .then_inc(s_tmp.sem, 1)
                    if k >= 1:
                        split_low(use, k - 1)
                split_low(use, KT - 1)

            layer_input(2, 1, "l0_pre_g")

            count = [0]

            def gate_step(ins):
                count[0] += 1
                ins.then_inc(g_dve.sem, 1)
                dve.wait_ge(g_dve.sem, count[0])

            dve.wait_ge(spill.sem, spill.at(0))
            dve.wait_ge(s_lo.sem, s_lo.at(1))
            gate_step(dve.memset(g_zero[:], 0.0))
            gate_step(dve.memset(g_m[:], 0.0))
            dve.wait_ge(g_act.sem, 3)
            gate_step(dve.scalar_tensor_tensor(g_lf[:], g_f[:], 0.0, g_a[:], ALU.min, ALU.subtract))
            for c in range(NC):
                gate_step(dve.tensor_tensor_scan(g_cum[:, c, :], g_lf[:, c, :], g_zero[:], 0.0, ALU.add, ALU.add))
            gate_step(dve.tensor_tensor(g_u[:], g_i[:], g_cum[:], ALU.subtract))
            for c in range(NC):
                gate_step(dve.tensor_tensor_scan(g_max[:, c, :], g_u[:, c, :], g_u[:, c, :], g_m[:, c:c + 1], ALU.max, ALU.max))
                gate_step(dve.tensor_tensor(g_m[:, c + 1:c + 2], g_cum[:, c, CHUNK - 1:CHUNK], g_max[:, c, CHUNK - 1:CHUNK], ALU.add))
            for c in range(NC):
                gate_step(dve.tensor_scalar(g_d[:, c, :], g_max[:, c, :], g_m[:, c:c + 1], None, ALU.subtract))
            gate_step(dve.tensor_tensor(g_d2[:], g_cum[:], g_max[:], ALU.add))
            for c in range(NC):
                gate_step(dve.tensor_scalar(g_d3[:, c, :], g_u[:, c, :], g_max[:, c, CHUNK - 1:CHUNK], None, ALU.subtract))
            assert count[0] == GATE_STEPS

            turn_bank = PS[2][:, 0:HALF]
            value_bank = PS[2][:, HALF:T]
            half_of = lambda e: slice(e * HALF, (e + 1) * HALF)

            def da_q_low(h, e):
                dve.wait_ge(a_qh.sem, a_qh.at(h, e))
                dve.scalar_tensor_tensor(q_lo[:, half_of(e)], PS[3][:, half_of(e)], DA_QK ** -0.5,
                                         q_hi[:, half_of(e)].bitcast(F32), ALU.mult, ALU.subtract).then_inc(a_ql.sem, 1)

            def da_k_low(h, e):
                dve.wait_ge(a_kh.sem, a_kh.at(h, e))
                dve.tensor_tensor(k_lo[:, half_of(e)], PS[3][:, half_of(e)], k_hi[:, half_of(e)].bitcast(F32), ALU.subtract)\
                   .then_inc(a_kl.sem, 1)

            def da_out_add(h, d):
                for e in range(2):
                    add_half(PS[3], C_DA + h, OUT_DA + h, d, e)

            def da_max(h, i):
                n = (i + 1) * P
                for c in range(2):
                    dve.wait_ge(a_score.sem, a_score.at(h, 2 * i + c))
                    dve.tensor_reduce(stat[:, 4 * (i % 2) + c:4 * (i % 2) + c + 1], PS[c][:, 0:n], AX_X, ALU.max, negate=True)\
                       .then_inc(a_max.sem, 1)

            def da_mix(h, i):
                n = (i + 1) * P
                st = 4 * (i % 2)
                dve.wait_ge(a_exp.sem, a_exp.at(h, 2 * i + 1))
                dve.reciprocal(stat2[:, st + 2:st + 4], stat2[:, st:st + 2]).then_inc(a_rec.sem, 1)
                dve.wait_ge(a_rec.sem, a_rec.at(h, i))
                dve.tensor_scalar(stat[:, st + 2:st + 3], stat2[:, st + 3:st + 4], neg_lam[:, 0:1], None, ALU.mult).then_inc(a_nr.sem, 1)
                dve.tensor_scalar(p_0[i % 2][:, 0:n], p_0[i % 2][:, 0:n], stat2[:, st + 2:st + 3], None, ALU.mult).then_inc(a_p0.sem, 1)
                dve.wait_ge(a_nr.sem, a_nr.at(h, i))
                dve.wait_ge(a_p0.sem, a_p0.at(h, i))
                dve.scalar_tensor_tensor(p_0[i % 2][:, 0:n], p_1[:, 0:n], stat[:, st + 2:st + 3], p_0[i % 2][:, 0:n],
                                         ALU.mult, ALU.add).then_inc(a_mix.sem, 1)

            def da_turn_low(h, i, part):
                blocks = slice(4 * part, min(4 * part + 4, i + 1))
                dve.wait_ge(a_hi_d.sem, a_hi_d.at(h, turn_event(i, part)))
                dve.tensor_tensor(a_lo[:, blocks, :].rearrange("p b q -> p (b q)"),
                                  turn_bank[:, 0:(blocks.stop - blocks.start) * P],
                                  a_hi[:, blocks, :].rearrange("p b q -> p (b q)").bitcast(F32), ALU.subtract).then_inc(a_lo_d.sem, 1)

            def da_gate(h, e):
                dve.wait_ge(a_pv.sem, a_pv.at(h, e))
                dve.wait_ge(a_z.sem, a_z.at(h, e))
                dve.tensor_tensor(da_o[:, half_of(e)], value_bank, da_z[:, half_of(e)], ALU.mult).then_inc(a_o.sem, 1)

            def da_norm(h, e):
                dve.wait_ge(a_std.sem, a_std.at(h))
                dve.reciprocal(da_sq[:, half_of(e)], da_sq[:, half_of(e)]).then_inc(a_r.sem, 1)

            def da_result(h):
                dve.wait_ge(a_r.sem, a_r.at(h))
                dve.scalar_tensor_tensor(da_o[:], da_o[:], da_gain[:, 0:1], da_sq[:], ALU.mult, ALU.mult).then_inc(a_y.sem, 1)
                dve.wait_ge(a_yh.sem, a_yh.at(h))
                dve.tensor_tensor(y_lo[:], da_o[:], y_hi[:].bitcast(F32), ALU.subtract).then_inc(a_yl.sem, 1)

            def da_head(h, first=False, last=False):
                out = not first
                if out:
                    da_gate(h - 1, 1)
                da_max(h, 0)
                for e in range(2):
                    dve.wait_ge(a_vh.sem, a_vh.at(h, e))
                    dve.tensor_tensor(v_lo[:, 4 * e:4 * e + 4, :].rearrange("p b v -> p (b v)"), PS[e][:, HALF:T],
                                      v_hi[:, 4 * e:4 * e + 4, :].rearrange("p b v -> p (b v)").bitcast(F32), ALU.subtract)\
                       .then_inc(a_vl.sem, 1)
                da_mix(h, 0)
                for i in range(KT):
                    if i + 1 < KT:
                        da_max(h, i + 1)
                    if i == 4:
                        da_gate(h, 0)
                    if out:
                        for d in ((), (), (0,), (1,), (4,), (5,), (6,), (7,))[i]:
                            da_out_add(h - 1, d)
                        if i < 2:
                            da_norm(h - 1, i)
                    da_turn_low(h, i, 0)
                    if i + 1 < KT:
                        da_mix(h, i + 1)
                    if out and i == 1:
                        da_result(h - 1)
                    if out and i == 3:
                        for d in (2, 3):
                            da_out_add(h - 1, d)
                    if not last and i in (4, 5):
                        da_q_low(h + 1, i - 4)
                    if not last and i in (6, 7):
                        da_k_low(h + 1, i - 6)
                    if i >= 4:
                        da_turn_low(h, i, 1)

            for e in range(2):
                da_q_low(0, e)
            for e in range(2):
                da_k_low(0, e)
            da_head(0, first=True)
            dve.wait_ge(acc_zero.sem, 1)
            with dve.Fori(1, DA_HEADS - 1) as h:
                da_head(h)
            da_head(DA_HEADS - 1, last=True)
            da_gate(DA_HEADS - 1, 1)
            for e in range(2):
                da_norm(DA_HEADS - 1, e)
            da_result(DA_HEADS - 1)
            add_out(C_DA + DA_HEADS - 1, OUT_DA + DA_HEADS - 1)

            def conv(h, which, event):
                col = lambda j: par[:, bass.ds(h + (COL["conv_w"] + 8 * j + 4 * which), 1)]
                dve.tensor_scalar(mt[:], xp[:, 0:T], col(0), par[:, bass.ds(h + (COL["conv_b"] + 4 * which), 1)], ALU.mult, ALU.add)\
                   .then_inc(m_conv.sem, 1)
                for j in range(1, CONV):
                    dve.wait_ge(m_conv.sem, m_conv.at(h, event + j - 1))
                    dve.scalar_tensor_tensor(mt[:], xp[:, j:j + T], col(j), mt[:], ALU.mult, ALU.add).then_inc(m_conv.sem, 1)

            def ml_qk(h):
                dve.wait_ge(out_ev.sem, out_ev.at(OUT_ML + 2 * h - 1))
                dve.memset(xp[:, 0:CONV - 1], 0.0).then_inc(m_vl.sem, 1)
                dve.memset(va_hi[:, :, ML_V:ML_V + 1].bitcast(F32), 1.0).then_inc(m_vl.sem, 1)
                dve.memset(va_hi[:, :, ML_V + 1:VA].bitcast(F32), 0.0).then_inc(m_vl.sem, 1)
                dve.memset(va_lo[:, :, ML_V:VA].bitcast(F32), 0.0).then_inc(m_vl.sem, 1)
                dve.wait_ge(m_vl.sem, m_vl.at(h, 0))
                dve.wait_ge(m_x.sem, m_x.at(h, 0))
                conv(h, 0, 0)
                dve.wait_ge(m_silu.sem, m_silu.at(h, 0))
                dve.tensor_scalar(mt[:], mt[:], ML_QK ** -0.5, None, ALU.mult).then_inc(m_q.sem, 1)
                dve.wait_ge(m_qkh.sem, m_qkh.at(h, 0))
                dve.tensor_tensor(mq_lo[:], mt[:], mq_hi[:].bitcast(F32), ALU.subtract).then_inc(m_qkl.sem, 1)
                dve.wait_ge(m_ld.sem, m_ld.at(h))
                dve.wait_ge(m_qkl.sem, m_qkl.at(h, 0))
                dve.tensor_tensor(mt[:], mt[:], iw_b[:], ALU.mult).then_inc(m_q.sem, 1)
                for c in range(NC):
                    cols = slice(c * CHUNK, (c + 1) * CHUNK)
                    dve.tensor_scalar(decay_t[:, cols], decay_t[:, cols], ml_cols[:, 0, c:c + 1], 0.0, ALU.subtract, ALU.max)\
                       .then_inc(m_dt.sem, 1)
                dve.tensor_copy(stat[:, 8:16], iw_b[:, CHUNK - 1:T:CHUNK]).then_inc(m_den.sem, 1)
                dve.wait_ge(m_qkh.sem, m_qkh.at(h, 1))
                dve.tensor_tensor(mi_lo[:], mt[:], mi_hi[:].bitcast(F32), ALU.subtract).then_inc(m_qkl.sem, 1)
                dve.wait_ge(m_x.sem, m_x.at(h, 1))
                dve.wait_ge(m_qkl.sem, m_qkl.at(h, 1))
                conv(h, 1, 4)
                dve.wait_ge(m_qkh.sem, m_qkh.at(h, 2))
                dve.tensor_tensor(mk_lo[:], mt[:], mk_hi[:].bitcast(F32), ALU.subtract).then_inc(m_qkl.sem, 1)

            def ml_head(h, last=False):
                dve.wait_ge(m_ktr.sem, m_ktr.at(h))
                for c in range(NC):
                    cols = slice(c * CHUNK, (c + 1) * CHUNK)
                    dve.tensor_scalar(xp[:, cols], PS[2][:, cols], ml_cols[:, 1, c:c + 1], None, ALU.mult).then_inc(m_kw.sem, 1)
                dve.wait_ge(m_kwh.sem, m_kwh.at(h))
                dve.tensor_tensor(kw_lo[:].rearrange("p c k -> p (c k)"), xp[:, 0:T],
                                  kw_hi[:].rearrange("p c k -> p (c k)").bitcast(F32), ALU.subtract).then_inc(m_kwl.sem, 1)
                dve.wait_ge(m_s.sem, m_s.at(h))
                dve.wait_ge(m_mask.sem, m_mask.at(h))
                dve.tensor_tensor(decay_t[:], PS[3], decay_t[:], ALU.mult).then_inc(m_am.sem, 1)
                for e in range(2):
                    dve.wait_ge(m_vh.sem, m_vh.at(h, e))
                    dve.tensor_tensor(va_lo[:, :, e * P:(e + 1) * P], PS[e].rearrange("p (c v) -> p c v", v=P),
                                      va_hi[:, :, e * P:(e + 1) * P].bitcast(F32), ALU.subtract).then_inc(m_vl.sem, 1)
                dve.wait_ge(m_ah.sem, m_ah.at(h))
                dve.tensor_tensor(am_lo[:], decay_t[:], am_hi[:].bitcast(F32), ALU.subtract).then_inc(m_al.sem, 1)
                for c in range(NC):
                    if c < NC - 1:
                        part = PS[3][:, (c % 2) * HALF:(c % 2) * HALF + VA]
                        dve.wait_ge(m_p.sem, m_p.at(h, c))
                        if c == 0:
                            dve.tensor_copy(c_32[:], part).then_inc(m_c.sem, 1)
                        else:
                            dve.wait_ge(m_cl.sem, m_cl.at(h, c - 1))
                            dve.scalar_tensor_tensor(c_32[:], c_32[:], stat[:, 8 + c:9 + c], part, ALU.mult, ALU.add).then_inc(m_c.sem, 1)
                        dve.wait_ge(m_ch.sem, m_ch.at(h, c))
                        dve.tensor_tensor(c_lo[:], c_32[:], c_hi[:].bitcast(F32), ALU.subtract).then_inc(m_cl.sem, 1)
                    num = PS[2][:, (c % 2) * HALF:(c % 2) * HALF + VA]
                    dve.wait_ge(m_num.sem, m_num.at(h, c))
                    den = num[:, ML_V:ML_V + 1]
                    dve.tensor_scalar(stat[:, 2:3], den, -1.0, ml_cols[:, 2, c:c + 1], ALU.mult, ALU.max).then_inc(m_den.sem, 1)
                    dve.wait_ge(m_den.sem, m_den.at(h, 1 + 2 * c))
                    dve.tensor_tensor(stat[:, 0:1], den, stat[:, 2:3], ALU.max).then_inc(m_den.sem, 1)
                    dve.wait_ge(m_den.sem, m_den.at(h, 2 + 2 * c))
                    dve.reciprocal(stat[:, 1:2], stat[:, 0:1]).then_inc(m_rd.sem, 1)
                    dve.wait_ge(m_rd.sem, m_rd.at(h, c))
                    dve.tensor_scalar(hm[:, c, :], num[:, 0:ML_V], stat[:, 1:2], None, ALU.mult).then_inc(m_hm.sem, 1)
                dve.wait_ge(m_so.sem, m_so.at(h))
                dve.wait_ge(m_hm.sem, m_hm.at(h))
                dve.tensor_tensor(hm[:], hm[:], ml_so[:], ALU.mult).then_inc(m_g.sem, 1)
                dve.wait_ge(m_std.sem, m_std.at(h))
                dve.reciprocal(stat[:, 0:8], stat2[:, 8:16]).then_inc(m_r.sem, 1)
                dve.wait_ge(m_r.sem, m_r.at(h))
                for c in range(NC):
                    dve.tensor_scalar(hm[:, c, :], hm[:, c, :], stat[:, c:c + 1], None, ALU.mult).then_inc(m_n.sem, 1)
                for e in range(2):
                    dst = (xp[:, 0:T], mt[:])[e]
                    dve.wait_ge(m_ntr.sem, m_ntr.at(h, e))
                    dve.tensor_scalar(dst, PS[2 + e], par_col("ml_g", e), None, ALU.mult).then_inc(m_y.sem, 1)
                for e in range(2):
                    dst = (xp[:, 0:T], mt[:])[e]
                    dve.wait_ge(m_y.sem, m_y.at(h, e))
                    dve.wait_ge(m_z.sem, m_z.at(h, e))
                    dve.tensor_tensor(dst, dst, ml_z[e][:], ALU.mult).then_inc(m_y.sem, 1)
                for e in range(2):
                    dve.wait_ge(m_yh.sem, m_yh.at(h, e))
                    dve.tensor_tensor(my_lo[e][:], (xp[:, 0:T], mt[:])[e], my_hi[e][:].bitcast(F32), ALU.subtract).then_inc(m_yl.sem, 1)
                for e in range(2):
                    add_out(IN_ML + 10 * h + ((8 if last else 10) + e), OUT_ML + 2 * h + e, done=in_mm)

            ml_qk(0)
            with dve.Fori(0, ML_HEADS - 1) as h:
                ml_head(h)
                ml_qk(h + 1)
            ml_head(ML_HEADS - 1, last=True)

            def layer_output(norm, use, g_name):
                reciprocal(norm)
                dve.wait_ge(refill.sem, refill.at(use))
                for k in range(KT):
                    dve.scalar_tensor_tensor(acc[:, k, :], acc[:, k, :], par_col(g_name, k), rstd[:], ALU.mult, ALU.mult)\
                       .then_inc(post_t.sem, 1)
                    if k >= 1:
                        residual(use, k - 1)
                residual(use, KT - 1)

            def residual(use, k):
                dve.wait_ge(post_t.sem, post_t.at(use, k))
                dve.tensor_tensor(resid[:, k, :], resid[:, k, :], acc[:, k, :], ALU.add).then_inc(post_h.sem, 1)

            layer_output(3, 0, "l0_post_g")
            layer_input(4, 2, "l1_pre_g")

            dve.wait_ge(sp_ld.sem, sp_ld.at(0))
            dve.wait_ge(acc_zero.sem, 2)
            with dve.Fori(0, SG_TILES // 2) as j:
                for s in range(2):
                    dve.wait_ge(v_tr.sem, v_tr.at(2 * j + s))
                    dve.wait_ge(v_st[s].sem, v_st[s].at(j - 1))
                    dve.wait_ge(v_sq.sem, v_sq.at(2 * j + (s - 2)))
                    dve.tensor_copy(g_tok[s][:].rearrange("p c d -> p (c d)"), PS[2 + s]).then_inc(v_tok.sem, 1)
            dve.wait_ge(v_sq.sem, v_sq.at(SG_TILES - 1))
            dve.tensor_reduce(stat[:, 0:8], ssq[:], AX_X, ALU.add).then_inc(v_r.sem, 1)
            dve.wait_ge(v_r.sem, 2)
            dve.reciprocal(stat[:, 8:16], stat2[:, 0:8]).then_inc(v_r.sem, 1)
            dve.wait_ge(v_r.sem, 3)
            dve.wait_ge(const.sem, 14)

            def sg_weights(g):
                dve.wait_ge(w_l.sem, w_l.at(g - 1))
                for c in range(NC):
                    dve.tensor_scalar(wr[:, c, :], wsp[:, bass.ds(g, 1), :].rearrange("p a t -> p (a t)"), stat[:, 8 + c:9 + c],
                                      None, ALU.mult).then_inc(w_s.sem, 1)
                dve.wait_ge(w_h.sem, w_h.at(g))
                dve.tensor_tensor(wr_lo[:], wr[:], wr_hi[:].bitcast(F32), ALU.subtract).then_inc(w_l.sem, 1)

            def sg_tile(d, g, n):
                dve.wait_ge(c_mm.sem, c_mm.at(n))
                dve.wait_ge(e_yl.sem, e_yl.at(d - 1))
                dve.scalar_tensor_tensor(sg_v[:].rearrange("p (c t) -> p c t", t=P), PS[2].rearrange("p (c t) -> p c t", t=P),
                                         par[:, bass.ds(d + COL["sg_g"], 1)],
                                         bsp[:, bass.ds(g, 1), :].to_broadcast([P, NC, P]), ALU.mult, ALU.add).then_inc(e_v.sem, 1)
                dve.wait_ge(e_v.sem, e_v.at(d))
                dve.wait_ge(e_u.sem, e_u.at(d))
                dve.tensor_tensor(sg_v[:], sg_v[:], sg_u[:], ALU.mult).then_inc(e_y.sem, 1)
                dve.wait_ge(e_y.sem, e_y.at(d, 0))
                dve.wait_ge(e_z.sem, e_z.at(d))
                dve.tensor_tensor(sg_v[:], sg_v[:], sg_z[:], ALU.mult).then_inc(e_y.sem, 1)

            sg_weights(0)
            sg_tile(0, 0, C_SG)
            sg_tile(1, 0, C_SG + 1)
            add_out(C_SG + 2, OUT_SG)
            with dve.Fori(1, SG_GROUPS - 1) as g:
                sg_weights(g)
                for e in range(2):
                    sg_tile(2 * g + e, g, C_SG + 4 * g + (2 * e - 1))
                    add_out(C_SG + 4 * g + 2 * e, OUT_SG + 2 * g + (e - 1))
            sg_weights(SG_GROUPS - 1)
            sg_tile(SG_TILES - 2, SG_GROUPS - 1, C_SG + 2 * SG_TILES - 5)
            add_out(C_SG + 2 * SG_TILES - 4, OUT_SG + SG_TILES - 3)
            sg_tile(SG_TILES - 1, SG_GROUPS - 1, C_SG + 2 * SG_TILES - 3)
            for b in range(2):
                add_out(IN_SG_OUT + b, OUT_SG + SG_TILES - 2 + b, done=in_mm)
            layer_output(5, 1, "l1_post_g")


def columns(v):
    return np.asarray(v).reshape(-1, P).T


def in_slab(w, cols):
    return np.asarray(w)[:, cols:cols + P].reshape(KT, P, P).transpose(1, 0, 2).reshape(P, T)


def kernel(**inputs):
    import concourse.bacc as bacc
    from concourse.bass_utils import run_bass_kernel_spmd

    a = {k: np.asarray(v) for k, v in inputs.items()}
    f32 = np.float32
    par = np.zeros((P, N_PAR), f32)

    def put(name, cols):
        par[:cols.shape[0], COL[name]:COL[name] + cols.shape[1]] = cols

    put("c", columns(a["c"][0]))
    put("mod_b", columns(a["mod_b"][0]))
    for n in range(2):
        put(f"ln_g{n}", columns(a["ln_g"][0, n]))
        put(f"ln_b{n}", columns(a["ln_b"][0, n]))
    put("pool_scale", columns(a["pool_scale"][0]))
    put("l0_pre_g", columns(a["l0_pre_g_2"]))
    put("l0_post_g", columns(a["l0_post_g_2"]))
    put("l1_pre_g", columns(a["l1_pre_g_2"]))
    put("l1_post_g", columns(a["l1_post_g_2"]))
    put("conv_w", columns(a["l0_conv_w_2"]))
    put("conv_b", columns(a["l0_conv_b_2"]))
    put("da_g", columns(a["l0_da_head_g_2"]))
    put("ml_g", columns(a["l0_ml_head_g_2"]))
    put("sg_g", columns(a["l1_sg_norm_g_2"]))
    par[0:ML_HEADS, COL["gate_b"]] = a["l0_b_igate_2"]
    par[32:32 + ML_HEADS, COL["gate_b"]] = a["l0_b_fgate_2"]
    put("lam_q", np.stack([a["l0_lambda_q1_2"], a["l0_lambda_q2_2"]], 1))
    put("lam_k", np.stack([a["l0_lambda_k1_2"], a["l0_lambda_k2_2"]], 1))

    edges = np.ones((P, 32), f32)
    for w in (2, 4, 8, 16):
        counts = [t + w // 2 for t in range(w // 2)] + [w - 1 - r for r in range(w // 2 - 1)]
        edges[:, w - 2:w - 2 + len(counts)] = np.array([w / n for n in counts], f32)

    ffn_in, w0, w1 = a["ffn_w_in"][0], a["l0_w_in_2"], a["l1_w_in_2"]
    hidden = F_TILES * P
    w_in = np.empty((N_IN, P, T), f32)
    for f in range(F_TILES):
        w_in[2 * f] = in_slab(ffn_in, f * P)
        w_in[2 * f + 1] = in_slab(ffn_in, hidden + f * P)
    da, qk = DA_HEADS * DA_V, ML_HEADS * ML_QK
    ml_qk = 4 * da
    ml_v = ml_qk + 2 * qk
    ml_i = ml_v + ML_HEADS * ML_V
    ml_o = ml_i + 2 * ML_HEADS
    ml_z = ml_o + ML_HEADS * ML_V
    for h in range(DA_HEADS):
        for s in range(4):
            w_in[IN_DA + 4 * h + s] = in_slab(w0, (2, 0, 1, 3)[s] * da + h * P)
    w_out = a["l0_w_out_2"].reshape(-1, P, D)
    ml_order = []
    for h in range(ML_HEADS):
        qk_of = lambda n: [in_slab(w0, ml_qk + e * qk + n * ML_QK) for e in range(2)]
        ml_order += qk_of(0) if h == 0 else []
        ml_order += [in_slab(w0, first + h * ML_V + e * P) for first in (ml_v, ml_o, ml_z) for e in range(2)]
        ml_order += qk_of(h + 1) if h + 1 < ML_HEADS else []
        ml_order += [w_out[DA_HEADS + 2 * h + e] for e in range(2)]
    for n, slab in enumerate(ml_order):
        w_in[IN_ML + n] = slab
    width = SG_TILES * P
    for d in range(SG_TILES):
        w_in[IN_SV + d] = in_slab(w1, width + d * P)
        w_in[IN_SG + 2 * d] = in_slab(w1, d * P)
        w_in[IN_SG + 2 * d + 1] = in_slab(w1, 2 * width + d * P)
    w_c = np.zeros((N_C_DRAM, P, T), f32)
    ffn_out = a["ffn_w_out"][0].reshape(F_TILES, P, D)
    sg_out = a["l1_w_out_2"].reshape(SG_TILES, P, D)
    w_c[0:C_GATES], w_in[IN_FFN_OUT:IN_DA] = ffn_out[:-2], ffn_out[-2:]
    w_c[C_SG:], w_in[IN_SG_OUT:] = sg_out[:-2], sg_out[-2:]
    gates = w_c[C_GATES].reshape(P, KT, P)
    gates[:, :, 0:ML_HEADS] = w0[:, ml_i:ml_i + ML_HEADS].reshape(KT, P, ML_HEADS).transpose(1, 0, 2)
    gates[:, :, 32:32 + ML_HEADS] = w0[:, ml_i + ML_HEADS:ml_o].reshape(KT, P, ML_HEADS).transpose(1, 0, 2)
    w_c[C_DA:C_SG] = w_out[:DA_HEADS]

    mod_w = a["mod_w"][0].reshape(KT, P, N_MOD * D // HALF, HALF).transpose(2, 1, 0, 3)
    arrays = {
        "x_t": a["x"][0].T.reshape(KT, P, T).transpose(1, 0, 2),
        "params": par,
        "mod_w": mod_w,
        "pool_w": a["pool_w"][0].reshape(4, 2, P, 256).transpose(2, 0, 1, 3),
        "w_in": w_in,
        "w_c": w_c,
        "edges": edges,
        "w_spatial": a["l1_w_spatial_2"].transpose(2, 0, 1),
        "b_spatial": a["l1_b_spatial_2"].reshape(1, SG_GROUPS * P),
    }
    arrays = {k: np.ascontiguousarray(v) for k, v in arrays.items()}
    nc = bacc.Bacc("TRN2", target_bir_lowering=False, num_devices=1)
    args = {k: nc.dram_tensor(k, v.shape, F32, kind="ExternalInput").ap() for k, v in arrays.items()}
    out = nc.dram_tensor("out", (P, KT, T), F32, kind="ExternalOutput").ap()
    build(nc, out=out, **args)
    result = run_bass_kernel_spmd(nc, [arrays], core_ids=[0]).results[0]["out"]
    return result.transpose(2, 1, 0).reshape(1, T, D)
```

```python
import math
from contextlib import ExitStack

import numpy as np

import concourse.bass as bass
from concourse import mybir

F32 = mybir.dt.float32
F32R = mybir.dt.float32r
BF16 = mybir.dt.bfloat16
ALU = mybir.AluOpType
ACT = mybir.ActivationFunctionType
AX_X = mybir.AxisListType.X

P = 128
T = 1024
HALF = 512
D = 1024
KT = D // P
F_TILES = 2816 // P
N_MOD = 6
DA_HEADS, DA_QK, DA_V = 8, 64, 128
ML_HEADS, ML_QK, ML_V, CHUNK, CONV = 4, 128, 256, 128, 4
VA = ML_V + 2
SG_TILES, SG_GROUPS = 16, 8
NC = T // CHUNK
ALPHA = 2.0 ** 0.25
EPS = 1e-6
LAM_INIT = 0.8 - 0.6 * math.exp(0.0)
MASKED = -1e30

PARAMS = [("c", 8), ("mod_b", 48), ("ln_g0", 8), ("ln_b0", 8), ("ln_g1", 8), ("ln_b1", 8),
          ("pool_scale", 8), ("l0_pre_g", 8), ("l0_post_g", 8), ("l1_pre_g", 8), ("l1_post_g", 8),
          ("conv_w", 32), ("conv_b", 8), ("da_g", 1), ("ml_g", 2), ("sg_g", 16), ("gate_b", 1),
          ("lam_q", 2), ("lam_k", 2)]
COL, N_PAR = {}, 0
for _name, _n in PARAMS:
    COL[_name] = N_PAR
    N_PAR += _n

IN_FFN_OUT = 2 * F_TILES
IN_DA = IN_FFN_OUT + 2
DA_V_SLAB, DA_Q_SLAB, DA_K_SLAB, DA_Z_SLAB = range(4)
IN_ML = IN_DA + 4 * DA_HEADS
IN_SV = IN_ML + 10 * ML_HEADS
IN_SG = IN_SV + SG_TILES
IN_SG_OUT = IN_SG + 2 * SG_TILES
N_IN = IN_SG_OUT + 2
C_GATES = F_TILES - 2
C_DA = C_GATES + 1
C_SG = C_DA + DA_HEADS
N_C_DRAM = C_SG + SG_TILES - 2
OUT_DA = F_TILES
OUT_ML = OUT_DA + DA_HEADS
OUT_SG = OUT_ML + 2 * ML_HEADS
GATE_STEPS = 4 + 3 * NC


DA_TILES = {3: (0, 1), 4: (2, 3), 5: (4, 5), 6: (6,), 7: (7,)}


def da_halves(d):
    step = next(i for i in DA_TILES if d in DA_TILES[i])
    return (1, 0) if step in (5, 7) else (0, 1)


def half_of(e):
    return slice(e * HALF, (e + 1) * HALF)


def da_blocks(tile, e, odd):
    return tile[:, half_of(e)].rearrange("p (a s q) -> p a s q", s=2, q=P)[:, :, odd, :]


def turned_slots(i, part):
    lo, hi = 4 * part, min(4 * part + 4, i + 1)
    return slice(2 * lo + (i + 1) % 2, 2 * hi - i % 2, 2), hi - lo


def turn_event(i, part):
    return i if i < 4 else 4 + 2 * (i - 4) + part


class Beat:

    def __init__(self, sem, per=1, prime=0):
        self.sem, self.per, self.prime = sem, per, prime

    def at(self, turn, event=None):
        event = self.per - 1 if event is None else event
        return turn * self.per + (self.prime * self.per + event + 1)


def build(nc, x_t, params, mod_w, pool_w, w_in, w_c, edges, w_spatial, b_spatial, out):
    with ExitStack() as ctx:
        base = (nc.sbuf_base + 63) // 64 * 64
        place = [base]

        def at_offset(name, shape, dtype, offset):
            return nc.alloc_sbuf_tensor_at(name, shape, dtype, offset=offset)

        def fixed(name, shape, dtype=F32):
            size = int(np.prod(shape[1:])) * (2 if dtype == BF16 else 4)
            tile = at_offset(name, shape, dtype, place[0])
            place[0] += (size + 31) // 32 * 32
            return tile

        raw = [fixed(f"slab_raw{s}", [P, T]) for s in range(3)]
        whi = [fixed(f"slab_hi{s}", [P, KT, P], F32R) for s in range(3)]
        wlo = [fixed(f"slab_lo{s}", [P, KT, P], F32R) for s in range(3)]
        C = 2
        h_base = place[0]
        h_hi = fixed("h_hi", [P, KT, T], F32R)
        h_lo = fixed("h_lo", [P, KT, T], F32R)
        acc_base = place[0]
        acc = fixed("acc", [P, KT, T])
        ident = fixed("ident", [P, P])
        ones = fixed("ones", [P, P])
        ident_b = fixed("ident_b", [P, P], BF16)
        mask_b = fixed("mask_b", [P, P], BF16)
        causal = fixed("causal", [P, P])
        zero = fixed("zero", [P, 1])
        eps = fixed("eps", [P, 1])
        par = fixed("par", [P, N_PAR])
        mod = fixed("mod", [P, N_MOD * KT])
        silu_c = fixed("silu_c", [P, KT])
        sc1p = fixed("sc1p", [P, KT])
        sc2p = fixed("sc2p", [P, KT])
        pool_gain = fixed("pool_gain", [P, KT])
        res_b0 = fixed("res_b0", [P, KT])
        ffn_b0 = fixed("ffn_b0", [P, KT])
        lam_prod = fixed("lam_prod", [P, 2])
        lam_exp = fixed("lam_exp", [P, 2])
        neg_lam = fixed("neg_lam", [P, 1])
        da_gain = fixed("da_gain", [P, 1])
        stat = fixed("stat", [P, 16])
        stat2 = fixed("stat2", [P, 16])
        ml_cols = fixed("ml_cols", [P, 3, NC])
        ssq = fixed("ssq", [P, NC, SG_TILES])
        resid_base = place[0]
        resid = fixed("resid", [P, KT, T])
        work_base = place[0]
        top = nc.sbuf_usable_end

        def overlay(start):
            cursor = [start]

            def take(name, shape, dtype=F32, at=None):
                size = int(np.prod(shape[1:])) * (2 if dtype == BF16 else 4)
                offset = cursor[0] if at is None else at
                if at is None:
                    cursor[0] += (size + 31) // 32 * 32
                assert offset + size <= top, (name, offset + size - top)
                tile = at_offset(name, shape, dtype, offset)
                return tile, offset
            return take

        def par_col(name, k=0):
            return par[:, COL[name] + k:COL[name] + k + 1]

        MOD_BLOCKS, MOD_BUFFERS = N_MOD * D // HALF, 3
        MOD_HALF = MOD_BLOCKS // 2
        X_AFTER = (1, 3)
        mod_big = [at_offset(f"mod_big{b}", [P, KT, HALF], F32, h_base + b * KT * HALF * 4) for b in range(MOD_BUFFERS)]
        pair = [at_offset(f"pair{b}", [P, T], F32, h_base + b * T * 4) for b in range(KT // 2)]
        mod_row = at_offset("mod_row", [1, MOD_HALF, HALF], F32, h_base + MOD_BUFFERS * KT * HALF * 4)
        take = overlay(work_base)
        PAD = 8
        TP = T + 2 * PAD
        xpad = [take(f"xpad{b}", [P, TP])[0] for b in range(2)]
        tree = [take(f"tree{n}", [P, TP])[0] for n in range(4)]
        pw = take("pw", [P, 4, 2, 256])[0]
        edge = take("edge", [P, 32])[0]
        take = overlay(work_base)
        sq = [take(f"sq{b}", [P, HALF])[0] for b in range(4)]
        mean = take("mean", [P, T])[0]
        rstd = take("rstd", [P, T])[0]
        std = take("std", [P, T])[0]
        tmp = [take(f"tmp{b}", [P, T])[0] for b in range(2)]
        take = overlay(work_base)
        ffn_g = take("ffn_g", [P, T])[0]
        ffn_p = take("ffn_p", [P, T])[0]
        ffn_hi = [take(f"ffn_hi{b}", [P, T], F32R)[0] for b in range(2)]
        ffn_lo = [take(f"ffn_lo{b}", [P, T], F32R)[0] for b in range(2)]
        take = overlay(acc_base)
        g_i, g_f, g_a, g_cum, g_u, g_max, g_d = (
            take(f"gate_{n}", [ML_HEADS, NC, CHUNK])[0] for n in ("i", "f", "log", "cum", "u", "max", "d"))
        g_zero = take("gate_zero", [ML_HEADS, CHUNK])[0]
        g_m = take("gate_m", [ML_HEADS, NC + 1])[0]
        g_lf, g_d2, g_d3 = g_a, g_f, g_i
        take = overlay(resid_base)
        q_hi, q_lo, k_hi, k_lo = (take(f"da_{n}", [P, T], F32R)[0] for n in ("qh", "ql", "kh", "kl"))
        v_t = take("da_vt", [P, T])[0]
        v_hi, v_lo = (take(f"da_{n}", [P, KT, P], F32R)[0] for n in ("vh", "vl"))
        da_z = take("da_z", [P, T])[0]
        p_0 = [take(f"da_p0{b}", [P, T])[0] for b in range(2)]
        a_hi, a_lo = (take(f"da_{n}", [P, 2 * KT - 1, P], F32R)[0] for n in ("ah", "al"))
        da_o = take("da_o", [P, T])[0]
        da_sq = take("da_sq", [P, T])[0]
        y_hi, y_lo = (take(f"da_{n}", [P, T], F32R)[0] for n in ("yh", "yl"))
        take = overlay(resid_base)
        xp = take("ml_xp", [P, CONV - 1 + T])[0]
        mt = take("ml_t", [P, T])[0]
        (mq_hi, o_q), (mq_lo, _) = (take(f"ml_{n}", [P, T], F32R) for n in ("qh", "ql"))
        (mi_hi, o_i), (mi_lo, _) = (take(f"ml_{n}", [P, T], F32R) for n in ("ih", "il"))
        (mk_hi, o_k), (mk_lo, _) = (take(f"ml_{n}", [P, T], F32R) for n in ("kh", "kl"))
        (kw_hi, o_w), (kw_lo, _) = (take(f"ml_{n}", [P, NC, P], F32R) for n in ("wh", "wl"))
        (va_hi, o_v), (va_lo, _) = (take(f"ml_{n}", [P, NC, VA], F32R) for n in ("vh", "vl"))
        decay_t = take("ml_dt", [P, T])[0]
        hm, o_hm = take("ml_hm", [P, NC, ML_V])
        c_32 = take("ml_c", [P, VA])[0]
        c_hi, c_lo = (take(f"ml_{n}", [P, VA], F32R)[0] for n in ("ch", "cl"))
        iw_b = take("ml_iw", [P, T], at=o_hm)[0]
        kt = take("ml_kt", [P, T], at=o_hm + 4 * T)[0]
        am_hi, am_lo = (take(f"ml_{n}", [P, T], F32R, at=o_q + 4 * T * n_)[0] for n_, n in enumerate(("ah", "al")))
        ml_so = take("ml_so", [P, NC, ML_V], at=o_v)[0]
        ml_z = [take(f"ml_z{b}", [P, T], at=o_w + 4 * T * b)[0] for b in range(2)]
        my_hi = [take(f"ml_yh{b}", [P, T], F32R, at=(o_i, o_k)[b])[0] for b in range(2)]
        my_lo = [take(f"ml_yl{b}", [P, T], F32R, at=(o_i, o_k)[b] + 4 * T)[0] for b in range(2)]
        take = overlay(resid_base)
        wsp = take("sg_w", [P, SG_GROUPS, P])[0]
        bsp = take("sg_b", [P, SG_GROUPS, P])[0]
        g_t = [take(f"sg_g{b}", [P, T])[0] for b in range(2)]
        g_tok = [take(f"sg_t{b}", [P, NC, P])[0] for b in range(2)]
        wr = take("sg_wr", [P, NC, P])[0]
        wr_hi, wr_lo = (take(f"sg_{n}", [P, NC, P], F32R)[0] for n in ("wrh", "wrl"))
        sg_v = take("sg_v", [P, T])[0]
        sy_hi = [take(f"sg_yh{b}", [P, T], F32R)[0] for b in range(2)]
        sy_lo = [take(f"sg_yl{b}", [P, T], F32R)[0] for b in range(2)]
        sg_u, sg_z = g_t

        ps = ctx.enter_context(nc.psum_tensor("ps", [P, 4 * T], F32))
        PS = [ps[:, n * T:(n + 1) * T] for n in range(4)]

        res_scr = nc.dram_tensor("res_scr", [P, KT, T], F32, kind="Internal").ap()
        gate_scr = nc.dram_tensor("gate_scr", [5, ML_HEADS, T], F32, kind="Internal").ap()
        gv_scr = nc.dram_tensor("gv_scr", [SG_TILES, P, T], F32, kind="Internal").ap()

        def beat(name, per=1, prime=0):
            return Beat(ctx.enter_context(nc.semaphore(name)), per, prime)

        in_load = [beat(f"in_load{s}", 16) for s in range(2)]
        c_load = beat("c_load", 16)
        in_hi, c_hi_done = beat("in_hi"), beat("c_hi")
        in_split, c_split = beat("in_split", 1, 2), beat("c_split", 1, 1)
        in_mm, c_mm = beat("in_mm", 1, 2), beat("c_mm", 1, 1)
        out_mm = beat("out_mm", 2 * KT - 1)
        out_ev = beat("out_ev", 2 * KT, 1)

        par_ld, small_ld = beat("par_ld", 16), beat("small_ld", 32)
        x_ld = [beat(f"x_ld{n}", 16) for n in range(2)]
        mod_ld = [beat(f"mod_ld{b}", 16) for b in range(MOD_BUFFERS)]
        const = beat("const")
        siluc = beat("siluc")
        mod_mm, mod_out, mod_turn, mod_col = beat("mod_mm"), beat("mod_out"), beat("mod_turn"), beat("mod_col")
        sc1_done = beat("sc1_done")
        lam_mm, lam_x, lam_done = beat("lam_mm"), beat("lam_x"), beat("lam_done")
        px, p_sum, p_hx, px_step, p_done = beat("px"), beat("p_sum"), beat("p_hx"), beat("px_step"), beat("p_done")
        x_scaled, pool_mm, z_done = beat("x_scaled"), beat("pool_mm"), beat("z_done")
        n_mean_mm, n_mean, n_cent = beat("n_mean_mm", 2), beat("n_mean", 2), beat("n_cent", 2 * KT)
        n_sq, n_ssum, n_std, n_rstd = beat("n_sq", 2 * KT), beat("n_ssum", 2 * KT), beat("n_std", 2), beat("n_rstd", 2)
        n_out, n_pair = beat("n_out", 2 * KT), beat("n_pair", KT // 2)
        s_tmp, s_hi = beat("s_tmp", 2 * KT), beat("s_hi", 2 * KT)
        s_lo = [beat(f"s_lo{b}", KT) for b in range(2)]
        post_h = [beat(f"post_h{b}", KT) for b in range(2)]
        n_res, n_gain = beat("n_res", KT), beat("n_gain", 2 * KT)
        spill, refill, acc_zero = beat("spill", 16), beat("refill", 16), beat("acc_zero")
        post_t = beat("post_t", 2 * KT)
        store = beat("store", 16)

        f_silu, f_mul, f_hi, f_lo = beat("f_silu", 1, 1), beat("f_mul", 1, 1), beat("f_hi"), beat("f_lo", 1, 1)

        g_in, g_act, g_dve, g_exp, g_st = beat("g_in"), beat("g_act"), beat("g_dve"), beat("g_exp"), beat("g_st", 16)

        in_half = beat("in_half")
        a_qh, a_ql, a_kh, a_kl, a_v, a_z = (beat(f"a_{n}", 2) for n in ("qh", "ql", "kh", "kl", "v", "z"))
        a_vtr, a_vh, a_vl = beat("a_vtr", 2), beat("a_vh", 2), beat("a_vl", 2)
        a_score, a_max, a_exp = beat("a_score", 16), beat("a_max", 16), beat("a_exp", 16)
        a_rec, a_nr, a_p0, a_mix = beat("a_rec", 8), beat("a_nr", 8), beat("a_p0", 8), beat("a_mix", 8)
        a_tr, a_hi_d, a_lo_d = beat("a_tr", 12), beat("a_hi_d", 12), beat("a_lo_d", 12)
        a_pv, a_o, a_sq, a_r = beat("a_pv", 2), beat("a_o", 4), beat("a_sq", 4), beat("a_r", 2)
        a_ss, a_std = beat("a_ss"), beat("a_std")
        a_y, a_yh, a_yl = beat("a_y", 2), beat("a_yh", 2), beat("a_yl", 2)

        m_ld = beat("m_ld", 80)
        m_x, m_conv, m_silu, m_q = beat("m_x", 2), beat("m_conv", 8), beat("m_silu", 2), beat("m_q", 2)
        m_qkh, m_qkl, m_vt, m_vh, m_vl = beat("m_qkh", 3), beat("m_qkl", 3), beat("m_vt", 2), beat("m_vh", 2), beat("m_vl", 6)
        m_ktr, m_kw, m_kwh, m_kwl = beat("m_ktr"), beat("m_kw", 8), beat("m_kwh"), beat("m_kwl")
        m_vtr, m_dt, m_de, m_mask = beat("m_vtr", 2), beat("m_dt", 8), beat("m_de"), beat("m_mask")
        m_s, m_am, m_ah, m_al = beat("m_s"), beat("m_am"), beat("m_ah"), beat("m_al")
        m_p, m_c, m_ch, m_cl, m_num = beat("m_p", 7), beat("m_c", 7), beat("m_ch", 7), beat("m_cl", 7), beat("m_num", 8)
        m_den, m_rd, m_hm = beat("m_den", 1 + 2 * NC), beat("m_rd", NC), beat("m_hm", NC)
        m_ot, m_otr, m_so, m_g = beat("m_ot", 2), beat("m_otr", 2), beat("m_so", 2), beat("m_g")
        m_ss, m_std, m_r, m_n = beat("m_ss", 8), beat("m_std"), beat("m_r"), beat("m_n", 8)
        m_ntr, m_z, m_y, m_yh, m_yl = beat("m_ntr", 2), beat("m_z", 2), beat("m_y", 4), beat("m_yh", 2), beat("m_yl", 2)

        v_g, v_tr, v_tok, v_sq = beat("v_g", 1, 2), beat("v_tr", 1, 2), beat("v_tok", 1, 2), beat("v_sq", 8, 2)
        v_st = [beat(f"v_st{b}", 16, 1) for b in range(2)]
        v_r = beat("v_r")
        w_s, w_h, w_l = beat("w_s", 8, 1), beat("w_h", 1, 1), beat("w_l", 1, 1)
        e_vs, e_u, e_z, e_v, e_y, e_yh, e_yl = (beat("e_vs"), beat("e_u", 1, 1), beat("e_z", 1, 1), beat("e_v", 1, 1),
                                              beat("e_y", 2, 1), beat("e_yh"), beat("e_yl", 1, 1))
        sp_ld = beat("sp_ld", 32)

        block = ctx.enter_context(nc.Block())

        @block.sync
        def _(sp):
            def load_in(n, slot):
                sp.wait_ge(in_split.sem, in_split.at(n - 2))
                sp.dma_start(raw[slot][:], w_in[bass.ds(n, 1)].rearrange("a p t -> p (a t)"))\
                  .then_inc(in_load[slot].sem, 16)

            def load_c(n, source, row):
                sp.wait_ge(c_split.sem, c_split.at(n - 1))
                sp.dma_start(raw[C][:], source[bass.ds(row, 1)].rearrange("a p t -> p (a t)"))\
                  .then_inc(c_load.sem, 16)

            for n in range(MOD_BLOCKS):
                if n >= MOD_BUFFERS:
                    sp.wait_ge(mod_mm.sem, mod_mm.at(n - MOD_BUFFERS))
                sp.dma_start(mod_big[n % MOD_BUFFERS][:], mod_w[n]).then_inc(mod_ld[n % MOD_BUFFERS].sem, 16)
                if n in X_AFTER:
                    half = X_AFTER.index(n)
                    tiles = slice(half * KT // 2, (half + 1) * KT // 2)
                    sp.dma_start(resid[:, tiles, :], x_t[:, tiles, :]).then_inc(x_ld[half].sem, 16)
            load_in(0, 0)
            load_in(1, 1)
            with sp.Fori(1, F_TILES - 1) as f:
                load_in(2 * f, 0)
                load_in(2 * f + 1, 1)
                load_c(f - 1, w_c, f - 1)
            for s in range(4):
                load_in(IN_FFN_OUT - 2 + s, s % 2)
            load_c(C_GATES, w_c, C_GATES)
            for s in range(8):
                load_in(IN_DA + s, s % 2)
            with sp.Fori(1, DA_HEADS - 1) as h:
                for s in range(4):
                    load_in(IN_DA + 4 * h + (4 + s), s % 2)
                    if s == 0:
                        load_c(C_DA + h - 1, w_c, C_DA + h - 1)
            load_c(C_SG - 2, w_c, C_SG - 2)
            for s in range(2):
                load_in(IN_ML + s, s)
            load_c(C_SG - 1, w_c, C_SG - 1)
            with sp.Fori(0, ML_HEADS - 1) as h:
                for s in range(10):
                    load_in(IN_ML + 10 * h + (2 + s), s % 2)
            for s in range(8):
                load_in(IN_SV - 8 + s, s % 2)
            with sp.Fori(0, SG_TILES // 2) as j:
                for s in range(2):
                    load_in(IN_SV + 2 * j + s, s)
            load_in(IN_SG, 0)
            load_in(IN_SG + 1, 1)
            for b in range(2):
                sp.wait_ge(v_st[b].sem, v_st[b].at(SG_TILES // 2 - 1))
            load_c(C_SG, gv_scr, 0)
            with sp.Fori(1, SG_TILES - 1) as d:
                load_in(IN_SG + 2 * d, 0)
                load_c(C_SG + 2 * d - 1, gv_scr, d)
                load_in(IN_SG + 2 * d + 1, 1)
                load_c(C_SG + 2 * d, w_c, C_SG + d - 1)
            load_in(IN_SG_OUT - 2, 0)
            load_c(C_SG + 2 * SG_TILES - 3, gv_scr, SG_TILES - 1)
            for s in range(1, 4):
                load_in(IN_SG_OUT - 2 + s, s % 2)
            for e in range(2):
                for k in range(KT):
                    n = e * KT + k
                    sp.wait_ge(post_h[n % 2].sem, post_h[n % 2].at(1, n // 2))
                    sp.dma_start(out[:, k, half_of(e)], resid[:, k, half_of(e)]).then_inc(store.sem, 16)
            sp.wait_ge(store.sem, 16 * 2 * KT)

        @block.gpsimd
        def _(pool):
            zeros = zero[:, 0:1].to_broadcast([P, T])
            pool.memset(ident[:], 0.0).then_inc(const.sem, 1)
            pool.memset(ident_b[:], 0.0).then_inc(const.sem, 1)
            pool.memset(mask_b[:], 0.0).then_inc(const.sem, 1)
            pool.memset(ones[:], 1.0).then_inc(const.sem, 1)
            pool.memset(causal[:], 1.0).then_inc(const.sem, 1)
            pool.memset(zero[:], 0.0).then_inc(const.sem, 1)
            pool.memset(eps[:], EPS).then_inc(const.sem, 1)
            for b in range(2):
                pool.memset(xpad[b][:], 0.0).then_inc(const.sem, 1)
            pool.wait_ge(const.sem, 9)
            for tile in (ident, ident_b):
                pool.affine_select(out=tile[:], in_=tile[:], compare_op=ALU.not_equal, fill=1.0, base=0,
                                   pattern=[[-1, P]], channel_multiplier=1).then_inc(const.sem, 1)
            pool.affine_select(out=mask_b[:], in_=mask_b[:], compare_op=ALU.is_ge, fill=MASKED, base=0,
                               pattern=[[-1, P]], channel_multiplier=1).then_inc(const.sem, 1)
            pool.affine_select(out=causal[:], in_=causal[:], compare_op=ALU.is_ge, fill=0.0, base=0,
                               pattern=[[1, P]], channel_multiplier=-1).then_inc(const.sem, 1)
            pool.sem_inc(in_split.sem, in_split.prime)
            pool.sem_inc(c_split.sem, c_split.prime)

            def split(n, slot, load, load_value, hi_done, used, done):
                pool.wait_ge(load.sem, load_value)
                pool.wait_ge(used.sem, used.at(n - used.prime))
                hi = whi[slot][:].rearrange("p k f -> p (k f)")
                pool.tensor_tensor(hi, raw[slot][:], zeros, ALU.add).then_inc(hi_done.sem, 1)
                pool.wait_ge(hi_done.sem, hi_done.at(n))
                pool.tensor_tensor(wlo[slot][:].rearrange("p k f -> p (k f)"), raw[slot][:], hi.bitcast(F32),
                                   ALU.subtract).then_inc(done.sem, 1)

            def split_in(n, slot, turn):
                split(n, slot, in_load[slot], in_load[slot].at(turn), in_hi, in_mm, in_split)

            def split_c(n):
                split(n, C, c_load, c_load.at(n), c_hi_done, c_mm, c_split)

            def split_low(use):
                for n in range(1, 2 * KT, 2):
                    e, k = divmod(n, KT)
                    pool.wait_ge(s_hi.sem, s_hi.at(use, n))
                    pool.tensor_tensor(h_lo[:, k, half_of(e)], tmp[k % 2][:, half_of(e)], h_hi[:, k, half_of(e)].bitcast(F32),
                                       ALU.subtract).then_inc(s_lo[1].sem, 1)

            def residual(use):
                for n in range(1, 2 * KT, 2):
                    e, k = divmod(n, KT)
                    pool.wait_ge(post_t.sem, post_t.at(use, n))
                    tile = resid[:, k, half_of(e)]
                    pool.tensor_tensor(tile, tile, acc[:, k, half_of(e)], ALU.add).then_inc(post_h[1].sem, 1)

            def pair_up(p):
                pool.tensor_tensor(pair[p][:], resid[:, 2 * p, :], resid[:, 2 * p + 1, :], ALU.add).then_inc(n_pair.sem, 1)

            split_in(0, 0, 0)
            split_in(1, 1, 0)
            for p in range(KT // 2):
                pool.wait_ge(z_done.sem, 2 * p + 2)
                pair_up(p)
            split_low(0)

            def low_part(hi_done, done, turn, low, src, high):
                pool.wait_ge(hi_done.sem, hi_done.at(turn))
                pool.tensor_tensor(low[:], src[:], high[:].bitcast(F32), ALU.subtract).then_inc(done.sem, 1)

            with pool.Fori(0, F_TILES // 2 - 1) as j:
                for b in range(2):
                    split_in(4 * j + 2 * (1 + b), 0, 2 * j + (1 + b))
                    split_in(4 * j + (2 * (1 + b) + 1), 1, 2 * j + (1 + b))
                    low_part(f_hi, f_lo, 2 * j + b, ffn_lo[b], ffn_p, ffn_hi[b])
                    split_c(2 * j + b)
            split_in(2 * F_TILES - 2, 0, F_TILES - 1)
            split_in(2 * F_TILES - 1, 1, F_TILES - 1)
            low_part(f_hi, f_lo, F_TILES - 2, ffn_lo[0], ffn_p, ffn_hi[0])
            for s in range(2):
                split_in(IN_FFN_OUT + s, s, IN_FFN_OUT // 2)
            low_part(f_hi, f_lo, F_TILES - 1, ffn_lo[1], ffn_p, ffn_hi[1])
            split_c(C_GATES)
            split_in(IN_DA, 0, IN_DA // 2)
            pool.wait_ge(in_mm.sem, in_mm.at(2 * F_TILES - 1))
            for p in range(KT // 2):
                pool.wait_ge(out_ev.sem, out_ev.at(F_TILES - 1, 4 * p + 3))
                pair_up(p)
            for s in range(1, 8):
                split_in(IN_DA + s, s % 2, (IN_DA + s) // 2)
                if s == 1:
                    split_low(1)
            pool.wait_ge(g_dve.sem, GATE_STEPS)
            by_chunk = lambda col: col.to_broadcast([ML_HEADS, NC, CHUNK])
            pool.tensor_tensor(g_d[:], g_max[:], by_chunk(g_m[:, 0:NC].unsqueeze(2)), ALU.subtract).then_inc(g_exp.sem, 1)
            pool.tensor_tensor(g_d2[:], g_cum[:], g_max[:], ALU.add).then_inc(g_exp.sem, 1)
            pool.tensor_tensor(g_d3[:], g_u[:], by_chunk(g_max[:, :, CHUNK - 1:CHUNK]), ALU.subtract).then_inc(g_exp.sem, 1)
            pool.wait_ge(g_st.sem, 16 * 5)
            pool.memset(acc[:], 0.0).then_inc(acc_zero.sem, 1)
            with pool.Fori(1, DA_HEADS - 1) as h:
                for s in range(4):
                    split_in(IN_DA + 4 * h + (4 + s), s % 2, 2 * h + (IN_DA + 4 + s) // 2)
                    if s == 0:
                        split_c(C_DA + h - 1)
            split_c(C_SG - 2)
            for s in range(2):
                split_in(IN_ML + s, s, IN_ML // 2)
            split_c(C_SG - 1)
            def causal_decays(h):
                pool.wait_ge(m_de.sem, m_de.at(h))
                dt3 = decay_t[:].rearrange("s (c t) -> s c t", t=CHUNK)
                pool.tensor_tensor(dt3, dt3, causal[:].unsqueeze(1).to_broadcast([P, NC, P]), ALU.mult).then_inc(m_mask.sem, 1)

            with pool.Fori(0, ML_HEADS - 1) as h:
                for s in range(10):
                    split_in(IN_ML + 10 * h + (2 + s), s % 2, 5 * h + (IN_ML + 2 + s) // 2)
                    if s == 1:
                        causal_decays(h)
            for s in range(8):
                split_in(IN_SV - 8 + s, s % 2, (IN_SV - 8 + s) // 2)
                if s == 1:
                    causal_decays(ML_HEADS - 1)
            for s in range(2):
                split_in(IN_SV + s, s, IN_SV // 2)
            residual(0)
            split_low(2)
            for half in post_h:
                pool.wait_ge(half.sem, half.at(0))
            for j in (1, 2):
                for s in range(2):
                    split_in(IN_SV + 2 * j + s, s, j + IN_SV // 2)
                if j == 1:
                    pool.memset(acc[:], 0.0).then_inc(acc_zero.sem, 1)
                else:
                    pool.wait_ge(sp_ld.sem, sp_ld.at(0))
                    pool.tensor_tensor(wsp[:], wsp[:], causal[:].unsqueeze(1).to_broadcast([P, SG_GROUPS, P]), ALU.mult)\
                        .then_inc(const.sem, 1)
            with pool.Fori(3, SG_TILES // 2) as j:
                for s in range(2):
                    split_in(IN_SV + 2 * j + s, s, j + IN_SV // 2)
            for s in range(2):
                split_in(IN_SG + s, s, IN_SG // 2)
            split_c(C_SG)

            def sg_tile(d, e, last=False):
                split_in(IN_SG + 2 * d, 0, d + IN_SG // 2)
                low_part(e_yh, e_yl, d - 1, sy_lo[1 - e], sg_v, sy_hi[1 - e])
                split_c(C_SG + 2 * d - 1)
                split_in(IN_SG + 2 * d + 1, 1, d + IN_SG // 2)
                if not last:
                    split_c(C_SG + 2 * d)

            sg_tile(1, 1)
            with pool.Fori(1, SG_GROUPS - 1) as g:
                for e in range(2):
                    sg_tile(2 * g + e, e)
            sg_tile(SG_TILES - 2, 0)
            sg_tile(SG_TILES - 1, 1, last=True)
            for s in range(2):
                split_in(IN_SG_OUT + s, s, IN_SG_OUT // 2)
            low_part(e_yh, e_yl, SG_TILES - 1, sy_lo[1], sg_v, sy_hi[1])
            residual(1)

        @block.tensor
        def _(pe):
            pe.sem_inc(in_mm.sem, in_mm.prime)
            pe.sem_inc(c_mm.sem, c_mm.prime)
            pe.sem_inc(v_tr.sem, v_tr.prime)

            def three(dst, w_h, w_l, r_h, r_l, first, last):
                pe.matmul(dst, w_h, r_h, start=first, stop=False, skip_group_check=True)
                pe.matmul(dst, w_h, r_l, start=False, stop=False, skip_group_check=True)
                return pe.matmul(dst, w_l, r_h, start=False, stop=last, skip_group_check=True)

            def project(n, slot, stream=in_split, done=in_mm, bank=None, between=None):
                dst = PS[slot if bank is None else bank]
                pe.wait_ge(stream.sem, stream.at(n))
                for t0 in (0, HALF):
                    if t0 and between is not None:
                        between()
                    for k in range(KT):
                        mm = three(dst[:, t0:t0 + HALF], whi[slot][:, k, :], wlo[slot][:, k, :],
                                   h_hi[:, k, t0:t0 + HALF], h_lo[:, k, t0:t0 + HALF], k == 0, k == KT - 1)
                mm.then_inc(done.sem, 1)

            def project_first(use, slabs):
                for slot, split, value, _, _ in slabs:
                    pe.wait_ge(split.sem, value)
                for e in range(2):
                    cols = half_of(e)
                    for k in range(KT):
                        n = e * KT + k
                        pe.wait_ge(s_lo[n % 2].sem, s_lo[n % 2].at(use, n // 2))
                        for slot, _, _, bank, done in slabs:
                            mm = three(PS[bank][:, cols], whi[slot][:, k, :], wlo[slot][:, k, :],
                                       h_hi[:, k, cols], h_lo[:, k, cols], k == 0, k == KT - 1)
                            if k == KT - 1 and done[e] is not None:
                                mm.then_inc(done[e].sem, 1)

            def project_quarter(n, slot, part):
                t0 = part // 2 * HALF
                if part == 0:
                    pe.wait_ge(in_split.sem, in_split.at(n))
                for k in range(part % 2 * (KT // 2), (part % 2 + 1) * (KT // 2)):
                    mm = three(PS[slot][:, t0:t0 + HALF], whi[slot][:, k, :], wlo[slot][:, k, :],
                               h_hi[:, k, t0:t0 + HALF], h_lo[:, k, t0:t0 + HALF], k == 0, k == KT - 1)
                if part == 3:
                    mm.then_inc(in_mm.sem, 1)

            def out_half(slot, d, e, dst, r_h, r_l, done, n):
                cols = slice(e * HALF, (e + 1) * HALF)
                mm = three(dst[:, cols], whi[slot][:, d, :], wlo[slot][:, d, :], r_h[:, cols], r_l[:, cols], True, True)
                mm.then_inc((done if d == KT - 1 and n == 1 else out_mm).sem, 1)

            def project_out(n, o, r_h, r_l, slot=C, split=c_split, done=c_mm):
                pe.wait_ge(split.sem, split.at(n))
                for d in range(KT):
                    for e in range(2):
                        if d >= 2:
                            pe.wait_ge(out_ev.sem, out_ev.at(o, 2 * (d - 2) + e))
                        else:
                            pe.wait_ge(out_ev.sem, out_ev.at(o - 1, 2 * (KT - 2 + d) + e))
                        out_half(slot, d, e, PS[2 + d % 2], r_h, r_l, done, e)

            def project_out_in(n, o, r_h, r_l, slot):
                project_out(n, o, r_h, r_l, slot, in_split, in_mm)

            def sum_squares(norm):
                for e in range(2):
                    if norm >= 1:
                        pe.wait_ge(n_std.sem, n_std.at(norm - 1, e))
                    for k in range(KT):
                        n = e * KT + k
                        pe.wait_ge(n_sq.sem, n_sq.at(norm, n))
                        pe.matmul(PS[0][:, half_of(e)], ones[:], sq[n % 4][:], start=(k == 0), stop=(k == KT - 1),
                                  skip_group_check=True).then_inc(n_ssum.sem, 1)

            def mean_of(norm):
                for e in range(2):
                    for p in range(KT // 2):
                        pe.wait_ge(n_pair.sem, n_pair.at(norm, p))
                        mm = pe.matmul(PS[2][:, half_of(e)], ones[:], pair[p][:, half_of(e)],
                                       start=(p == 0), stop=(p == KT // 2 - 1), skip_group_check=True)
                    mm.then_inc(n_mean_mm.sem, 1)

            def turn_tiles(dst, src, sem):
                for b in range(KT):
                    mm = pe.transpose(dst[:, b * P:(b + 1) * P], src(b), ident[:])
                mm.then_inc(sem, 1)

            def mod_block(n):
                pe.wait_ge(mod_ld[n % MOD_BUFFERS].sem, mod_ld[n % MOD_BUFFERS].at(n // MOD_BUFFERS))
                if n >= 2:
                    pe.wait_ge(mod_out.sem, mod_out.at(n - 2))
                for k in range(KT):
                    mm = pe.matmul(PS[3][0:1, n % 2 * HALF:(n % 2 + 1) * HALF], silu_c[:, k:k + 1], mod_big[n % MOD_BUFFERS][:, k, :],
                                   start=(k == 0), stop=(k == KT - 1), skip_group_check=True)
                mm.then_inc(mod_mm.sem, 1)

            def mod_columns(half):
                pe.wait_ge(mod_out.sem, mod_out.at((half + 1) * MOD_HALF - 1))
                for j in range(MOD_HALF * HALF // P):
                    row = mod_row[0:1, j * P // HALF, j * P % HALF:j * P % HALF + P]
                    mm = pe.transpose(PS[1][:, HALF + j:HALF + j + 1], row, ident[0:1, 0:1])
                mm.then_inc(mod_turn.sem, 1)

            pe.wait_ge(const.sem, 13)
            pe.wait_ge(siluc.sem, 1)
            for n in range(MOD_HALF):
                mod_block(n)
            mod_columns(0)
            pe.wait_ge(lam_done.sem, 1)
            pe.matmul(PS[0][:, 0:2], ones[:], lam_prod[:], start=True, stop=True).then_inc(lam_mm.sem, 1)
            for n in range(MOD_HALF, MOD_BLOCKS - 1):
                mod_block(n)
            pe.wait_ge(small_ld.sem, small_ld.at(0))
            pe.wait_ge(lam_x.sem, 1)
            pe.wait_ge(mod_col.sem, 1)
            for j in range(KT):
                g, e = j // 2, j % 2
                pe.wait_ge(p_done.sem, 2 * g + 2)
                if j >= 2:
                    pe.wait_ge(z_done.sem, j - 1)
                for t0 in (0, HALF):
                    for k in range(2):
                        mm = pe.matmul(PS[e][:, t0:t0 + HALF], pw[:, g, k, e * P:(e + 1) * P],
                                       acc[:, 2 * g + k, t0:t0 + HALF], start=(k == 0), stop=(k == 1),
                                       skip_group_check=True)
                mm.then_inc(pool_mm.sem, 1)

            mean_of(0)
            mod_block(MOD_BLOCKS - 1)
            mod_columns(1)
            sum_squares(0)
            pe.wait_ge(n_std.sem, n_std.at(0))
            pe.wait_ge(mod_col.sem, 2)
            project_first(0, [(slot, in_split, in_split.at(slot), slot, (None, in_mm)) for slot in range(2)])

            def ffn_in(f):
                pe.wait_ge(f_silu.sem, f_silu.at(f - 1))
                project(2 * f, 0)
                pe.wait_ge(f_mul.sem, f_mul.at(f - 1))
                project(2 * f + 1, 1)

            def ffn_out(f, b):
                pe.wait_ge(f_lo.sem, f_lo.at(f))
                project_out(f, f, ffn_hi[b], ffn_lo[b])

            with pe.Fori(0, F_TILES // 2 - 1) as j:
                for b in range(2):
                    ffn_in(2 * j + (1 + b))
                    ffn_out(2 * j + b, b)
            ffn_in(F_TILES - 1)
            for b in range(2):
                pe.wait_ge(f_lo.sem, f_lo.at(F_TILES - 2 + b))
                project_out_in(IN_FFN_OUT + b, F_TILES - 2 + b, ffn_hi[b], ffn_lo[b], b)
            pe.wait_ge(out_ev.sem, out_ev.at(F_TILES - 1))
            mean_of(1)
            sum_squares(1)
            sum_squares(2)
            pe.wait_ge(n_std.sem, n_std.at(2))
            project_first(1, [(C, c_split, c_split.at(C_GATES), 0, (None, c_mm)),
                              (0, in_split, in_split.at(IN_DA), 3, (in_half, in_mm))])

            score_bank = (PS[0], PS[1])
            turn_bank = PS[2][:, 0:HALF]
            value_bank = PS[2][:, HALF:T]

            def da_half(h, s, e, ks=range(KT)):
                slot, t0 = s % 2, e * HALF
                if e == 0 and ks[0] == 0:
                    pe.wait_ge(in_split.sem, in_split.at(4 * h + (IN_DA + s)))
                for k in ks:
                    mm = three(PS[3][:, t0:t0 + HALF], whi[slot][:, k, :], wlo[slot][:, k, :],
                               h_hi[:, k, t0:t0 + HALF], h_lo[:, k, t0:t0 + HALF], k == 0, k == KT - 1)
                if ks[-1] == KT - 1:
                    mm.then_inc((in_half, in_mm)[e].sem, 1)

            def da_out_half(h, d, n):
                e = da_halves(d)[n]
                if d == 0 and n == 0:
                    pe.wait_ge(c_split.sem, c_split.at(C_DA + h))
                if d == 0:
                    pe.wait_ge(a_yl.sem, a_yl.at(h, e))
                if d >= 1:
                    pe.wait_ge(out_ev.sem, out_ev.at(OUT_DA + h, 2 * (d - 1) + da_halves(d - 1).index(e)))
                out_half(C, d, e, PS[3], y_hi, y_lo, c_mm, n)

            def da_scores(h, i):
                if i == 0:
                    pe.wait_ge(a_kl.sem, a_kl.at(h, 0))
                if i == HALF // P:
                    pe.wait_ge(a_kl.sem, a_kl.at(h, 1))
                    pe.wait_ge(a_vl.sem, a_vl.at(h))
                cols = slice(i * P, (i + 1) * P)
                for c in range(2):
                    rows = slice(c * DA_QK, (c + 1) * DA_QK)
                    if i >= 1 and c == 0:
                        pe.wait_ge(a_exp.sem, a_exp.at(h, 2 * (i - 1)))
                    elif i >= 1:
                        pe.wait_ge(a_mix.sem, a_mix.at(h, i - 1))
                    for t0 in range(0, (i + 1) * P, HALF):
                        t1 = min(t0 + HALF, (i + 1) * P)
                        three(score_bank[c][:, t0:t1], q_hi[rows, cols], q_lo[rows, cols],
                              k_hi[rows, t0:t1], k_lo[rows, t0:t1], True, True)
                    pe.matmul(score_bank[c][:, cols], ident_b[:], mask_b[:], start=False, stop=True,
                              skip_group_check=True).then_inc(a_score.sem, 1)

            def da_turn(h, i, part):
                pe.wait_ge(a_mix.sem, a_mix.at(h, i))
                if part == 1 or i >= 1:
                    pe.wait_ge(a_lo_d.sem, a_lo_d.at(h, turn_event(i, part) - 1))
                for b in range(4 * part, min(4 * part + 4, i + 1)):
                    mm = pe.transpose(turn_bank[:, (b % 4) * P:(b % 4 + 1) * P], p_0[i % 2][:, b * P:(b + 1) * P], ident[:])
                mm.then_inc(a_tr.sem, 1)

            def da_values(h, j):
                pe.wait_ge(a_lo_d.sem, a_lo_d.at(h, turn_event(2 * j + 1, (2 * j + 1) // 4)))
                if j == 0:
                    pe.wait_ge(a_vl.sem, a_vl.at(h))
                if j == 2:
                    pe.wait_ge(a_o.sem, a_o.at(h, 1))
                    pe.wait_ge(a_sq.sem, a_sq.at(h, 1))
                first_col = j % 2 * 2 * P
                for b in range(2 * j + 2):
                    both = b <= 2 * j
                    slots = slice(2 * b, 2 * b + (2 if both else 1))
                    mm = three(value_bank[:, first_col:first_col + (2 if both else 1) * P], v_hi[:, b, :], v_lo[:, b, :],
                               a_hi[:, slots, :].rearrange("p b q -> p (b q)"), a_lo[:, slots, :].rearrange("p b q -> p (b q)"),
                               b == 0, b == 2 * j + 1)
                if j % 2 == 1:
                    mm.then_inc(a_pv.sem, 1)

            def da_squares(h):
                pe.wait_ge(a_sq.sem, a_sq.at(h))
                pe.wait_ge(a_o.sem, a_o.at(h))
                for t0 in (0, HALF):
                    mm = pe.matmul(PS[2][:, t0:t0 + HALF], ones[:], da_sq[:, t0:t0 + HALF], start=True, stop=True,
                                   skip_group_check=True)
                mm.then_inc(a_ss.sem, 1)

            def da_head(h, first=False, last=False):
                out = not first
                pe.wait_ge(a_kl.sem, a_kl.at(h, 0))
                if out:
                    pe.wait_ge(out_ev.sem, out_ev.at(OUT_DA + h - 2))
                if not last:
                    da_half(h, DA_Z_SLAB, 0, range(0, KT // 2))
                if out:
                    da_values(h - 1, KT // 2 - 1)
                da_scores(h, 0)
                pe.wait_ge(a_v.sem, a_v.at(h))
                for e in range(2):
                    for b in range(4):
                        mm = pe.transpose(score_bank[e][:, HALF + b * P:HALF + (b + 1) * P],
                                          v_t[:, (4 * e + b) * P:(4 * e + b + 1) * P], ident[:])
                    mm.then_inc(a_vtr.sem, 1)
                if not last:
                    da_half(h, DA_Z_SLAB, 0, range(KT // 2, KT))
                if out:
                    da_squares(h - 1)
                da_scores(h, 1)
                pe.wait_ge(a_kl.sem, a_kl.at(h, 1))
                da_half(h, DA_Z_SLAB, 0 if last else 1)
                if out:
                    pe.wait_ge(a_std.sem, a_std.at(h - 1))
                da_turn(h, 0, 0)
                da_scores(h, 2)
                da_turn(h, 1, 0)
                if last:
                    da_half(h, DA_Z_SLAB, 1, range(0, KT // 2))
                else:
                    pe.wait_ge(a_z.sem, a_z.at(h, 0))
                    da_half(h + 1, DA_V_SLAB, 0)
                da_values(h, 0)
                da_turn(h, 2, 0)
                da_scores(h, 3)
                if last:
                    da_half(h, DA_Z_SLAB, 1, range(KT // 2, KT))
                else:
                    pe.wait_ge(a_z.sem, a_z.at(h, 1))
                    da_half(h + 1, DA_V_SLAB, 1)
                da_turn(h, 3, 0)
                da_scores(h, 4)
                if not last:
                    pe.wait_ge(a_v.sem, a_v.at(h + 1))
                if out:
                    pe.wait_ge(a_z.sem, a_z.at(h))
                    for d in DA_TILES[3]:
                        for n in range(2):
                            da_out_half(h - 1, d, n)
                for i in range(4, KT):
                    s, e = (DA_Q_SLAB, DA_K_SLAB)[(i - 4) // 2], i % 2
                    tiles = DA_TILES[i] if out else ()
                    if out:
                        da_out_half(h - 1, tiles[0], 0)
                    if i % 2 == 0:
                        da_values(h, i // 2 - 1)
                    if i >= 5 or not tiles[1:]:
                        da_turn(h, i, 0)
                    if i == 6:
                        da_scores(h, 7)
                        if not last:
                            if out:
                                pe.wait_ge(out_ev.sem, out_ev.at(OUT_DA + h - 1, 2 * tiles[0]))
                            da_half(h + 1, s, e)
                    if not last and i >= 5:
                        before = (a_ql, a_ql, a_kl)[i - 5]
                        pe.wait_ge(before.sem, before.at(h + 1, (0, 1, 0)[i - 5]))
                    if out:
                        da_out_half(h - 1, tiles[0], 1)
                    for d in tiles[1:]:
                        da_out_half(h - 1, d, 0)
                        if d == tiles[1] and i < 5:
                            da_turn(h, i, 0)
                        da_out_half(h - 1, d, 1)
                    if i < 6:
                        da_scores(h, i + 1)
                    if not last and i != 6:
                        if out:
                            pe.wait_ge(out_ev.sem, out_ev.at(OUT_DA + h - 1, 2 * tiles[-1]))
                        da_half(h + 1, s, e)
                    da_turn(h, i, 1)

            for n, (s, e) in enumerate((s, e) for s in (DA_Q_SLAB, DA_K_SLAB) for e in range(2)):
                read = (a_v, a_ql)[n // 2]
                pe.wait_ge(read.sem, read.at(0, e))
                da_half(0, s, e)
            pe.wait_ge(g_in.sem, 2)
            da_head(0, first=True)
            with pe.Fori(1, DA_HEADS - 1) as h:
                da_head(h)
            da_head(DA_HEADS - 1, last=True)
            da_values(DA_HEADS - 1, KT // 2 - 1)
            project(IN_ML, 0)
            da_squares(DA_HEADS - 1)
            project(IN_ML + 1, 1)
            pe.wait_ge(a_std.sem, a_std.at(DA_HEADS - 1))
            pe.wait_ge(a_yl.sem, a_yl.at(DA_HEADS - 1))
            project_out(C_DA + DA_HEADS - 1, OUT_DA + DA_HEADS - 1, y_hi, y_lo)

            def ml_head(h, last=False):
                pe.wait_ge(m_x.sem, m_x.at(h, 0))
                project(IN_ML + 10 * h + 2, 0)
                pe.wait_ge(m_x.sem, m_x.at(h, 1))

                def turn_keys():
                    pe.wait_ge(out_ev.sem, out_ev.at(OUT_ML + 2 * h - 1))
                    pe.wait_ge(m_silu.sem, m_silu.at(h, 1))
                    turn_tiles(PS[2], lambda b: kt[:, b * P:(b + 1) * P], m_ktr.sem)

                project(IN_ML + 10 * h + 3, 1, between=turn_keys)
                pe.wait_ge(m_qkl.sem, m_qkl.at(h, 1))
                for c in range(NC):
                    cols = slice(c * CHUNK, (c + 1) * CHUNK)
                    mm = three(PS[3][:, cols], mk_hi[:, cols], mk_lo[:, cols], mq_hi[:, cols], mq_lo[:, cols], True, True)
                mm.then_inc(m_s.sem, 1)
                pe.wait_ge(m_vt.sem, m_vt.at(h, 0))
                turn_tiles(PS[0], lambda b: mt[:, b * P:(b + 1) * P], m_vtr.sem)
                pe.wait_ge(m_vt.sem, m_vt.at(h, 1))
                turn_tiles(PS[1], lambda b: kt[:, b * P:(b + 1) * P], m_vtr.sem)

                def state_part(c):
                    if c >= 2:
                        pe.wait_ge(m_c.sem, m_c.at(h, c - 2))
                    dst = PS[3][:, (c % 2) * HALF:(c % 2) * HALF + VA]
                    three(dst, kw_hi[:, c, :], kw_lo[:, c, :], va_hi[:, c, :], va_lo[:, c, :], True, True)\
                        .then_inc(m_p.sem, 1)

                pe.wait_ge(m_kwl.sem, m_kwl.at(h))
                pe.wait_ge(m_vl.sem, m_vl.at(h))
                pe.wait_ge(m_am.sem, m_am.at(h))
                state_part(0)
                pe.wait_ge(m_qkl.sem, m_qkl.at(h, 2))
                pe.wait_ge(m_al.sem, m_al.at(h))
                for c in range(NC):
                    if c + 1 < NC - 1:
                        state_part(c + 1)
                    if c >= 2:
                        pe.wait_ge(m_hm.sem, m_hm.at(h, c - 2))
                    cols = slice(c * CHUNK, (c + 1) * CHUNK)
                    dst = PS[2][:, (c % 2) * HALF:(c % 2) * HALF + VA]
                    mm = three(dst, am_hi[:, cols], am_lo[:, cols], va_hi[:, c, :], va_lo[:, c, :], True, c == 0)
                    if c >= 1:
                        pe.wait_ge(m_cl.sem, m_cl.at(h, c - 1))
                        mm = three(dst, mi_hi[:, cols], mi_lo[:, cols], c_hi[:], c_lo[:], False, True)
                    mm.then_inc(m_num.sem, 1)
                    project_quarter(IN_ML + 10 * h + (4 + c // 4), c // 4, c % 4)
                pe.wait_ge(m_ot.sem, m_ot.at(h, 0))
                project(IN_ML + 10 * h + 6, 0)
                for e in range(2):
                    pe.wait_ge(m_ot.sem, m_ot.at(h, e))
                    if e == 0:
                        pe.wait_ge(m_hm.sem, m_hm.at(h))
                    turn_tiles(PS[2 + e], lambda b: (xp[:, b * P:(b + 1) * P], mt[:, b * P:(b + 1) * P])[e], m_otr.sem)
                project(IN_ML + 10 * h + 7, 1)

                def turn_outputs():
                    pe.wait_ge(m_n.sem, m_n.at(h))
                    for e in range(2):
                        turn_tiles(PS[2 + e], lambda b: hm[:, b, e * P:(e + 1) * P], m_ntr.sem)

                if last:
                    turn_outputs()
                else:
                    for e in range(2):
                        pe.wait_ge(m_z.sem, m_z.at(h, e))
                        project(IN_ML + 10 * h + (8 + e), e, between=None if e else turn_outputs)
                for e in range(2):
                    pe.wait_ge(m_yl.sem, m_yl.at(h, e))
                    if e == 0:
                        pe.wait_ge(m_y.sem, m_y.at(h, 1))
                    project_out_in(IN_ML + 10 * h + ((8 if last else 10) + e), OUT_ML + 2 * h + e, my_hi[e], my_lo[e], e)

            with pe.Fori(0, ML_HEADS - 1) as h:
                ml_head(h)
            ml_head(ML_HEADS - 1, last=True)

            pe.wait_ge(m_z.sem, m_z.at(ML_HEADS - 1))
            sum_squares(3)
            sum_squares(4)
            pe.wait_ge(n_std.sem, n_std.at(4))
            def sg_turn(j, s):
                pe.wait_ge(v_g.sem, v_g.at(2 * j + s))
                pe.wait_ge(v_tok.sem, v_tok.at(2 * j + (s - 2)))
                turn_tiles(PS[2 + s], lambda b: g_t[s][:, b * P:(b + 1) * P], v_tr.sem)

            project_first(2, [(s, in_split, in_split.at(IN_SV + s), s, (None, in_mm)) for s in range(2)])
            sg_turn(0, 0)
            with pe.Fori(1, SG_TILES // 2) as j:
                for s in range(2):
                    pe.wait_ge(v_g.sem, v_g.at(2 * j + (s - 2)))
                    project(IN_SV + 2 * j + s, s)
                    sg_turn(j + (s - 1), 1 - s)
            sg_turn(SG_TILES // 2 - 1, 1)

            def sg_tile(d, e, g, first):
                pe.wait_ge(e_u.sem, e_u.at(d - 1))
                project(IN_SG + 2 * d, 0)
                if first and e == 0:
                    project(IN_SG + 2 * d + 1, 1)
                    pe.wait_ge(v_tok.sem, v_tok.at(SG_TILES - 1))
                n = C_SG if first and e == 0 else C_SG + 2 * d - 1
                pe.wait_ge(w_l.sem, w_l.at(g))
                pe.wait_ge(e_v.sem, e_v.at(d - 1))
                pe.wait_ge(c_split.sem, c_split.at(n))
                pe.wait_ge(out_ev.sem, out_ev.at(OUT_SG + d - 2))
                for c in range(NC):
                    mm = three(PS[2][:, c * CHUNK:(c + 1) * CHUNK], whi[C][:, c, :], wlo[C][:, c, :],
                               wr_hi[:, c, :], wr_lo[:, c, :], True, True)
                mm.then_inc(c_mm.sem, 1)
                if not (first and e == 0):
                    pe.wait_ge(e_z.sem, e_z.at(d - 1))
                    project(IN_SG + 2 * d + 1, 1)

            def sg_out(d, e, n):
                pe.wait_ge(e_yl.sem, e_yl.at(d))
                project_out(n, OUT_SG + d, sy_hi[e], sy_lo[e])

            sg_tile(0, 0, 0, True)
            sg_tile(1, 1, 0, True)
            pe.wait_ge(e_v.sem, e_v.at(1))
            sg_out(0, 0, C_SG + 2)

            def sg_turn_out(g, e):
                sg_tile(2 * g + e, e, g, False)
                pe.wait_ge(e_v.sem, e_v.at(2 * g + e))
                sg_out(2 * g + (e - 1), 1 - e, C_SG + 4 * g + 2 * e)

            with pe.Fori(1, SG_GROUPS - 1) as g:
                for e in range(2):
                    sg_turn_out(g, e)
            sg_turn_out(SG_GROUPS - 1, 0)
            sg_tile(SG_TILES - 1, 1, SG_GROUPS - 1, False)
            pe.wait_ge(e_v.sem, e_v.at(SG_TILES - 1))
            for b in range(2):
                pe.wait_ge(e_yl.sem, e_yl.at(SG_TILES - 2 + b))
                project_out_in(IN_SG_OUT + b, OUT_SG + SG_TILES - 2 + b, sy_hi[b], sy_lo[b], b)
            pe.wait_ge(e_z.sem, e_z.at(SG_TILES - 1))
            sum_squares(5)

        @block.scalar
        def _(act):
            for b in (f_silu, v_g, v_sq, w_h, e_u, e_z):
                act.sem_inc(b.sem, b.prime * b.per)
            for b in v_st:
                act.sem_inc(b.sem, b.prime * b.per)
            act.dma_start(par[:], params).then_inc(par_ld.sem, 16)
            act.dma_start(pw[:], pool_w).then_inc(small_ld.sem, 16)
            act.dma_start(edge[:], edges).then_inc(small_ld.sem, 16)
            act.wait_ge(par_ld.sem, 16)
            act.activation(silu_c[:], par[:, COL["c"]:COL["c"] + KT], ACT.Silu).then_inc(siluc.sem, 1)

            def mod_read(n):
                act.wait_ge(mod_mm.sem, mod_mm.at(n))
                if n == MOD_HALF:
                    act.wait_ge(mod_turn.sem, mod_turn.at(0))
                act.activation(mod_row[0:1, n % MOD_HALF, :], PS[3][0:1, n % 2 * HALF:(n % 2 + 1) * HALF], ACT.Copy)\
                   .then_inc(mod_out.sem, 1)

            def pad(k):
                act.wait_ge(x_ld[k // (KT // 2)].sem, 16)
                if k >= 2:
                    act.wait_ge(p_sum.sem, p_sum.at(k - 2))
                act.activation(xpad[k % 2][:, PAD:PAD + T], resid[:, k, :], ACT.Copy).then_inc(px.sem, 1)

            def modulate(k):
                if k >= 2:
                    act.wait_ge(p_done.sem, p_done.at(k - 2))
                act.activation(xpad[k % 2][:, PAD:PAD + T], resid[:, k, :], ACT.Identity, scale=sc1p[:, k:k + 1], bias=mod[:, k:k + 1])\
                   .then_inc(p_hx.sem, 1)
                act.wait_ge(p_hx.sem, p_hx.at(k))
                act.activation(resid[:, k, :], resid[:, k, :], ACT.Copy, scale=ALPHA).then_inc(x_scaled.sem, 1)

            act.wait_ge(const.sem, 13)
            pad(0)
            for k in range(1, MOD_HALF):
                mod_read(k - 1)
                pad(k)
            mod_read(MOD_HALF - 1)
            for k in range(MOD_HALF, KT):
                pad(k)
            act.wait_ge(lam_mm.sem, 1)
            act.activation(lam_exp[:], PS[0][:, 0:2], ACT.Exp).then_inc(lam_x.sem, 1)
            act.wait_ge(sc1_done.sem, 1)
            for k in range(KT):
                modulate(k)
                if k in (1, 4):
                    mod_read(MOD_HALF + k // 3)
            for n in range(MOD_HALF + 2, MOD_BLOCKS - 1):
                mod_read(n)

            def square(norm, src, ready, value, ahead=0, bias=None):
                order = [(0, k) for k in range(KT)] + [(1, k) for k in range(KT)]
                for n, (e, k) in enumerate(order):
                    if n == KT + ahead:
                        root(norm, 0)
                    of_tile = ready[k % 2] if ready is post_h else ready
                    act.wait_ge(of_tile.sem, value(e, k))
                    if n >= 4:
                        act.wait_ge(n_ssum.sem, n_ssum.at(norm, n - 4))
                    src_half = src[:, k, half_of(e)]
                    if bias is None:
                        act.activation(sq[n % 4][:], src_half, ACT.Square).then_inc(n_sq.sem, 1)
                    else:
                        act.activation(sq[n % 4][:], src_half, ACT.Square, bias=bias(k)).then_inc(n_sq.sem, 1)
                        act.wait_ge(n_sq.sem, n_sq.at(norm, n))
                        act.activation(src_half, src_half, ACT.Identity, bias=bias(k)).then_inc(n_out.sem, 1)
                root(norm, 1)

            def root(norm, e):
                act.wait_ge(n_ssum.sem, n_ssum.at(norm, e * KT + KT - 1))
                act.activation(std[:, half_of(e)], PS[0][:, half_of(e)], ACT.Sqrt, bias=eps[:, 0:1], scale=1.0 / D)\
                   .then_inc(n_std.sem, 1)

            def mean_out(norm):
                for e in range(2):
                    act.wait_ge(n_mean_mm.sem, n_mean_mm.at(norm, e))
                    act.activation(mean[:, half_of(e)], PS[2][:, half_of(e)], ACT.Copy, scale=1.0 / D).then_inc(n_mean.sem, 1)

            def split_high(use, n):
                e, k = divmod(n, KT)
                act.wait_ge(s_tmp.sem, s_tmp.at(use, n))
                act.activation(h_hi[:, k, half_of(e)], tmp[k % 2][:, half_of(e)], ACT.Copy).then_inc(s_hi.sem, 1)

            mean_out(0)
            mod_read(MOD_BLOCKS - 1)
            square(0, resid, n_cent, lambda e, k: n_cent.at(0, e * KT + k), ahead=4)
            act.wait_ge(mod_col.sem, 2)
            for n in range(2 * KT):
                e, k = divmod(n, KT)
                act.wait_ge(n_out.sem, n_out.at(0, n))
                if k >= 2:
                    act.wait_ge(s_lo[n % 2].sem, s_lo[n % 2].at(0, (n - 2) // 2))
                act.activation(tmp[k % 2][:, half_of(e)], resid[:, k, half_of(e)], ACT.Identity, scale=sc2p[:, k:k + 1],
                               bias=ffn_b0[:, k:k + 1]).then_inc(s_tmp.sem, 1)
                split_high(0, n)
            def ffn(f, b):
                act.wait_ge(in_mm.sem, in_mm.at(2 * f))
                act.wait_ge(f_mul.sem, f_mul.at(f - 1))
                act.activation(ffn_g[:], PS[0], ACT.Silu).then_inc(f_silu.sem, 1)
                act.wait_ge(f_mul.sem, f_mul.at(f))
                act.activation(ffn_hi[b][:], ffn_p[:], ACT.Copy).then_inc(f_hi.sem, 1)

            for low in s_lo:
                act.wait_ge(low.sem, low.at(0))
            ffn(0, 0)
            for k in range(KT):
                act.activation(resid[:, k, :], resid[:, k, :], ACT.Identity, scale=ALPHA,
                               bias=res_b0[:, k:k + 1]).then_inc(n_res.sem, 1)
            ffn(1, 1)
            with act.Fori(1, F_TILES // 2) as j:
                for b in range(2):
                    ffn(2 * j + b, b)

            mean_out(1)
            square(1, resid, n_cent, lambda e, k: n_cent.at(1, e * KT + k), ahead=4)
            square(2, resid, n_gain, lambda e, k: n_gain.at(0, e * KT + k), bias=lambda k: par_col("ln_b1", k))
            act.wait_ge(n_out.sem, n_out.at(1))
            act.dma_start(res_scr, resid[:]).then_inc(spill.sem, 16)
            for n in range(2 * KT):
                split_high(1, n)

            def gate_rows():
                act.wait_ge(g_exp.sem, 3)
                act.activation(g_d[:], g_d[:], ACT.Exp, scale=-1.0).then_inc(g_act.sem, 1)
                act.activation(g_d2[:], g_d2[:], ACT.Exp, scale=-1.0).then_inc(g_act.sem, 1)
                act.activation(g_d3[:], g_d3[:], ACT.Exp).then_inc(g_act.sem, 1)
                act.wait_ge(g_act.sem, 6)
                for n, row in enumerate((g_max, g_d, g_u, g_d3, g_d2)):
                    act.dma_start(gate_scr[n], flat(row)).then_inc(g_st.sem, 16)

            turn_bank = PS[2][:, 0:HALF]
            value_blocks = PS[2][:, HALF:T].rearrange("p (a s q) -> p a s q", s=2, q=P)

            def half_done(h, s, e):
                done, n = (in_half, 4 * h + s) if e == 0 else (in_mm, 4 * h + (IN_DA + s))
                act.wait_ge(done.sem, done.at(n))

            def da_z_half(h, e, first):
                half_done(h, DA_Z_SLAB, e)
                if not first:
                    act.wait_ge(a_o.sem, a_o.at(h - 1, 2 * e + 1))
                act.activation(da_z[:, half_of(e)], PS[3][:, half_of(e)], ACT.Silu).then_inc(a_z.sem, 1)

            def da_v_half(h, e):
                half_done(h, DA_V_SLAB, e)
                act.activation(v_t[:, half_of(e)], PS[3][:, half_of(e)], ACT.Copy).then_inc(a_v.sem, 1)

            def da_q_half(h, e, first=False):
                half_done(h, DA_Q_SLAB, e)
                if not first:
                    act.wait_ge(a_score.sem, a_score.at(h - 1, (7, 15)[e]))
                act.activation(q_hi[:, half_of(e)], PS[3][:, half_of(e)], ACT.Copy, scale=DA_QK ** -0.5).then_inc(a_qh.sem, 1)

            def da_k_half(h, e, first=False):
                half_done(h, DA_K_SLAB, e)
                if not first:
                    act.wait_ge(a_score.sem, a_score.at(h - 1))
                act.activation(k_hi[:, half_of(e)], PS[3][:, half_of(e)], ACT.Copy).then_inc(a_kh.sem, 1)

            def da_turned(h, i, part):
                slots, blocks = turned_slots(i, part)
                act.wait_ge(a_tr.sem, a_tr.at(h, turn_event(i, part)))
                act.activation(a_hi[:, slots, :], turn_bank[:, 0:blocks * P].rearrange("p (b q) -> p b q", q=P), ACT.Copy)\
                   .then_inc(a_hi_d.sem, 1)

            def da_square(h, e):
                act.wait_ge(a_o.sem, a_o.at(h, 2 * e + 1))
                for odd in range(2):
                    act.activation(da_blocks(da_sq, e, odd), value_blocks[:, :, 1 - odd, :], ACT.Square).then_inc(a_sq.sem, 1)

            def da_root(h):
                act.wait_ge(a_ss.sem, a_ss.at(h))
                act.activation(da_sq[:], PS[2], ACT.Sqrt, bias=eps[:, 0:1], scale=1.0 / DA_V).then_inc(a_std.sem, 1)

            def da_high(h, e):
                act.wait_ge(a_y.sem, a_y.at(h, e))
                act.activation(y_hi[:, half_of(e)], da_o[:, half_of(e)], ACT.Copy).then_inc(a_yh.sem, 1)

            def da_head(h, first=False, last=False):
                if not first:
                    da_square(h - 1, 1)
                da_exp(h, 0)
                for e in range(2):
                    act.wait_ge(a_vtr.sem, a_vtr.at(h, e))
                    act.activation(v_hi[:, 4 * e:4 * e + 4, :].rearrange("p b v -> p (b v)"), PS[e][:, HALF:T], ACT.Copy)\
                       .then_inc(a_vh.sem, 1)
                if not first:
                    da_root(h - 1)
                for i in range(KT):
                    if i >= 2:
                        da_turned(h, i, 0)
                    if i + 1 < KT:
                        da_exp(h, i + 1)
                    if i == 0:
                        da_z_half(h, 0, first)
                        if not last:
                            da_z_half(h, 1, first)
                    if i < 2:
                        da_turned(h, i, 0)
                    if i == 4:
                        da_square(h, 0)
                    if i == 5:
                        da_turned(h, i, 1)
                    if i == 2 and not first:
                        for e in range(2):
                            da_high(h - 1, e)
                    if i in (1, 2) and not last:
                        da_v_half(h + 1, i - 1)
                    if i == 2 and last:
                        da_z_half(h, 1, first)
                    if not last and i in (4, 6):
                        da_q_half(h + 1, (i - 4) // 2)
                    if not last and i in (6, 7):
                        da_k_half(h + 1, i - 6)
                    if i >= 4 and i != 5:
                        da_turned(h, i, 1)
                    if i == KT - 1 and first:
                        gate_rows()

            def da_exp(h, i):
                n = (i + 1) * P
                for c in range(2):
                    act.wait_ge(a_max.sem, a_max.at(h, 2 * i + c))
                    dst = p_0[i % 2] if c == 0 else PS[1]
                    act.activation(dst[:, 0:n], PS[c][:, 0:n], ACT.Exp, bias=stat[:, 4 * (i % 2) + c:4 * (i % 2) + c + 1],
                                   accum_out=stat2[:, 4 * (i % 2) + c:4 * (i % 2) + c + 1]).then_inc(a_exp.sem, 1)

            for low in s_lo:
                act.wait_ge(low.sem, low.at(1))
            act.wait_ge(spill.sem, spill.at(0))
            for e in range(2):
                da_v_half(0, e)
            act.wait_ge(c_mm.sem, c_mm.at(C_GATES))
            gb = COL["gate_b"]
            flat = lambda tile: tile[:].rearrange("h c t -> h (c t)")
            act.activation(flat(g_i), PS[0][0:4, :], ACT.Identity, bias=par[0:4, gb:gb + 1]).then_inc(g_in.sem, 1)
            act.activation(flat(g_f), PS[0][32:36, :], ACT.Identity, bias=par[32:36, gb:gb + 1]).then_inc(g_in.sem, 1)
            act.wait_ge(g_in.sem, 2)
            act.activation(g_a[:], g_f[:], ACT.Abs).then_inc(g_act.sem, 1)
            act.wait_ge(g_act.sem, 1)
            act.activation(g_a[:], g_a[:], ACT.Exp, scale=-1.0).then_inc(g_act.sem, 1)
            act.wait_ge(g_act.sem, 2)
            act.activation(g_a[:], g_a[:], ACT.Ln, bias=ones[0:4, 0:1]).then_inc(g_act.sem, 1)

            for e in range(2):
                da_q_half(0, e, True)
            for e in range(2):
                da_k_half(0, e, True)
            da_head(0, first=True)
            with act.Fori(1, DA_HEADS - 1) as h:
                da_head(h)
            da_head(DA_HEADS - 1, last=True)
            da_square(DA_HEADS - 1, 1)
            da_root(DA_HEADS - 1)
            for e in range(2):
                da_high(DA_HEADS - 1, e)

            def ml_qk(h, first=False):
                if not first:
                    act.wait_ge(m_yl.sem, m_yl.at(h - 1))
                n = IN_ML if first else IN_ML + 10 * h - 2
                act.wait_ge(in_mm.sem, in_mm.at(n))
                act.activation(xp[:, CONV - 1:], PS[0], ACT.Copy).then_inc(m_x.sem, 1)
                act.wait_ge(out_ev.sem, out_ev.at(OUT_ML + 2 * h - 1))
                act.dma_start(decay_t[:], gate_scr[0, bass.ds(h, 1), :].to_broadcast([P, T])).then_inc(m_ld.sem, 16)
                act.dma_start(iw_b[:], gate_scr[1, bass.ds(h, 1), :].to_broadcast([P, T])).then_inc(m_ld.sem, 16)
                for n in range(3):
                    act.dma_start(ml_cols[:, n, :], gate_scr[2 + n, bass.ds(h, 1), :].rearrange("a (c s) -> s (a c)", s=CHUNK),
                                  allow_slow_non_contiguous=True).then_inc(m_ld.sem, 16)
                act.wait_ge(m_conv.sem, m_conv.at(h, 3))
                act.wait_ge(in_mm.sem, in_mm.at(n + 1))
                act.activation(xp[:, CONV - 1:], PS[1], ACT.Copy).then_inc(m_x.sem, 1)
                act.activation(mt[:], mt[:], ACT.Silu).then_inc(m_silu.sem, 1)
                act.wait_ge(m_conv.sem, m_conv.at(h, 7))
                act.activation(kt[:], kt[:], ACT.Silu).then_inc(m_silu.sem, 1)
                act.wait_ge(m_q.sem, m_q.at(h, 0))
                act.activation(mq_hi[:], mt[:], ACT.Copy).then_inc(m_qkh.sem, 1)
                act.wait_ge(m_silu.sem, m_silu.at(h, 1))
                act.activation(mk_hi[:], kt[:], ACT.Copy).then_inc(m_qkh.sem, 1)
                act.wait_ge(m_dt.sem, m_dt.at(h))
                act.activation(decay_t[:], decay_t[:], ACT.Exp, scale=-1.0).then_inc(m_de.sem, 1)
                act.wait_ge(m_kw.sem, m_kw.at(h))
                act.activation(kw_hi[:].rearrange("p c k -> p (c k)"), xp[:, 0:T], ACT.Copy).then_inc(m_kwh.sem, 1)
                act.wait_ge(m_q.sem, m_q.at(h, 1))
                act.activation(mi_hi[:], mt[:], ACT.Copy).then_inc(m_qkh.sem, 1)

            def ml_gate(h, e):
                act.wait_ge(in_mm.sem, in_mm.at(IN_ML + 10 * h + (6 + e)))
                act.activation(ml_z[e][:], PS[e], ACT.Silu).then_inc(m_z.sem, 1)

            def ml_head(h):
                act.wait_ge(in_mm.sem, in_mm.at(IN_ML + 10 * h + 2))
                act.wait_ge(m_qkl.sem, m_qkl.at(h, 2))
                act.activation(mt[:], PS[0], ACT.Copy).then_inc(m_vt.sem, 1)
                act.wait_ge(in_mm.sem, in_mm.at(IN_ML + 10 * h + 3))
                act.wait_ge(m_qkl.sem, m_qkl.at(h, 1))
                act.wait_ge(m_ktr.sem, m_ktr.at(h))
                act.activation(kt[:], PS[1], ACT.Copy).then_inc(m_vt.sem, 1)
                for e in range(2):
                    act.wait_ge(m_vtr.sem, m_vtr.at(h, e))
                    act.activation(va_hi[:, :, e * P:(e + 1) * P], PS[e].rearrange("p (c v) -> p c v", v=P), ACT.Copy)\
                       .then_inc(m_vh.sem, 1)
                act.wait_ge(m_am.sem, m_am.at(h))
                act.activation(am_hi[:], decay_t[:], ACT.Copy).then_inc(m_ah.sem, 1)
                for c in range(NC - 1):
                    act.wait_ge(m_c.sem, m_c.at(h, c))
                    act.wait_ge(m_num.sem, m_num.at(h, c))
                    act.activation(c_hi[:], c_32[:], ACT.Copy).then_inc(m_ch.sem, 1)
                    if c == 4:
                        act.wait_ge(in_mm.sem, in_mm.at(IN_ML + 10 * h + 4))
                        act.activation(xp[:, 0:T], PS[0], ACT.Copy).then_inc(m_ot.sem, 1)
                act.wait_ge(in_mm.sem, in_mm.at(IN_ML + 10 * h + 5))
                act.activation(mt[:], PS[1], ACT.Copy).then_inc(m_ot.sem, 1)
                ml_gate(h, 0)
                for e in range(2):
                    act.wait_ge(m_otr.sem, m_otr.at(h, e))
                    act.activation(ml_so[:, :, e * P:(e + 1) * P], PS[2 + e].rearrange("p (c v) -> p c v", v=P), ACT.Sigmoid)\
                       .then_inc(m_so.sem, 1)
                act.wait_ge(m_g.sem, m_g.at(h))
                for c in range(NC):
                    act.activation(ml_so[:, c, :], hm[:, c, :], ACT.Square, accum_out=stat2[:, c:c + 1]).then_inc(m_ss.sem, 1)
                act.wait_ge(m_ss.sem, m_ss.at(h))
                act.activation(stat2[:, 8:16], stat2[:, 0:8], ACT.Sqrt, bias=eps[:, 0:1], scale=1.0 / ML_V).then_inc(m_std.sem, 1)
                ml_gate(h, 1)
                for e in range(2):
                    act.wait_ge(m_y.sem, m_y.at(h, 2 + e))
                    act.activation(my_hi[e][:], (xp[:, 0:T], mt[:])[e], ACT.Copy).then_inc(m_yh.sem, 1)

            ml_qk(0, first=True)
            with act.Fori(0, ML_HEADS - 1) as h:
                ml_head(h)
                ml_qk(h + 1)
            ml_head(ML_HEADS - 1)

            act.wait_ge(m_yl.sem, m_yl.at(ML_HEADS - 1))
            act.wait_ge(in_mm.sem, in_mm.at(IN_SV - 1))
            act.dma_start(resid[:], res_scr).then_inc(refill.sem, 16)
            square(3, acc, out_ev, lambda e, k: out_ev.at(OUT_SG - 1, 2 * k + e), ahead=4)
            square(4, resid, post_h, lambda e, k: post_h[k % 2].at(0, (e * KT + k) // 2))
            act.dma_start(res_scr, resid[:]).then_inc(spill.sem, 16)
            for n in range(2 * KT):
                split_high(2, n)
            for low in s_lo:
                act.wait_ge(low.sem, low.at(2))
            act.wait_ge(spill.sem, spill.at(1))
            act.dma_start(wsp[:], w_spatial).then_inc(sp_ld.sem, 16)
            act.dma_start(bsp[:].rearrange("p g t -> p (g t)"), b_spatial.to_broadcast([P, SG_GROUPS * P])).then_inc(sp_ld.sem, 16)

            with act.Fori(0, SG_TILES // 2) as j:
                for s in range(2):
                    act.wait_ge(in_mm.sem, in_mm.at(IN_SV + 2 * j + s))
                    act.wait_ge(v_tr.sem, v_tr.at(2 * j + (s - 2)))
                    act.activation(g_t[s][:], PS[s], ACT.Gelu_apprx_tanh).then_inc(v_g.sem, 1)
                for s in range(2):
                    act.wait_ge(v_tok.sem, v_tok.at(2 * j + s))
                    act.dma_start(gv_scr[bass.ds(2 * j + s, 1)].rearrange("a p t -> p (a t)"),
                                  g_tok[s][:].rearrange("p c d -> p (c d)")).then_inc(v_st[s].sem, 16)
                    act.wait_ge(v_sq.sem, v_sq.at(2 * j + (s - 1)))
                    for c in range(NC):
                        act.activation(wr[:, c, :], g_tok[s][:, c, :], ACT.Square,
                                       accum_out=ssq[:, c, bass.ds(2 * j + s, 1)]).then_inc(v_sq.sem, 1)
            act.wait_ge(v_r.sem, 1)
            act.activation(stat2[:, 0:8], stat[:, 0:8], ACT.Sqrt, bias=eps[:, 0:1], scale=1.0 / (SG_TILES * P)).then_inc(v_r.sem, 1)

            def sg_weights(g):
                act.wait_ge(w_s.sem, w_s.at(g))
                act.wait_ge(in_mm.sem, in_mm.at(IN_SG + 4 * g - 1))
                act.activation(wr_hi[:], wr[:], ACT.Copy).then_inc(w_h.sem, 1)

            def sg_tile(d, e):
                act.wait_ge(in_mm.sem, in_mm.at(IN_SG + 2 * d))
                act.wait_ge(e_y.sem, e_y.at(d - 1))
                act.activation(sg_u[:], PS[0], ACT.Gelu_apprx_tanh).then_inc(e_u.sem, 1)
                act.wait_ge(in_mm.sem, in_mm.at(IN_SG + 2 * d + 1))
                act.activation(sg_z[:], PS[1], ACT.Silu).then_inc(e_z.sem, 1)
                act.wait_ge(e_y.sem, e_y.at(d))
                act.activation(sy_hi[e][:], sg_v[:], ACT.Copy).then_inc(e_yh.sem, 1)

            with act.Fori(0, SG_GROUPS) as g:
                sg_weights(g)
                for e in range(2):
                    sg_tile(2 * g + e, e)

            act.wait_ge(e_yl.sem, e_yl.at(SG_TILES - 1))
            act.wait_ge(in_mm.sem, in_mm.at(N_IN - 1))
            act.dma_start(resid[:], res_scr).then_inc(refill.sem, 16)
            square(5, acc, out_ev, lambda e, k: out_ev.at(OUT_SG + SG_TILES - 1, 2 * k + e), ahead=4)

        @block.vector
        def _(dve):
            for b in (out_ev, f_mul, f_lo, v_tok, w_s, w_l, e_v, e_y, e_yl):
                dve.sem_inc(b.sem, b.prime * b.per)

            dve.wait_ge(par_ld.sem, 16)
            dve.tensor_tensor(lam_prod[:], par[:, COL["lam_q"]:COL["lam_q"] + 2], par[:, COL["lam_k"]:COL["lam_k"] + 2],
                              ALU.mult).then_inc(lam_done.sem, 1)
            step = [0]

            def chained(ins):
                step[0] += 1
                ins.then_inc(px_step.sem, 1)
                dve.wait_ge(px_step.sem, step[0])

            SH1, SC1, G1, SH2, SC2, G2 = (slice(n * KT, (n + 1) * KT) for n in range(N_MOD))
            dve.wait_ge(small_ld.sem, 32)
            for k in range(KT):
                levels = k // 2 + 1
                w = 2 ** levels
                dve.wait_ge(px.sem, px.at(k))
                src, lo, hi = xpad[k % 2], 0, TP
                for n in range(levels):
                    back, ahead = (1, 0) if n == 0 else (2 ** (n - 1), 2 ** (n - 1))
                    lo, hi = lo + back, hi - ahead
                    ins = dve.tensor_tensor(tree[n][:, lo:hi], src[:, lo - back:hi - back], src[:, lo + ahead:hi + ahead], ALU.add)
                    if n == 0:
                        ins.then_inc(p_sum.sem, 1)
                        dve.wait_ge(p_sum.sem, p_sum.at(k))
                    else:
                        chained(ins)
                    src = tree[n]
                left, right = w // 2, w // 2 - 1
                e0 = w - 2
                chained(dve.tensor_tensor(src[:, PAD:PAD + left], src[:, PAD:PAD + left], edge[:, e0:e0 + left], ALU.mult))
                if right:
                    chained(dve.tensor_tensor(src[:, PAD + T - right:PAD + T], src[:, PAD + T - right:PAD + T],
                                              edge[:, e0 + left:e0 + left + right], ALU.mult))
                chained(dve.tensor_scalar(acc[:, k, :], src[:, PAD:PAD + T], 1.0 / w, None, ALU.mult))

            dve.wait_ge(mod_turn.sem, mod_turn.at(0))
            nb = COL["mod_b"]
            dve.tensor_tensor(mod[:, 0:24], PS[1][:, HALF:HALF + 24], par[:, nb:nb + 24], ALU.add).then_inc(mod_col.sem, 1)
            dve.wait_ge(mod_col.sem, 1)
            dve.tensor_scalar(sc1p[:], mod[:, SC1], 1.0, None, ALU.add).then_inc(sc1_done.sem, 1)
            dve.wait_ge(sc1_done.sem, 1)
            chained(dve.tensor_tensor(pool_gain[:], mod[:, G1], par[:, COL["pool_scale"]:COL["pool_scale"] + KT], ALU.mult))
            for k in range(KT):
                chained(dve.tensor_scalar(acc[:, k, :], acc[:, k, :], sc1p[:, k:k + 1], mod[:, k:k + 1], ALU.mult, ALU.add))
                dve.wait_ge(p_hx.sem, p_hx.at(k))
                dve.tensor_tensor(acc[:, k, :], acc[:, k, :], xpad[k % 2][:, PAD:PAD + T], ALU.subtract).then_inc(p_done.sem, 1)

            def modulation_rest():
                dve.wait_ge(mod_turn.sem, mod_turn.at(1))
                dve.tensor_tensor(mod[:, 24:48], PS[1][:, HALF:HALF + 24], par[:, nb + 24:nb + 48], ALU.add).then_inc(mod_col.sem, 1)
                dve.wait_ge(mod_col.sem, 2)
                chained(dve.tensor_scalar(sc2p[:], mod[:, SC2], 1.0, None, ALU.add))
                chained(dve.tensor_tensor(ffn_b0[:], ln_b0, sc2p[:], ALU.mult))
                chained(dve.tensor_tensor(ffn_b0[:], ffn_b0[:], mod[:, SH2], ALU.add))

            ln_b0 = par[:, COL["ln_b0"]:COL["ln_b0"] + KT]
            chained(dve.tensor_scalar(res_b0[:], ln_b0, ALPHA, None, ALU.mult))
            chained(dve.tensor_scalar(da_gain[:], par_col("da_g"), 1.0 - LAM_INIT, None, ALU.mult))
            dve.wait_ge(lam_x.sem, 1)
            chained(dve.scalar_tensor_tensor(neg_lam[:], lam_exp[:, 1:2], LAM_INIT, lam_exp[:, 0:1], ALU.subtract, ALU.subtract))
            for j in range(KT):
                dve.wait_ge(pool_mm.sem, j + 1)
                dve.wait_ge(x_scaled.sem, j + 1)
                dve.scalar_tensor_tensor(resid[:, j, :], PS[j % 2], pool_gain[:, j:j + 1], resid[:, j, :], ALU.mult, ALU.add)\
                   .then_inc(z_done.sem, 1)

            def center(norm, ready, value):
                for e in range(2):
                    dve.wait_ge(n_mean.sem, n_mean.at(norm, e))
                    dve.wait_ge(ready, value)
                    for k in range(KT):
                        tile = resid[:, k, half_of(e)]
                        dve.tensor_tensor(tile, tile, mean[:, half_of(e)], ALU.subtract).then_inc(n_cent.sem, 1)

            def reciprocal(norm, e):
                dve.wait_ge(n_std.sem, n_std.at(norm, e))
                dve.reciprocal(rstd[:, half_of(e)], std[:, half_of(e)]).then_inc(n_rstd.sem, 1)
                dve.wait_ge(n_rstd.sem, n_rstd.at(norm, e))

            def gain(tile, k, e, g_name, done, dst=None):
                src = tile[:, k, half_of(e)]
                dve.scalar_tensor_tensor(src if dst is None else dst, src, par_col(g_name, k), rstd[:, half_of(e)], ALU.mult, ALU.mult)\
                   .then_inc(done.sem, 1)

            def split_low(use, n):
                e, k = divmod(n, KT)
                dve.wait_ge(s_hi.sem, s_hi.at(use, n))
                dve.tensor_tensor(h_lo[:, k, half_of(e)], tmp[k % 2][:, half_of(e)], h_hi[:, k, half_of(e)].bitcast(F32),
                                  ALU.subtract).then_inc(s_lo[0].sem, 1)

            center(0, z_done.sem, KT)
            modulation_rest()
            for e in range(2):
                reciprocal(0, e)
                for k in range(KT):
                    gain(resid, k, e, "ln_g0", n_out)
                    if k % 2 == 1:
                        split_low(0, e * KT + k - 1)

            def add_out(slab, o, gain=None, to=acc, done=c_mm):
                dve.wait_ge(out_ev.sem, out_ev.at(o - 1))
                for d in range(KT):
                    for e in range(2):
                        add_half(PS[2 + d % 2], slab, o, d, e, gain, to, done, e)

            def add_half(src, slab, o, d, e, gain=None, to=acc, done=c_mm, n=0):
                cols = slice(e * HALF, (e + 1) * HALF)
                if 2 * d + n < 2 * KT - 1:
                    dve.wait_ge(out_mm.sem, out_mm.at(o, 2 * d + n))
                else:
                    dve.wait_ge(done.sem, done.at(slab))
                if gain is not None:
                    ins = dve.scalar_tensor_tensor(to[:, d, cols], src[:, cols], gain[:, d:d + 1], to[:, d, cols], ALU.mult, ALU.add)
                else:
                    ins = dve.tensor_tensor(to[:, d, cols], src[:, cols], to[:, d, cols], ALU.add)
                ins.then_inc(out_ev.sem, 1)

            def ffn(f):
                dve.wait_ge(in_mm.sem, in_mm.at(2 * f + 1))
                dve.wait_ge(f_silu.sem, f_silu.at(f))
                dve.wait_ge(f_lo.sem, f_lo.at(f - 1))
                dve.tensor_tensor(ffn_p[:], PS[1], ffn_g[:], ALU.mult).then_inc(f_mul.sem, 1)

            g2 = mod[:, G2]
            ffn(0)
            dve.wait_ge(n_res.sem, n_res.at(0))
            with dve.Fori(0, F_TILES // 2 - 1) as j:
                for b in range(2):
                    ffn(2 * j + (1 + b))
                    add_out(2 * j + b, 2 * j + b, g2, resid)
            ffn(F_TILES - 1)
            for b in range(2):
                add_out(IN_FFN_OUT + b, F_TILES - 2 + b, g2, resid, in_mm)

            center(1, out_ev.sem, out_ev.at(F_TILES - 1))
            for e in range(2):
                reciprocal(1, e)
                for k in range(KT):
                    gain(resid, k, e, "ln_g1", n_gain)

            def layer_input(norm, use, g_name):
                for e in range(2):
                    reciprocal(norm, e)
                    if norm == 2:
                        dve.wait_ge(n_out.sem, n_out.at(1, e * KT + KT - 1))
                    for k in range(KT):
                        n = e * KT + k
                        if k >= 2:
                            dve.wait_ge(s_lo[n % 2].sem, s_lo[n % 2].at(use, (n - 2) // 2))
                        gain(resid, k, e, g_name, s_tmp, tmp[k % 2][:, half_of(e)])
                        if k % 2 == 1:
                            split_low(use, n - 1)

            layer_input(2, 1, "l0_pre_g")

            count = [0]

            def gate_step(ins):
                count[0] += 1
                ins.then_inc(g_dve.sem, 1)
                dve.wait_ge(g_dve.sem, count[0])

            dve.wait_ge(spill.sem, spill.at(0))
            for low in s_lo:
                dve.wait_ge(low.sem, low.at(1))

            def gates(part):
                if part == 0:
                    gate_step(dve.memset(g_zero[:], 0.0))
                    gate_step(dve.memset(g_m[:], 0.0))
                    dve.wait_ge(g_act.sem, 3)
                    gate_step(dve.scalar_tensor_tensor(g_lf[:], g_f[:], 0.0, g_a[:], ALU.min, ALU.subtract))
                if part == 1:
                    for c in range(NC):
                        gate_step(dve.tensor_tensor_scan(g_cum[:, c, :], g_lf[:, c, :], g_zero[:], 0.0, ALU.add, ALU.add))
                if part == 2:
                    gate_step(dve.tensor_tensor(g_u[:], g_i[:], g_cum[:], ALU.subtract))
                for c in {2: range(0, 2), 3: range(2, NC)}.get(part, ()):
                    last_of = slice(CHUNK - 1, CHUNK)
                    gate_step(dve.tensor_tensor_scan(g_max[:, c, :], g_u[:, c, :], g_u[:, c, :], g_m[:, c:c + 1], ALU.max, ALU.max))
                    gate_step(dve.tensor_tensor(g_m[:, c + 1:c + 2], g_cum[:, c, last_of], g_max[:, c, last_of], ALU.add))
                if part == 3:
                    assert count[0] == GATE_STEPS

            turn_bank = PS[2][:, 0:HALF]
            value_blocks = PS[2][:, HALF:T].rearrange("p (a s q) -> p a s q", s=2, q=P)

            def da_q_low(h, e):
                dve.wait_ge(a_qh.sem, a_qh.at(h, e))
                dve.scalar_tensor_tensor(q_lo[:, half_of(e)], PS[3][:, half_of(e)], DA_QK ** -0.5,
                                         q_hi[:, half_of(e)].bitcast(F32), ALU.mult, ALU.subtract).then_inc(a_ql.sem, 1)

            def da_k_low(h, e):
                dve.wait_ge(a_kh.sem, a_kh.at(h, e))
                dve.tensor_tensor(k_lo[:, half_of(e)], PS[3][:, half_of(e)], k_hi[:, half_of(e)].bitcast(F32), ALU.subtract)\
                   .then_inc(a_kl.sem, 1)

            def da_out_add(h, d, n):
                add_half(PS[3], C_DA + h, OUT_DA + h, d, da_halves(d)[n], n=n)

            def da_max(h, i):
                n = (i + 1) * P
                for c in range(2):
                    dve.wait_ge(a_score.sem, a_score.at(h, 2 * i + c))
                    dve.tensor_reduce(stat[:, 4 * (i % 2) + c:4 * (i % 2) + c + 1], PS[c][:, 0:n], AX_X, ALU.max, negate=True)\
                       .then_inc(a_max.sem, 1)

            def da_mix(h, i):
                n = (i + 1) * P
                st = 4 * (i % 2)
                dve.wait_ge(a_exp.sem, a_exp.at(h, 2 * i + 1))
                dve.reciprocal(stat2[:, st + 2:st + 4], stat2[:, st:st + 2]).then_inc(a_rec.sem, 1)
                dve.wait_ge(a_rec.sem, a_rec.at(h, i))
                dve.tensor_scalar(stat[:, st + 2:st + 3], stat2[:, st + 3:st + 4], neg_lam[:, 0:1], None, ALU.mult).then_inc(a_nr.sem, 1)
                dve.tensor_scalar(p_0[i % 2][:, 0:n], p_0[i % 2][:, 0:n], stat2[:, st + 2:st + 3], None, ALU.mult).then_inc(a_p0.sem, 1)
                dve.wait_ge(a_nr.sem, a_nr.at(h, i))
                dve.wait_ge(a_p0.sem, a_p0.at(h, i))
                dve.scalar_tensor_tensor(p_0[i % 2][:, 0:n], PS[1][:, 0:n], stat[:, st + 2:st + 3], p_0[i % 2][:, 0:n],
                                         ALU.mult, ALU.add).then_inc(a_mix.sem, 1)

            def da_turn_low(h, i, part):
                slots, blocks = turned_slots(i, part)
                dve.wait_ge(a_hi_d.sem, a_hi_d.at(h, turn_event(i, part)))
                dve.tensor_tensor(a_lo[:, slots, :], turn_bank[:, 0:blocks * P].rearrange("p (b q) -> p b q", q=P),
                                  a_hi[:, slots, :].bitcast(F32), ALU.subtract).then_inc(a_lo_d.sem, 1)

            def da_gate(h, e):
                dve.wait_ge(a_pv.sem, a_pv.at(h, e))
                dve.wait_ge(a_z.sem, a_z.at(h, e))
                for odd in range(2):
                    dve.tensor_tensor(da_blocks(da_o, e, odd), value_blocks[:, :, 1 - odd, :], da_blocks(da_z, e, odd), ALU.mult)\
                       .then_inc(a_o.sem, 1)

            def da_norm(h, e):
                dve.wait_ge(a_std.sem, a_std.at(h))
                dve.reciprocal(da_sq[:, half_of(e)], da_sq[:, half_of(e)]).then_inc(a_r.sem, 1)

            def da_result(h, e):
                dve.wait_ge(a_r.sem, a_r.at(h, e))
                dve.scalar_tensor_tensor(da_o[:, half_of(e)], da_o[:, half_of(e)], da_gain[:, 0:1], da_sq[:, half_of(e)],
                                         ALU.mult, ALU.mult).then_inc(a_y.sem, 1)

            def da_result_low(h, e):
                dve.wait_ge(a_yh.sem, a_yh.at(h, e))
                dve.tensor_tensor(y_lo[:, half_of(e)], da_o[:, half_of(e)], y_hi[:, half_of(e)].bitcast(F32), ALU.subtract)\
                   .then_inc(a_yl.sem, 1)

            def da_head(h, first=False, last=False):
                out = not first
                if out:
                    da_gate(h - 1, 1)
                da_max(h, 0)
                for e in range(2):
                    dve.wait_ge(a_vh.sem, a_vh.at(h, e))
                    dve.tensor_tensor(v_lo[:, 4 * e:4 * e + 4, :].rearrange("p b v -> p (b v)"), PS[e][:, HALF:T],
                                      v_hi[:, 4 * e:4 * e + 4, :].rearrange("p b v -> p (b v)").bitcast(F32), ALU.subtract)\
                       .then_inc(a_vl.sem, 1)
                da_mix(h, 0)
                for i in range(KT):
                    tiles = DA_TILES[i] if out and i >= 3 else ()
                    if out and i == 3:
                        dve.wait_ge(acc_zero.sem, 1)
                    if i >= 4:
                        for d in tiles[:1]:
                            da_out_add(h - 1, d, 0)
                        if i == 6 or not tiles[1:]:
                            da_turn_low(h, i, 0)
                        if i == 6:
                            da_max(h, 7)
                            if not last:
                                da_q_low(h + 1, 1)
                            da_mix(h, 7)
                        for d in tiles[:1]:
                            da_out_add(h - 1, d, 1)
                        for d in tiles[1:]:
                            for n in range(2):
                                da_out_add(h - 1, d, n)
                        if i != 6 and tiles[1:]:
                            da_turn_low(h, i, 0)
                    if i in (2, 3):
                        da_turn_low(h, i, 0)
                    if i + 1 < KT and i != 6:
                        da_max(h, i + 1)
                    if i == 1:
                        da_turn_low(h, i, 0)
                    if i == 3:
                        for d in tiles:
                            for n in range(2):
                                da_out_add(h - 1, d, n)
                    if out and i == 1:
                        da_norm(h - 1, 0)
                    if out and i == 2:
                        for e in range(2):
                            da_result(h - 1, e)
                    if i + 1 < KT and i != 6:
                        da_mix(h, i + 1)
                    if out and i == 1:
                        da_norm(h - 1, 1)
                    if i == 0:
                        da_turn_low(h, i, 0)
                    if out and i == 2:
                        for e in range(2):
                            da_result_low(h - 1, e)
                    if i == 4:
                        da_gate(h, 0)
                    if first and i < 4:
                        gates(i)
                    if i == 5:
                        da_turn_low(h, i, 1)
                    if not last and i == 4:
                        da_q_low(h + 1, 0)
                    if not last and i in (6, 7):
                        da_k_low(h + 1, i - 6)
                    if i >= 4 and i != 5:
                        da_turn_low(h, i, 1)

            for e in range(2):
                da_q_low(0, e)
            for e in range(2):
                da_k_low(0, e)
            da_head(0, first=True)
            with dve.Fori(1, DA_HEADS - 1) as h:
                da_head(h)
            da_head(DA_HEADS - 1, last=True)
            da_gate(DA_HEADS - 1, 1)
            for e in range(2):
                da_norm(DA_HEADS - 1, e)
            for e in range(2):
                da_result(DA_HEADS - 1, e)
            for e in range(2):
                da_result_low(DA_HEADS - 1, e)
            add_out(C_DA + DA_HEADS - 1, OUT_DA + DA_HEADS - 1)

            def conv(h, which, event, dst):
                col = lambda j: par[:, bass.ds(h + (COL["conv_w"] + 8 * j + 4 * which), 1)]
                dve.tensor_scalar(dst[:], xp[:, 0:T], col(0), par[:, bass.ds(h + (COL["conv_b"] + 4 * which), 1)], ALU.mult, ALU.add)\
                   .then_inc(m_conv.sem, 1)
                for j in range(1, CONV):
                    dve.wait_ge(m_conv.sem, m_conv.at(h, event + j - 1))
                    dve.scalar_tensor_tensor(dst[:], xp[:, j:j + T], col(j), dst[:], ALU.mult, ALU.add).then_inc(m_conv.sem, 1)

            def ml_qk(h):
                dve.wait_ge(out_ev.sem, out_ev.at(OUT_ML + 2 * h - 1))
                dve.memset(xp[:, 0:CONV - 1], 0.0).then_inc(m_vl.sem, 1)
                dve.memset(va_hi[:, :, ML_V:ML_V + 1].bitcast(F32), 1.0).then_inc(m_vl.sem, 1)
                dve.memset(va_hi[:, :, ML_V + 1:VA].bitcast(F32), 0.0).then_inc(m_vl.sem, 1)
                dve.memset(va_lo[:, :, ML_V:VA].bitcast(F32), 0.0).then_inc(m_vl.sem, 1)
                dve.wait_ge(m_vl.sem, m_vl.at(h, 0))
                dve.wait_ge(m_x.sem, m_x.at(h, 0))
                conv(h, 0, 0, mt)
                dve.wait_ge(m_x.sem, m_x.at(h, 1))
                conv(h, 1, 4, kt)
                dve.wait_ge(m_silu.sem, m_silu.at(h, 0))
                dve.tensor_scalar(mt[:], mt[:], ML_QK ** -0.5, None, ALU.mult).then_inc(m_q.sem, 1)
                dve.wait_ge(m_ld.sem, m_ld.at(h))
                for c in range(NC):
                    cols = slice(c * CHUNK, (c + 1) * CHUNK)
                    dve.tensor_scalar(decay_t[:, cols], decay_t[:, cols], ml_cols[:, 0, c:c + 1], 0.0, ALU.subtract, ALU.max)\
                       .then_inc(m_dt.sem, 1)
                dve.tensor_copy(stat[:, 8:16], iw_b[:, CHUNK - 1:T:CHUNK]).then_inc(m_den.sem, 1)
                dve.wait_ge(m_qkh.sem, m_qkh.at(h, 0))
                dve.tensor_tensor(mq_lo[:], mt[:], mq_hi[:].bitcast(F32), ALU.subtract).then_inc(m_qkl.sem, 1)
                dve.wait_ge(m_qkh.sem, m_qkh.at(h, 1))
                dve.tensor_tensor(mk_lo[:], kt[:], mk_hi[:].bitcast(F32), ALU.subtract).then_inc(m_qkl.sem, 1)
                dve.wait_ge(m_ktr.sem, m_ktr.at(h))
                for c in range(NC):
                    cols = slice(c * CHUNK, (c + 1) * CHUNK)
                    dve.tensor_scalar(xp[:, cols], PS[2][:, cols], ml_cols[:, 1, c:c + 1], None, ALU.mult).then_inc(m_kw.sem, 1)
                dve.wait_ge(m_qkl.sem, m_qkl.at(h, 0))
                dve.tensor_tensor(mt[:], mt[:], iw_b[:], ALU.mult).then_inc(m_q.sem, 1)
                dve.wait_ge(m_kwh.sem, m_kwh.at(h))
                dve.tensor_tensor(kw_lo[:].rearrange("p c k -> p (c k)"), xp[:, 0:T],
                                  kw_hi[:].rearrange("p c k -> p (c k)").bitcast(F32), ALU.subtract).then_inc(m_kwl.sem, 1)
                dve.wait_ge(m_qkh.sem, m_qkh.at(h, 2))
                dve.tensor_tensor(mi_lo[:], mt[:], mi_hi[:].bitcast(F32), ALU.subtract).then_inc(m_qkl.sem, 1)

            def ml_head(h, last=False):
                dve.wait_ge(m_s.sem, m_s.at(h))
                dve.wait_ge(m_mask.sem, m_mask.at(h))
                dve.tensor_tensor(decay_t[:], PS[3], decay_t[:], ALU.mult).then_inc(m_am.sem, 1)
                for e in range(2):
                    dve.wait_ge(m_vh.sem, m_vh.at(h, e))
                    dve.tensor_tensor(va_lo[:, :, e * P:(e + 1) * P], PS[e].rearrange("p (c v) -> p c v", v=P),
                                      va_hi[:, :, e * P:(e + 1) * P].bitcast(F32), ALU.subtract).then_inc(m_vl.sem, 1)
                dve.wait_ge(m_ah.sem, m_ah.at(h))
                dve.tensor_tensor(am_lo[:], decay_t[:], am_hi[:].bitcast(F32), ALU.subtract).then_inc(m_al.sem, 1)
                for c in range(NC):
                    if c < NC - 1:
                        part = PS[3][:, (c % 2) * HALF:(c % 2) * HALF + VA]
                        dve.wait_ge(m_p.sem, m_p.at(h, c))
                        if c == 0:
                            dve.tensor_copy(c_32[:], part).then_inc(m_c.sem, 1)
                        else:
                            dve.wait_ge(m_cl.sem, m_cl.at(h, c - 1))
                            dve.scalar_tensor_tensor(c_32[:], c_32[:], stat[:, 8 + c:9 + c], part, ALU.mult, ALU.add).then_inc(m_c.sem, 1)
                        dve.wait_ge(m_ch.sem, m_ch.at(h, c))
                        dve.tensor_tensor(c_lo[:], c_32[:], c_hi[:].bitcast(F32), ALU.subtract).then_inc(m_cl.sem, 1)
                    num = PS[2][:, (c % 2) * HALF:(c % 2) * HALF + VA]
                    dve.wait_ge(m_num.sem, m_num.at(h, c))
                    den = num[:, ML_V:ML_V + 1]
                    dve.tensor_scalar(stat[:, 2:3], den, -1.0, ml_cols[:, 2, c:c + 1], ALU.mult, ALU.max).then_inc(m_den.sem, 1)
                    dve.wait_ge(m_den.sem, m_den.at(h, 1 + 2 * c))
                    dve.tensor_tensor(stat[:, 0:1], den, stat[:, 2:3], ALU.max).then_inc(m_den.sem, 1)
                    dve.wait_ge(m_den.sem, m_den.at(h, 2 + 2 * c))
                    dve.reciprocal(stat[:, 1:2], stat[:, 0:1]).then_inc(m_rd.sem, 1)
                    dve.wait_ge(m_rd.sem, m_rd.at(h, c))
                    dve.tensor_scalar(hm[:, c, :], num[:, 0:ML_V], stat[:, 1:2], None, ALU.mult).then_inc(m_hm.sem, 1)
                dve.wait_ge(m_so.sem, m_so.at(h))
                dve.wait_ge(m_hm.sem, m_hm.at(h))
                dve.tensor_tensor(hm[:], hm[:], ml_so[:], ALU.mult).then_inc(m_g.sem, 1)
                dve.wait_ge(m_std.sem, m_std.at(h))
                dve.reciprocal(stat[:, 0:8], stat2[:, 8:16]).then_inc(m_r.sem, 1)
                dve.wait_ge(m_r.sem, m_r.at(h))
                for c in range(NC):
                    dve.tensor_scalar(hm[:, c, :], hm[:, c, :], stat[:, c:c + 1], None, ALU.mult).then_inc(m_n.sem, 1)
                for e in range(2):
                    dst = (xp[:, 0:T], mt[:])[e]
                    dve.wait_ge(m_ntr.sem, m_ntr.at(h, e))
                    dve.tensor_scalar(dst, PS[2 + e], par_col("ml_g", e), None, ALU.mult).then_inc(m_y.sem, 1)
                for e in range(2):
                    dst = (xp[:, 0:T], mt[:])[e]
                    dve.wait_ge(m_y.sem, m_y.at(h, e))
                    dve.wait_ge(m_z.sem, m_z.at(h, e))
                    dve.tensor_tensor(dst, dst, ml_z[e][:], ALU.mult).then_inc(m_y.sem, 1)
                for e in range(2):
                    dve.wait_ge(m_yh.sem, m_yh.at(h, e))
                    dve.tensor_tensor(my_lo[e][:], (xp[:, 0:T], mt[:])[e], my_hi[e][:].bitcast(F32), ALU.subtract).then_inc(m_yl.sem, 1)
                for e in range(2):
                    add_out(IN_ML + 10 * h + ((8 if last else 10) + e), OUT_ML + 2 * h + e, done=in_mm)

            ml_qk(0)
            with dve.Fori(0, ML_HEADS - 1) as h:
                ml_head(h)
                ml_qk(h + 1)
            ml_head(ML_HEADS - 1, last=True)

            def layer_output(norm, use, g_name):
                for e in range(2):
                    reciprocal(norm, e)
                    if e == 0:
                        dve.wait_ge(refill.sem, refill.at(use))
                    for k in range(KT):
                        gain(acc, k, e, g_name, post_t)
                        if k % 2 == 1:
                            residual(use, k - 1, e)

            def residual(use, k, e):
                dve.wait_ge(post_t.sem, post_t.at(use, e * KT + k))
                tile = resid[:, k, half_of(e)]
                dve.tensor_tensor(tile, tile, acc[:, k, half_of(e)], ALU.add).then_inc(post_h[0].sem, 1)

            layer_output(3, 0, "l0_post_g")
            layer_input(4, 2, "l1_pre_g")

            dve.wait_ge(sp_ld.sem, sp_ld.at(0))
            with dve.Fori(0, SG_TILES // 2) as j:
                for s in range(2):
                    dve.wait_ge(v_tr.sem, v_tr.at(2 * j + s))
                    dve.wait_ge(v_st[s].sem, v_st[s].at(j - 1))
                    dve.wait_ge(v_sq.sem, v_sq.at(2 * j + (s - 2)))
                    dve.tensor_copy(g_tok[s][:].rearrange("p c d -> p (c d)"), PS[2 + s]).then_inc(v_tok.sem, 1)
            dve.wait_ge(v_sq.sem, v_sq.at(SG_TILES - 1))
            dve.tensor_reduce(stat[:, 0:8], ssq[:], AX_X, ALU.add).then_inc(v_r.sem, 1)
            dve.wait_ge(v_r.sem, 2)
            dve.reciprocal(stat[:, 8:16], stat2[:, 0:8]).then_inc(v_r.sem, 1)
            dve.wait_ge(v_r.sem, 3)
            dve.wait_ge(const.sem, 14)
            dve.wait_ge(acc_zero.sem, 2)

            def sg_weights(g):
                dve.wait_ge(w_l.sem, w_l.at(g - 1))
                for c in range(NC):
                    dve.tensor_scalar(wr[:, c, :], wsp[:, bass.ds(g, 1), :].rearrange("p a t -> p (a t)"), stat[:, 8 + c:9 + c],
                                      None, ALU.mult).then_inc(w_s.sem, 1)
                dve.wait_ge(w_h.sem, w_h.at(g))
                dve.tensor_tensor(wr_lo[:], wr[:], wr_hi[:].bitcast(F32), ALU.subtract).then_inc(w_l.sem, 1)

            def sg_tile(d, g, n):
                dve.wait_ge(c_mm.sem, c_mm.at(n))
                dve.wait_ge(e_yl.sem, e_yl.at(d - 1))
                dve.scalar_tensor_tensor(sg_v[:].rearrange("p (c t) -> p c t", t=P), PS[2].rearrange("p (c t) -> p c t", t=P),
                                         par[:, bass.ds(d + COL["sg_g"], 1)],
                                         bsp[:, bass.ds(g, 1), :].to_broadcast([P, NC, P]), ALU.mult, ALU.add).then_inc(e_v.sem, 1)
                dve.wait_ge(e_v.sem, e_v.at(d))
                dve.wait_ge(e_u.sem, e_u.at(d))
                dve.tensor_tensor(sg_v[:], sg_v[:], sg_u[:], ALU.mult).then_inc(e_y.sem, 1)
                dve.wait_ge(e_y.sem, e_y.at(d, 0))
                dve.wait_ge(e_z.sem, e_z.at(d))
                dve.tensor_tensor(sg_v[:], sg_v[:], sg_z[:], ALU.mult).then_inc(e_y.sem, 1)

            sg_weights(0)
            sg_tile(0, 0, C_SG)
            sg_tile(1, 0, C_SG + 1)
            add_out(C_SG + 2, OUT_SG)
            with dve.Fori(1, SG_GROUPS - 1) as g:
                sg_weights(g)
                for e in range(2):
                    sg_tile(2 * g + e, g, C_SG + 4 * g + (2 * e - 1))
                    add_out(C_SG + 4 * g + 2 * e, OUT_SG + 2 * g + (e - 1))
            sg_weights(SG_GROUPS - 1)
            sg_tile(SG_TILES - 2, SG_GROUPS - 1, C_SG + 2 * SG_TILES - 5)
            add_out(C_SG + 2 * SG_TILES - 4, OUT_SG + SG_TILES - 3)
            sg_tile(SG_TILES - 1, SG_GROUPS - 1, C_SG + 2 * SG_TILES - 3)
            for b in range(2):
                add_out(IN_SG_OUT + b, OUT_SG + SG_TILES - 2 + b, done=in_mm)
            layer_output(5, 1, "l1_post_g")


def columns(v):
    return np.asarray(v).reshape(-1, P).T


def in_slab(w, cols):
    return np.asarray(w)[:, cols:cols + P].reshape(KT, P, P).transpose(1, 0, 2).reshape(P, T)


def kernel(**inputs):
    import concourse.bacc as bacc
    from concourse.bass_utils import run_bass_kernel_spmd

    a = {k: np.asarray(v) for k, v in inputs.items()}
    f32 = np.float32
    par = np.zeros((P, N_PAR), f32)

    def put(name, cols):
        par[:cols.shape[0], COL[name]:COL[name] + cols.shape[1]] = cols

    put("c", columns(a["c"][0]))
    put("mod_b", columns(a["mod_b"][0]))
    for n in range(2):
        put(f"ln_g{n}", columns(a["ln_g"][0, n]))
        put(f"ln_b{n}", columns(a["ln_b"][0, n]))
    put("pool_scale", columns(a["pool_scale"][0]))
    put("l0_pre_g", columns(a["l0_pre_g_2"]))
    put("l0_post_g", columns(a["l0_post_g_2"]))
    put("l1_pre_g", columns(a["l1_pre_g_2"]))
    put("l1_post_g", columns(a["l1_post_g_2"]))
    put("conv_w", columns(a["l0_conv_w_2"]))
    put("conv_b", columns(a["l0_conv_b_2"]))
    put("da_g", columns(a["l0_da_head_g_2"]))
    put("ml_g", columns(a["l0_ml_head_g_2"]))
    put("sg_g", columns(a["l1_sg_norm_g_2"]))
    par[0:ML_HEADS, COL["gate_b"]] = a["l0_b_igate_2"]
    par[32:32 + ML_HEADS, COL["gate_b"]] = a["l0_b_fgate_2"]
    put("lam_q", np.stack([a["l0_lambda_q1_2"], a["l0_lambda_q2_2"]], 1))
    put("lam_k", np.stack([a["l0_lambda_k1_2"], a["l0_lambda_k2_2"]], 1))

    edges = np.ones((P, 32), f32)
    for w in (2, 4, 8, 16):
        counts = [t + w // 2 for t in range(w // 2)] + [w - 1 - r for r in range(w // 2 - 1)]
        edges[:, w - 2:w - 2 + len(counts)] = np.array([w / n for n in counts], f32)

    ffn_in, w0, w1 = a["ffn_w_in"][0], a["l0_w_in_2"], a["l1_w_in_2"]
    hidden = F_TILES * P
    w_in = np.empty((N_IN, P, T), f32)
    for f in range(F_TILES):
        w_in[2 * f] = in_slab(ffn_in, f * P)
        w_in[2 * f + 1] = in_slab(ffn_in, hidden + f * P)
    da, qk = DA_HEADS * DA_V, ML_HEADS * ML_QK
    ml_qk = 4 * da
    ml_v = ml_qk + 2 * qk
    ml_i = ml_v + ML_HEADS * ML_V
    ml_o = ml_i + 2 * ML_HEADS
    ml_z = ml_o + ML_HEADS * ML_V
    for h in range(DA_HEADS):
        for s in range(4):
            w_in[IN_DA + 4 * h + s] = in_slab(w0, (2, 0, 1, 3)[s] * da + h * P)
    w_out = a["l0_w_out_2"].reshape(-1, P, D)
    ml_order = []
    for h in range(ML_HEADS):
        qk_of = lambda n: [in_slab(w0, ml_qk + e * qk + n * ML_QK) for e in range(2)]
        ml_order += qk_of(0) if h == 0 else []
        ml_order += [in_slab(w0, first + h * ML_V + e * P) for first in (ml_v, ml_o, ml_z) for e in range(2)]
        ml_order += qk_of(h + 1) if h + 1 < ML_HEADS else []
        ml_order += [w_out[DA_HEADS + 2 * h + e] for e in range(2)]
    for n, slab in enumerate(ml_order):
        w_in[IN_ML + n] = slab
    width = SG_TILES * P
    for d in range(SG_TILES):
        w_in[IN_SV + d] = in_slab(w1, width + d * P)
        w_in[IN_SG + 2 * d] = in_slab(w1, d * P)
        w_in[IN_SG + 2 * d + 1] = in_slab(w1, 2 * width + d * P)
    w_c = np.zeros((N_C_DRAM, P, T), f32)
    ffn_out = a["ffn_w_out"][0].reshape(F_TILES, P, D)
    sg_out = a["l1_w_out_2"].reshape(SG_TILES, P, D)
    w_c[0:C_GATES], w_in[IN_FFN_OUT:IN_DA] = ffn_out[:-2], ffn_out[-2:]
    w_c[C_SG:], w_in[IN_SG_OUT:] = sg_out[:-2], sg_out[-2:]
    gates = w_c[C_GATES].reshape(P, KT, P)
    gates[:, :, 0:ML_HEADS] = w0[:, ml_i:ml_i + ML_HEADS].reshape(KT, P, ML_HEADS).transpose(1, 0, 2)
    gates[:, :, 32:32 + ML_HEADS] = w0[:, ml_i + ML_HEADS:ml_o].reshape(KT, P, ML_HEADS).transpose(1, 0, 2)
    w_c[C_DA:C_SG] = w_out[:DA_HEADS]

    mod_w = a["mod_w"][0].reshape(KT, P, N_MOD * D // HALF, HALF).transpose(2, 1, 0, 3)
    arrays = {
        "x_t": a["x"][0].T.reshape(KT, P, T).transpose(1, 0, 2),
        "params": par,
        "mod_w": mod_w,
        "pool_w": a["pool_w"][0].reshape(4, 2, P, 256).transpose(2, 0, 1, 3),
        "w_in": w_in,
        "w_c": w_c,
        "edges": edges,
        "w_spatial": a["l1_w_spatial_2"].transpose(2, 0, 1),
        "b_spatial": a["l1_b_spatial_2"].reshape(1, SG_GROUPS * P),
    }
    arrays = {k: np.ascontiguousarray(v) for k, v in arrays.items()}
    nc = bacc.Bacc("TRN2", target_bir_lowering=False, num_devices=1)
    args = {k: nc.dram_tensor(k, v.shape, F32, kind="ExternalInput").ap() for k, v in arrays.items()}
    out = nc.dram_tensor("out", (P, KT, T), F32, kind="ExternalOutput").ap()
    build(nc, out=out, **args)
    result = run_bass_kernel_spmd(nc, [arrays], core_ids=[0]).results[0]["out"]
    return result.transpose(2, 1, 0).reshape(1, T, D)
```
